# Optimizing a Trainium2 kernel written in Bass

```python
import math
import jax
import jax.numpy as jnp
from jax import lax
import numpy as np
import jax, jax.numpy as jnp

D_MODEL = 1024
BATCH = 1
SEQ = 1024
DEPTH = 1

CHUNK = 64
HEAD_DIM = 64
N_BRANCH = 4
BRANCH_WIDTH = D_MODEL // N_BRANCH
CONV_WIDTH = 3
SC_WIDTH = BRANCH_WIDTH
SB_HEADS = BRANCH_WIDTH // HEAD_DIM
SB_WIDTH = SB_HEADS * HEAD_DIM
SB_BLOCK = 128
RW_HEADS = BRANCH_WIDTH // HEAD_DIM
RW_WIDTH = RW_HEADS * HEAD_DIM
RW_DECAY_LORA = 64
RW_A_LORA = 64
RW_GATE_LORA = 128
RW_GN_EPS = 64e-5
RW_DECAY_SCALE = math.exp(-0.5)
SG_GROUPS = 4
SG_WIDTH = BRANCH_WIDTH
SG_GROUP_WIDTH = SG_WIDTH // SG_GROUPS
SG_CHUNK = 128
D_FF = ((8 * D_MODEL // 3 + 127) // 128) * 128
RMS_EPS = 1e-6
LN_EPS = 1e-5

SC_OFF = 0
SB_OFF = SC_OFF + 3 * SC_WIDTH
RW_OFF = SB_OFF + 3 * SB_WIDTH
RW_COLS = 3 * RW_WIDTH + RW_DECAY_LORA + RW_A_LORA + RW_GATE_LORA
SG_OFF = RW_OFF + RW_COLS
GATE_OFF = SG_OFF + 2 * SG_WIDTH
IN_COLS = GATE_OFF + N_BRANCH * D_MODEL


def rms_norm(x, g):
    xf = x.astype(jnp.float32)
    y = xf * lax.rsqrt(jnp.mean(xf * xf, axis=-1, keepdims=True) + RMS_EPS)
    return (y * g.astype(jnp.float32)).astype(x.dtype)

def layer_norm(x, g, b):
    xf = x.astype(jnp.float32)
    mu = jnp.mean(xf, axis=-1, keepdims=True)
    var = jnp.mean(jnp.square(xf - mu), axis=-1, keepdims=True)
    y = (xf - mu) * lax.rsqrt(var + LN_EPS) * g.astype(jnp.float32) + b.astype(jnp.float32)
    return y.astype(x.dtype)

def causal_dwconv(x, w):
    k = w.shape[0]
    t = x.shape[1]
    xp = jnp.pad(x, ((0, 0), (k - 1, 0), (0, 0)))
    out = xp[:, 0:t] * w[0]
    for i in range(1, k):
        out = out + xp[:, i:i + t] * w[i]
    return out

def token_shift(x):
    return jnp.pad(x, ((0, 0), (1, 0), (0, 0)))[:, :-1]

def short_conv_mixer(z, conv_w):
    b_gate, c_gate, xin = jnp.split(z, 3, axis=-1)
    return b_gate * causal_dwconv(c_gate * xin, conv_w)

def stick_breaking_attention(q, k, v):
    bsz, t, h, dh = q.shape
    nb = t // SB_BLOCK
    scale = 1.0 / math.sqrt(dh)
    qb = q.reshape(bsz, nb, SB_BLOCK, h, dh).transpose(1, 0, 3, 2, 4)
    kh = k.transpose(0, 2, 1, 3)
    vh = v.transpose(0, 2, 1, 3)
    kpos = jnp.arange(t)

    def block(args):
        qi, bi = args
        z = jnp.einsum('bhqd,bhkd->bhqk', qi, kh).astype(jnp.float32) * scale
        qpos = bi * SB_BLOCK + jnp.arange(SB_BLOCK)
        mask = kpos[None, :] < qpos[:, None]
        log_beta = jax.nn.log_sigmoid(z)
        log_keep = jnp.where(mask, log_beta - z, 0.0)
        suffix = lax.cumsum(log_keep, axis=3, reverse=True) - log_keep
        attn = jnp.where(mask, jnp.exp(log_beta + suffix), 0.0)
        return jnp.einsum('bhqk,bhkd->bhqd', attn.astype(vh.dtype), vh)

    out = lax.map(block, (qb, jnp.arange(nb)))
    return out.transpose(1, 0, 3, 2, 4).reshape(bsz, t, h * dh)

def rwkv7_scan(r, w, k, v, a_vec, b_vec):
    bsz, t, h, n = r.shape

    def step(s, inp):
        r_t, w_t, k_t, v_t, a_t, b_t = inp
        sa = jnp.einsum('bhvk,bhk->bhv', s, a_t)
        s = s * w_t[:, :, None, :] + sa[..., None] * b_t[:, :, None, :] + v_t[..., None] * k_t[:, :, None, :]
        return s, jnp.einsum('bhvk,bhk->bhv', s, r_t)

    xs = tuple(u.astype(jnp.float32).transpose(1, 0, 2, 3) for u in (r, w, k, v, a_vec, b_vec))
    s0 = jnp.zeros((bsz, h, n, n), jnp.float32)
    _, y = lax.scan(step, s0, xs)
    return y.transpose(1, 0, 2, 3)

def rwkv7_mixer(z, mu, w0, w2, a0, a2, g2, k_k, k_a, r_k, gn_g, gn_b):
    bsz, t, _ = z.shape
    z = z + (token_shift(z) - z) * mu
    c0, c1, c2 = RW_WIDTH, 2 * RW_WIDTH, 3 * RW_WIDTH
    c3, c4 = c2 + RW_DECAY_LORA, c2 + RW_DECAY_LORA + RW_A_LORA
    r, k, v = z[..., :c0], z[..., c0:c1], z[..., c1:c2]
    xw, xa, xg = z[..., c2:c3], z[..., c3:c4], z[..., c4:]
    decay = jnp.exp(-RW_DECAY_SCALE * jax.nn.sigmoid((w0 + jnp.tanh(xw) @ w2).astype(jnp.float32)))
    a = jax.nn.sigmoid(a0 + xa @ a2)
    g = jax.nn.sigmoid(xg) @ g2
    hs = (bsz, t, RW_HEADS, HEAD_DIM)
    kk = (k * k_k).reshape(hs).astype(jnp.float32)
    kk = kk / jnp.maximum(jnp.sqrt(jnp.sum(kk * kk, axis=-1, keepdims=True)), 1e-12)
    k = k * (1.0 + (a - 1.0) * k_a)
    rh, kh, vh, ah = r.reshape(hs), k.reshape(hs), v.reshape(hs), a.reshape(hs)
    y = rwkv7_scan(rh, decay.reshape(hs), kh, vh, -kk, kk * ah.astype(jnp.float32))
    mean = jnp.mean(y, axis=-1, keepdims=True)
    var = jnp.mean(jnp.square(y - mean), axis=-1, keepdims=True)
    y = ((y - mean) * lax.rsqrt(var + RW_GN_EPS)).reshape(bsz, t, RW_WIDTH)
    y = y * gn_g.astype(jnp.float32) + gn_b.astype(jnp.float32)
    bonus = jnp.sum((rh * kh * r_k).astype(jnp.float32), axis=-1, keepdims=True) * vh.astype(jnp.float32)
    y = (y + bonus.reshape(bsz, t, RW_WIDTH)).astype(z.dtype)
    return y * g

def spatial_gating(z, ln_g, ln_b, w_s, b_s):
    bsz, t, _ = z.shape
    u, v = jnp.split(jax.nn.gelu(z), 2, axis=-1)
    v = layer_norm(v, ln_g, ln_b)
    vb = v.reshape(bsz, t // SG_CHUNK, SG_CHUNK, SG_GROUPS, SG_GROUP_WIDTH)
    w_causal = jnp.tril(w_s)
    mixed = jnp.einsum('gts,bnsgc->bntgc', w_causal, vb) + b_s.T[:, :, None]
    return u * mixed.reshape(bsz, t, SG_WIDTH)

def hybrid_mixer(h, w_in, gate_b, sc_conv_w, sc_out, sb_out, rw_mu, rw_w0, rw_w2, rw_a0, rw_a2,
                 rw_g2, rw_k_k, rw_k_a, rw_r_k, rw_gn_g, rw_gn_b, rw_out, sg_ln_g, sg_ln_b,
                 sg_w, sg_b, sg_out, w_o):
    bsz, t, _ = h.shape
    proj = h @ w_in
    y_a = short_conv_mixer(proj[..., SC_OFF:SB_OFF], sc_conv_w)
    q, k, v = jnp.split(proj[..., SB_OFF:RW_OFF], 3, axis=-1)
    hs = (bsz, t, SB_HEADS, HEAD_DIM)
    y_b = stick_breaking_attention(q.reshape(hs), k.reshape(hs), v.reshape(hs))
    y_c = rwkv7_mixer(proj[..., RW_OFF:SG_OFF], rw_mu, rw_w0, rw_w2, rw_a0, rw_a2, rw_g2,
                      rw_k_k, rw_k_a, rw_r_k, rw_gn_g, rw_gn_b)
    y_d = spatial_gating(proj[..., SG_OFF:GATE_OFF], sg_ln_g, sg_ln_b, sg_w, sg_b)
    gates = jax.nn.sigmoid((proj[..., GATE_OFF:] + gate_b).astype(jnp.float32)).astype(h.dtype)
    gates = gates.reshape(bsz, t, N_BRANCH, D_MODEL)
    merged = (gates[:, :, 0] * (y_a @ sc_out) + gates[:, :, 1] * (y_b @ sb_out)
              + gates[:, :, 2] * (y_c @ rw_out) + gates[:, :, 3] * (y_d @ sg_out))
    return merged @ w_o

def conv_glu_ffn(h, w_up, conv_w, w_down):
    up = causal_dwconv(h @ w_up, conv_w)
    gate, val = jnp.split(up, 2, axis=-1)
    return (jax.nn.silu(gate) * val) @ w_down

def first_inputs(seed: int = 0) -> dict:
    key = jax.random.key(seed)
    keys = iter(jax.random.split(key, 40))
    f32 = jnp.float32
    L = DEPTH

    def nrm(shape, scale):
        return jax.random.normal(next(keys), shape, f32) * scale

    return {
        "x": nrm((BATCH, SEQ, D_MODEL), 1.0),
        "mix_norm_g": 1.0 + nrm((L, D_MODEL), 0.05),
        "w_in": nrm((L, D_MODEL, IN_COLS), D_MODEL ** -0.5),
        "gate_b": nrm((L, N_BRANCH * D_MODEL), 0.1),
        "sc_conv_w": nrm((L, CONV_WIDTH, SC_WIDTH), CONV_WIDTH ** -0.5),
        "sc_out": nrm((L, SC_WIDTH, D_MODEL), SC_WIDTH ** -0.5),
        "sb_out": nrm((L, SB_WIDTH, D_MODEL), SB_WIDTH ** -0.5),
        "rw_mu": jax.random.uniform(next(keys), (L, RW_COLS), f32),
        "rw_w0": nrm((L, RW_WIDTH), 0.5),
        "rw_w2": nrm((L, RW_DECAY_LORA, RW_WIDTH), 0.1),
        "rw_a0": nrm((L, RW_WIDTH), 0.1),
        "rw_a2": nrm((L, RW_A_LORA, RW_WIDTH), 0.1),
        "rw_g2": nrm((L, RW_GATE_LORA, RW_WIDTH), RW_GATE_LORA ** -0.5),
        "rw_k_k": 0.85 + nrm((L, RW_WIDTH), 0.05),
        "rw_k_a": 1.0 + nrm((L, RW_WIDTH), 0.05),
        "rw_r_k": nrm((L, RW_HEADS, HEAD_DIM), 0.1),
        "rw_gn_g": 1.0 + nrm((L, RW_WIDTH), 0.05),
        "rw_gn_b": nrm((L, RW_WIDTH), 0.01),
        "rw_out": nrm((L, RW_WIDTH, D_MODEL), RW_WIDTH ** -0.5),
        "sg_ln_g": 1.0 + nrm((L, SG_WIDTH), 0.05),
        "sg_ln_b": nrm((L, SG_WIDTH), 0.01),
        "sg_w": nrm((L, SG_GROUPS, SG_CHUNK, SG_CHUNK), 0.05),
        "sg_b": 1.0 + nrm((L, SG_GROUPS, SG_CHUNK), 0.05),
        "sg_out": nrm((L, SG_WIDTH, D_MODEL), SG_WIDTH ** -0.5),
        "w_o": nrm((L, D_MODEL, D_MODEL), 0.5 * D_MODEL ** -0.5),
        "ffn_norm_g": 1.0 + nrm((L, D_MODEL), 0.05),
        "w_up": nrm((L, D_MODEL, 2 * D_FF), D_MODEL ** -0.5),
        "ffn_conv_w": nrm((L, CONV_WIDTH, 2 * D_FF), CONV_WIDTH ** -0.5),
        "w_down": nrm((L, D_FF, D_MODEL), 0.5 * D_FF ** -0.5),
        "final_norm_g": 1.0 + nrm((D_MODEL,), 0.05),
    }

def first_block(x, mix_norm_g, w_in, gate_b, sc_conv_w, sc_out, sb_out, rw_mu, rw_w0, rw_w2,
              rw_a0, rw_a2, rw_g2, rw_k_k, rw_k_a, rw_r_k, rw_gn_g, rw_gn_b, rw_out, sg_ln_g,
              sg_ln_b, sg_w, sg_b, sg_out, w_o, ffn_norm_g, w_up, ffn_conv_w, w_down,
              final_norm_g):
    for l in range(DEPTH):
        h = rms_norm(x, mix_norm_g[l])
        x = x + hybrid_mixer(h, w_in[l], gate_b[l], sc_conv_w[l], sc_out[l], sb_out[l], rw_mu[l],
                             rw_w0[l], rw_w2[l], rw_a0[l], rw_a2[l], rw_g2[l], rw_k_k[l],
                             rw_k_a[l], rw_r_k[l], rw_gn_g[l], rw_gn_b[l], rw_out[l], sg_ln_g[l],
                             sg_ln_b[l], sg_w[l], sg_b[l], sg_out[l], w_o[l])
        h = rms_norm(x, ffn_norm_g[l])
        x = x + conv_glu_ffn(h, w_up[l], ffn_conv_w[l], w_down[l])
    return rms_norm(x, final_norm_g)


D_MIX = D_MODEL
A_HEAD_DIM = 64
A_HEADS = (D_MIX // 2) // A_HEAD_DIM
A_WIDTH = A_HEADS * A_HEAD_DIM
DILATED_PATTERNS = ((128, 1), (512, 4), (2048, 16))
BLOCK = 128
B_HEADS = 8
QK_NOPE_DIM = 64
QK_ROPE_DIM = 32
V_HEAD_DIM = (D_MIX - A_WIDTH) // B_HEADS
B_WIDTH = B_HEADS * V_HEAD_DIM
Q_LORA_RANK = 256
KV_LORA_RANK = 128
ROPE_THETA = 10000.0
REL_BUCKETS = 32
REL_MAX_DISTANCE = 2048
EPS = 1e-6

IN_SPLITS = (A_WIDTH, A_WIDTH, A_WIDTH, A_WIDTH,
             Q_LORA_RANK, KV_LORA_RANK, QK_ROPE_DIM, B_WIDTH)
IN_COLS_2 = sum(IN_SPLITS)


def rmsnorm(t, gain):
    tf = t.astype(jnp.float32)
    return tf * lax.rsqrt(jnp.mean(tf * tf, axis=-1, keepdims=True) + EPS) * gain.astype(jnp.float32)

def rope(t, cos, sin):
    t1, t2 = jnp.split(t, 2, axis=-1)
    return jnp.concatenate([t1 * cos - t2 * sin, t1 * sin + t2 * cos], axis=-1)

def t5_bucket(dist):
    max_exact = REL_BUCKETS // 2
    d = jnp.maximum(dist.astype(jnp.float32), 1.0)
    large = max_exact + (jnp.log(d / max_exact) / math.log(REL_MAX_DISTANCE / max_exact)
                         * (REL_BUCKETS - max_exact)).astype(jnp.int32)
    large = jnp.minimum(large, REL_BUCKETS - 1)
    return jnp.where(dist < max_exact, dist, large)

def dilated_pattern(q, k, v, rel_bias, window, dilation):
    B, S, H, D = q.shape
    steps = window // dilation
    span = dilation * BLOCK
    Sp = -(-S // span) * span
    nb = Sp // span
    pad = ((0, 0), (0, Sp - S), (0, 0), (0, 0))

    def blocks(t):
        return jnp.pad(t, pad).reshape(B, nb, BLOCK, dilation, H, D)

    def with_prev(t):
        prev = jnp.pad(t[:, :-1], ((0, 0), (1, 0), (0, 0), (0, 0), (0, 0), (0, 0)))
        return jnp.concatenate([prev, t], axis=2)

    qb = blocks(q)
    kw = with_prev(blocks(k))
    vw = with_prev(blocks(v))

    qi = jnp.arange(BLOCK)[:, None]
    ki = jnp.arange(2 * BLOCK)[None, :]
    j = qi + BLOCK - ki
    bias = rel_bias[t5_bucket(jnp.maximum(j, 0) * dilation)]
    bias = jnp.transpose(bias, (2, 0, 1)).astype(jnp.float32)
    valid = ((j >= 0) & (j <= steps))[None] & \
        ((jnp.arange(nb)[:, None, None] > 0) | (ki >= BLOCK)[None])

    s = jnp.einsum('bnqrhd,bnkrhd->bnrhqk', qb, kw) * (A_HEAD_DIM ** -0.5) + bias
    s = jnp.where(valid[None, :, None, None], s, -jnp.inf)
    m = jnp.max(s, axis=-1, keepdims=True)
    p = jnp.exp(s - m)
    den = jnp.sum(p, axis=-1)
    den_q = jnp.transpose(den, (0, 1, 4, 2, 3))
    o = jnp.einsum('bnrhqk,bnkrhd->bnqrhd', p, vw) / den_q[..., None]
    o = o.reshape(B, Sp, H, D)[:, :S]
    m = jnp.transpose(m[..., 0], (0, 1, 4, 2, 3)).reshape(B, Sp, H)[:, :S]
    den = den_q.reshape(B, Sp, H)[:, :S]
    return o, m, den

def dilated_window_attention(q, k, v, rel_bias):
    outs, log_dens = [], []
    for window, dilation in DILATED_PATTERNS:
        o, m, den = dilated_pattern(q, k, v, rel_bias, window, dilation)
        outs.append(o)
        log_dens.append(m + jnp.log(den))
    alpha = jax.nn.softmax(jnp.stack(log_dens, axis=0), axis=0)
    return jnp.sum(alpha[..., None] * jnp.stack(outs, axis=0), axis=0)

def latent_attention(c_q, c_kv, k_rope_in, positions, q_c_gain, w_uq, kv_c_gain, w_ukv,
                     qn_gain, qr_gain, kn_gain, kr_gain):
    B, S, _ = c_q.shape
    q = jnp.matmul(rmsnorm(c_q, q_c_gain), w_uq.astype(jnp.float32))
    q = q.reshape(B, S, B_HEADS, QK_NOPE_DIM + QK_ROPE_DIM)
    kv = jnp.matmul(rmsnorm(c_kv, kv_c_gain), w_ukv.astype(jnp.float32))
    kv = kv.reshape(B, S, B_HEADS, QK_NOPE_DIM + V_HEAD_DIM)
    q_nope = rmsnorm(q[..., :QK_NOPE_DIM], qn_gain)
    q_rope = rmsnorm(q[..., QK_NOPE_DIM:], qr_gain)
    k_nope = rmsnorm(kv[..., :QK_NOPE_DIM], kn_gain)
    v = kv[..., QK_NOPE_DIM:]
    k_rope = rmsnorm(k_rope_in, kr_gain)

    inv_freq = ROPE_THETA ** (-jnp.arange(0, QK_ROPE_DIM, 2, dtype=jnp.float32) / QK_ROPE_DIM)
    ang = positions.astype(jnp.float32)[..., None] * inv_freq
    cos, sin = jnp.cos(ang), jnp.sin(ang)
    q_rope = rope(q_rope, cos[:, :, None], sin[:, :, None])
    k_rope = rope(k_rope, cos, sin)

    scale = (QK_NOPE_DIM + QK_ROPE_DIM) ** -0.5
    nb = S // BLOCK
    qn_b = q_nope.reshape(B, nb, BLOCK, B_HEADS, QK_NOPE_DIM).transpose(1, 0, 2, 3, 4)
    qr_b = q_rope.reshape(B, nb, BLOCK, B_HEADS, QK_ROPE_DIM).transpose(1, 0, 2, 3, 4)
    kpos = jnp.arange(S)

    def one_block(args):
        qn, qr, i = args
        s = (jnp.einsum('bqhd,bkhd->bhqk', qn, k_nope)
             + jnp.einsum('bqhd,bkd->bhqk', qr, k_rope)) * scale
        qpos = i * BLOCK + jnp.arange(BLOCK)
        s = jnp.where((qpos[:, None] >= kpos[None, :])[None, None], s, -jnp.inf)
        p = jax.nn.softmax(s, axis=-1)
        return jnp.einsum('bhqk,bkhd->bqhd', p, v)

    o = lax.map(one_block, (qn_b, qr_b, jnp.arange(nb)))
    return o.transpose(1, 0, 2, 3, 4).reshape(B, S, B_WIDTH)

def hybrid_layer(x, positions, rel_bias, norm_gain, w_in, a_q_gain, a_k_gain, q_c_gain, w_uq,
                 kv_c_gain, w_ukv, qn_gain, qr_gain, kn_gain, kr_gain, w_out):
    B, S, _ = x.shape
    h = rmsnorm(x, norm_gain)
    proj = jnp.matmul(h, w_in.astype(jnp.float32))
    idx = np.cumsum(IN_SPLITS)[:-1].tolist()
    q_a, k_a, v_a, z_a, c_q, c_kv, k_rope, z_b = jnp.split(proj, idx, axis=-1)

    q_a = rmsnorm(q_a.reshape(B, S, A_HEADS, A_HEAD_DIM), a_q_gain)
    k_a = rmsnorm(k_a.reshape(B, S, A_HEADS, A_HEAD_DIM), a_k_gain)
    v_a = v_a.reshape(B, S, A_HEADS, A_HEAD_DIM)
    o_a = dilated_window_attention(q_a, k_a, v_a, rel_bias).reshape(B, S, A_WIDTH)

    o_b = latent_attention(c_q, c_kv, k_rope, positions, q_c_gain, w_uq, kv_c_gain, w_ukv,
                           qn_gain, qr_gain, kn_gain, kr_gain)

    mixed = jnp.concatenate([o_a * jax.nn.silu(z_a), o_b * jax.nn.silu(z_b)], axis=-1)
    out = jnp.matmul(mixed, w_out.astype(jnp.float32))
    return (x.astype(jnp.float32) + out).astype(x.dtype)

def second_inputs(seed: int = 0) -> dict:
    key = jax.random.key(seed)
    ks = jax.random.split(key, 18)
    f32 = jnp.float32

    def nrm(k, shape, scale):
        return jax.random.normal(k, shape, f32) * scale

    def gain(k, shape):
        return 1.0 + 0.05 * jax.random.normal(k, shape, f32)

    x = jax.random.normal(ks[0], (BATCH, SEQ, D_MODEL), f32)
    offsets = jax.random.randint(ks[1], (BATCH, 1), 0, 1024, dtype=jnp.int32)
    positions = (jnp.arange(SEQ, dtype=jnp.int32)[None, :] + offsets).astype(jnp.int32)
    return {
        "x": x,
        "positions": positions,
        "rel_bias": nrm(ks[2], (REL_BUCKETS, A_HEADS), 0.1),
        "norm_gain": gain(ks[3], (DEPTH, D_MODEL)),
        "w_in": nrm(ks[4], (DEPTH, D_MODEL, IN_COLS_2), D_MODEL ** -0.5),
        "a_q_gain": gain(ks[5], (DEPTH, A_HEAD_DIM)),
        "a_k_gain": gain(ks[6], (DEPTH, A_HEAD_DIM)),
        "q_c_gain": gain(ks[7], (DEPTH, Q_LORA_RANK)),
        "w_uq": nrm(ks[8], (DEPTH, Q_LORA_RANK, B_HEADS * (QK_NOPE_DIM + QK_ROPE_DIM)), Q_LORA_RANK ** -0.5),
        "kv_c_gain": gain(ks[9], (DEPTH, KV_LORA_RANK)),
        "w_ukv": nrm(ks[10], (DEPTH, KV_LORA_RANK, B_HEADS * (QK_NOPE_DIM + V_HEAD_DIM)), KV_LORA_RANK ** -0.5),
        "qn_gain": gain(ks[11], (DEPTH, QK_NOPE_DIM)),
        "qr_gain": gain(ks[12], (DEPTH, QK_ROPE_DIM)),
        "kn_gain": gain(ks[13], (DEPTH, QK_NOPE_DIM)),
        "kr_gain": gain(ks[14], (DEPTH, QK_ROPE_DIM)),
        "w_out": nrm(ks[15], (DEPTH, D_MIX, D_MODEL), D_MIX ** -0.5),
    }

def second_block(x, positions, rel_bias, norm_gain, w_in, a_q_gain, a_k_gain, q_c_gain, w_uq,
              kv_c_gain, w_ukv, qn_gain, qr_gain, kn_gain, kr_gain, w_out):
    for l in range(DEPTH):
        x = hybrid_layer(x, positions, rel_bias, norm_gain[l], w_in[l], a_q_gain[l], a_k_gain[l],
                         q_c_gain[l], w_uq[l], kv_c_gain[l], w_ukv[l], qn_gain[l], qr_gain[l],
                         kn_gain[l], kr_gain[l], w_out[l])
    return x


def setup_inputs(seed=0):
    out = dict(first_inputs(seed))
    for name, value in second_inputs(seed + 1).items():
        if name != "x":
            out[name + "_2"] = value
    return out


def reference(
    x, mix_norm_g, w_in, gate_b, sc_conv_w, sc_out, sb_out, rw_mu, rw_w0, rw_w2, rw_a0, rw_a2,
    rw_g2, rw_k_k, rw_k_a, rw_r_k, rw_gn_g, rw_gn_b, rw_out, sg_ln_g, sg_ln_b, sg_w, sg_b,
    sg_out, w_o, ffn_norm_g, w_up, ffn_conv_w, w_down, final_norm_g, positions_2, rel_bias_2,
    norm_gain_2, w_in_2, a_q_gain_2, a_k_gain_2, q_c_gain_2, w_uq_2, kv_c_gain_2, w_ukv_2,
    qn_gain_2, qr_gain_2, kn_gain_2, kr_gain_2, w_out_2,
):
    x = first_block(
        x, mix_norm_g, w_in, gate_b, sc_conv_w, sc_out, sb_out, rw_mu, rw_w0, rw_w2, rw_a0,
        rw_a2, rw_g2, rw_k_k, rw_k_a, rw_r_k, rw_gn_g, rw_gn_b, rw_out, sg_ln_g, sg_ln_b, sg_w,
        sg_b, sg_out, w_o, ffn_norm_g, w_up, ffn_conv_w, w_down, final_norm_g,
    )
    return second_block(
        x, positions_2, rel_bias_2, norm_gain_2, w_in_2, a_q_gain_2, a_k_gain_2, q_c_gain_2,
        w_uq_2, kv_c_gain_2, w_ukv_2, qn_gain_2, qr_gain_2, kn_gain_2, kr_gain_2, w_out_2,
    )


_drawn_inputs = setup_inputs


def setup_inputs(seed=0):
    import zlib

    import numpy as np

    out = dict(_drawn_inputs(seed))
    spreads = {}
    factors = {'gate_b': 3.707,
     'rw_w2': 4.082,
     'rw_a0': 7.69,
     'rw_k_k': 8.0,
     'rw_k_a': 6.841,
     'rw_gn_g': 7.526,
     'rw_gn_b': 8.0,
     'sg_ln_g': 8.0,
     'sg_ln_b': 8.0,
     'sg_b': 6.434,
     'ffn_norm_g': 2.807,
     'rel_bias_2': 8.0,
     'norm_gain_2': 6.438,
     'a_q_gain_2': 8.0,
     'a_k_gain_2': 8.0,
     'q_c_gain_2': 8.0,
     'kv_c_gain_2': 8.0,
     'qn_gain_2': 8.0,
     'qr_gain_2': 8.0,
     'kn_gain_2': 8.0,
     'kr_gain_2': 8.0}
    for name, (base, spread) in spreads.items():
        noise = np.random.default_rng([zlib.crc32(name.encode()), seed]).standard_normal(out[name].shape)
        drawn = base * np.exp(spread * noise) if base else spread * noise
        out[name] = jnp.asarray(drawn.astype(out[name].dtype))
    for name, factor in factors.items():
        out[name] = (out[name] * factor).astype(out[name].dtype)
    return out
```

```python
import math
from contextlib import ExitStack

import numpy as np
import concourse.bass as bass
from concourse import mybir

P = 128
T = 1024
D = 1024
KT = D // P
HALF = 512
NB = T // P
BW = 256
BT = BW // P
C = 64
NCH = T // C
FT = 22
HEADS_A = 8
HEADS_B = 8
DQK = 96
RMS_EPS = 1e-6
LN_EPS = 1e-5
GN_EPS = 64e-5
DECAY = math.exp(-0.5)
NEG = -1e30
UNITS = 64
ROUND = 1.5 * 2.0 ** 23
TURN = (6.28125, 0.0019350051879882812, 3.0198944141e-07)
PI_IN = 3.1415925

ALU = mybir.AluOpType
ACT = mybir.ActivationFunctionType
F32 = mybir.dt.float32
FR = mybir.dt.float32r
I32 = mybir.dt.int32
AX = mybir.AxisListType.X

ROWS = {}
_n = 0
for _name, _count in (("mix_g", 8), ("gate_b", 32), ("sc_w", 6), ("mu", 8), ("w0", 2), ("a0", 2),
                      ("k_k", 2), ("k_a", 2), ("r_k", 2), ("ffn_g", 8), ("fin_g", 8), ("g2", 8),
                      ("q_c", 2), ("kv_c", 1), ("a_q", 1), ("a_k", 1), ("qn", 1), ("kn", 1)):
    ROWS[_name] = _n
    _n += _count
assert _n <= P
ROWS["conv"] = P
NCOL = P + 3 * 2 * FT

T_IN = 0
T_GATE = 24
T_BR = 56
T_WO = 64
T_FFN = 72
T_IN2 = T_FFN + 6 * (FT // 2)
T_UQ = T_IN2 + 24
T_UKV = T_UQ + 2
T_OUT = T_UKV + 1
T_END = T_OUT + 8
P_IN = 0
P_GATE = 24
P_BR = 56
P_WO = P_BR + 32
P_FFN = P_WO + 8
P_IN2 = P_FFN + 12 * (FT // 2)
P_UQ = P_IN2 + 24
P_UKV = P_UQ + 8
P_OUT = P_UKV + 8
P_END = P_OUT + 8


def outs_through(t):
    if t < T_BR:
        return t + 1
    if t < T_WO:
        return P_BR + 4 * (t - T_BR + 1)
    if t < T_FFN:
        return P_WO + (t - T_WO + 1)
    if t < T_IN2:
        n = t - T_FFN
        if n < 4:
            return P_FFN + n + 1
        f, u = divmod(n - 4, 6)
        if f == FT // 2 - 1:
            return P_FFN + 4 + 12 * f + 4 * (u + 1)
        return P_FFN + 4 + 12 * f + (1, 5, 9, 10, 11, 12)[u]
    if t < T_UQ:
        return P_IN2 + (t - T_IN2 + 1)
    if t < T_UKV:
        return P_UQ + 4 * (t - T_UQ + 1)
    if t < T_OUT:
        return P_UKV + 8
    return P_OUT + (t - T_OUT + 1)


def ffn_block(t):
    n = t - T_FFN
    if n < 4:
        f, u = 0, (0, 3, 4, 5)[n]
    else:
        f, u = 1 + (n - 4) // 6, (n - 4) % 6
        if f == FT // 2:
            u += 1
    if u in (1, 2):
        return "down", 2 * (f - 1), u - 1
    j = 2 * f + (u > 3)
    return "up", P * j + (P * FT if u in (3, 5) else 0)


def block_dmas(t):
    if T_BR <= t < T_WO or t == T_IN2 + 19:
        return 4
    return 1


def loaded_value(t):
    return 16 * sum(block_dmas(s) for s in range(t % 2, t + 1, 2))


def block_columns(t):
    return 768 if T_UQ <= t < T_UKV else 1024


def frees_before(p):
    return p // 2 if p < P_GATE else P_GATE // 2 + (p - P_BR) // 2


def merge_adds(q):
    return 3 * (q // 4) + q % 4


PRM_DMAS = 14 + 8 + 2
PAR_DMAS = 4 + 6

SEMS = (
    "w_split", "prm_clear", "prm_in", "rel_in", "par_in", "h_ready", "x_out", "gate_ready",
    "y_split", "p_ready", "bias_rows", "bias_out", "at_s", "q_split", "kv_split", "pos_in",
    "at_pt_copied", "out_taken", "consts", "wsg_copied", "wsg_ready", "rk_m", "rk_p", "rk_lv",
    "merge_add", "mla_ones", "causal", "square", "square_used", "col_t", "wsg_t", "cols", "x_t",
    "h_split", "v_turned", "v_taken", "sg_normed", "sg_mixed", "sg_done", "sb_z_free", "sb_z",
    "sb_pt_copied", "sb_p_cut", "sb_pt", "sb_o", "sb_o_copied", "sb_y_free", "sb_y", "rk_lora",
    "rk_g_free", "rk_lora_p", "rk_kk2", "rk_bonus", "rk_bonus_p", "rk_bonus_taken", "rk_prep",
    "rk_tok_t", "rk_mats", "rk_mats_done", "rk_copied", "rk_x", "rk_x_added", "rk_nv", "rk_xnv",
    "rk_round", "rk_round_act", "rk_state", "rk_chain", "rk_u_added", "rk_y", "rk_y_ready",
    "rk_y_t", "m_split", "g_split", "bias_p", "n2_sq", "n2_ss", "n2_q", "at_z", "at_p", "at_pt",
    "at_o_taken", "at_o", "z_done", "z_turned", "c_sq", "c_ss", "c_root", "rot", "krope_normed",
    "rot_used", "hn_sq", "hn_ss", "hn_done", "vb_turned", "vb_taken", "k_rope_spread",
    "mix_split", "out_t", "w_high", "root", "high", "x_turned0", "x_turned1", "sc_done",
    "sg_var", "sg_root", "sb_l", "sb_p", "rk_shift", "rk_kk1", "rk_w", "rk_pow", "rk_cum",
    "rk_tok0", "rk_gvar", "rk_groot", "c_first", "silu", "g_raw", "g_high", "at_m", "kv_normed",
    "q_normed", "angles", "hn_rt", "x_normed", "p_free0", "p_free1", "sb_sp", "sb_sp_cut",
    "rk_tok1", "conv_mid", "n2_rt", "w_loaded0", "w_loaded1", "x_in0", "x_in1", "gate_stored0",
    "gate_stored1", "gate_in0", "gate_in1", "gate_in2", "gate_in3", "x_back0", "x_back1",
    "table_in0", "table_in1", "stored0", "stored1", "pool_own", "act_own", "dve_own",
)


def hybrid_layers(nc, x, mix_norm_g, w_in, gate_b, sc_conv_w, sc_out, sb_out, rw_mu, rw_w0, rw_w2,
                  rw_a0, rw_a2, rw_g2, rw_k_k, rw_k_a, rw_r_k, rw_gn_g, rw_gn_b, rw_out, sg_ln_g,
                  sg_ln_b, sg_w, sg_b, sg_out, w_o, ffn_norm_g, w_up, ffn_conv_w, w_down,
                  final_norm_g, positions_2, rel_bias_2, norm_gain_2, w_in_2, a_q_gain_2,
                  a_k_gain_2, q_c_gain_2, w_uq_2, kv_c_gain_2, w_ukv_2, qn_gain_2, qr_gain_2,
                  kn_gain_2, kr_gain_2, w_out_2, bucket_table, rope_freq, out):
    x_spill = nc.dram_tensor("x_spill", [P, KT, T], F32, kind="Internal").ap()
    gates_spill = nc.dram_tensor("gates_spill", [32, P, T], F32, kind="Internal").ap()
    bias_spill = nc.dram_tensor("bias_spill", [HEADS_A, P, 1152], F32, kind="Internal").ap()

    with ExitStack() as ctx:
        base = [-(-nc.sbuf_base // 32) * 32]

        def at(name, shape, dtype, offset):
            return nc.alloc_sbuf_tensor_at(name, shape, dtype, offset=offset)

        def fixed(name, shape, dtype=F32):
            size = int(np.prod(shape[1:])) * 4
            h = at(name, shape, dtype, base[0])
            base[0] += -(-size // 32) * 32
            return h

        ident = fixed("ident", [P, P])
        ones = fixed("ones", [P, P])
        head_ones = fixed("head_ones", [P, P])
        rope_turn = fixed("rope_turn", [P, 32])
        mask_s = fixed("mask_s", [P, P])
        mask_i = fixed("mask_i", [P, P])
        level = [fixed(f"level{n}", [P, P]) for n in range(6)]
        level0_t = fixed("level0_t", [P, P])
        group_sel = fixed("group_sel", [4, 2, P])
        col = fixed("col", [P, NCOL])
        k_a_rest = fixed("k_a_rest", [P, 2])
        a_q_scaled = fixed("a_q_scaled", [P, 1])
        row_g = fixed("row_g", [P, 4, BW])
        lora = fixed("lora", [P, 2, BW])
        sg_bias = fixed("sg_bias", [4, P])
        rel_rows = fixed("rel_rows", [33, HEADS_A])
        small = fixed("small", [P, 128])
        ones_row = fixed("ones_row", [P, T])
        mla_ones = fixed("mla_ones", [DQK, DQK])
        freq = fixed("freq", [P, 1])

        X0 = base[0]
        x_t = at("x_t", [P, KT, T], F32, X0)
        W0 = X0 + 32768
        w_raw = at("w_raw", [P, 2, 1024], F32, W0)
        w_hi = at("w_hi", [P, 2, 1024], FR, W0 + 8192)
        w_lo = at("w_lo", [P, 2, 1024], FR, W0 + 16384)
        H0 = W0 + 24576
        h_hi = at("h_hi", [P, KT, T], FR, H0)
        h_lo = at("h_lo", [P, KT, T], FR, H0 + 32768)
        A0 = H0 + 65536
        K = 1024

        x_tok = at("x_tok", [P, NB, D], F32, A0)
        squares = at("squares", [P, 2, T], F32, A0 + 40 * K)
        root = at("root", [P, T], F32, A0 + 48 * K)
        rstd = at("rstd", [P, T], F32, A0 + 52 * K)
        h_tmp = at("h_tmp", [P, 2, T], F32, A0 + 56 * K)
        prm = at("prm", [P, 3, P], F32, A0 + 32 * K)
        sg_w_raw = at("sg_w_raw", [P, 4, P], F32, A0 + 36 * K)
        y_a = at("y_a", [P, BT, T], F32, A0)
        y_d = at("y_d", [P, BT, T], F32, A0 + 8 * K)
        q_sb = at("q_sb", [P, BT, T], F32, A0 + 16 * K)
        k_sb = at("k_sb", [P, BT, T], F32, A0 + 24 * K)
        v_sb = at("v_sb", [P, NB, BW], F32, A0 + 32 * K)
        y_b = at("y_b", [P, BT, T], F32, A0 + 40 * K)
        y_c = at("y_c", [P, BT, T], F32, A0 + 48 * K)
        zr = at("zr", [P, 8, T], F32, X0)
        sc_c = at("sc_c", [P, BT, T], F32, A0 + 48 * K)
        sc_cx = at("sc_cx", [P, BT, T], F32, A0 + 56 * K)
        vt_sb = at("vt_sb", [P, BT, T], F32, A0 + 56 * K)
        vt_sg = at("vt_sg", [P, BT, T], F32, A0 + 56 * K)
        v_sg = at("v_sg", [P, NB, BW], F32, A0 + 40 * K)
        w_sg = at("w_sg", [P, 4, P], F32, A0 + 64 * K)
        gate_out = at("gate_out", [P, 2, T], F32, A0 + 56 * K)
        sb_l = at("sb_l", [P, 2, T], F32, H0)
        sb_sp = at("sb_sp", [P, 2, T], F32, H0 + 8 * K)
        sb_sum = at("sb_sum", [P, 2, T], F32, H0 + 16 * K)
        sb_p = at("sb_p", [P, 2, T], F32, H0 + 24 * K)
        sb_pt = at("sb_pt", [P, 2, T], F32, H0 + 32 * K)
        sb_o = at("sb_o", [P, 2, BW], F32, H0 + 40 * K)
        rk_a = at("rk_a", [P, T], F32, H0)
        rk_b = at("rk_b", [P, T], F32, H0 + 4 * K)
        rk_kk = at("rk_kk", [P, T], F32, H0 + 8 * K)
        rk_l = at("rk_l", [P, T], F32, H0 + 12 * K)
        rk_lx = at("rk_lx", [P, T], F32, H0 + 16 * K)
        rk_e = at("rk_e", [P, T], F32, H0 + 20 * K)
        rk_f = at("rk_f", [P, T], F32, H0 + 24 * K)
        rk_sg = at("rk_sg", [P, T], F32, H0 + 28 * K)
        rk_th = at("rk_th", [P, T], F32, H0 + 32 * K)
        a_tok = at("a_tok", [P, NB, P], F32, H0 + 36 * K)
        b_tok = at("b_tok", [P, NB, P], F32, H0 + 40 * K)
        k_tok = at("k_tok", [P, NB, P], F32, H0 + 44 * K)
        v_tok = at("v_tok", [P, NB, P], F32, H0 + 48 * K)
        xa_t = at("xa_t", [P, T], F32, H0 + 52 * K)
        xnv = at("xnv", [P, NB, P], F32, H0 + 56 * K)
        y_loc = at("y_loc", [P, NB, P], F32, H0 + 60 * K)
        g_tok = at("g_tok", [P, NB, P], F32, H0 + 28 * K)
        rb_t = at("rb_t", [P, 2, NB, P], F32, A0 + 16 * K)
        y_tok = at("y_tok", [P, NB, P], F32, A0 + 24 * K)
        u_tok = at("u_tok", [P, NB, P], F32, A0 + 28 * K)
        s_all = at("s_all", [P, NCH + 1, C], F32, A0 + 32 * K)
        m_t = at("m_t", [P, 2, 4, P], F32, H0 + 8 * K)
        m_lv = at("m_lv", [P, 2, 4, P], F32, H0 + 12 * K)
        inv = at("inv", [P, 2, 4, P], F32, H0 + 16 * K)
        inv_t = at("inv_t", [P, 2, 4, P], F32, H0 + 20 * K)
        m_p = at("m_p", [P, 2, 4, P], F32, H0 + 24 * K)
        n_t = at("n_t", [P, 2, 4, P], F32, A0 + 56 * K)
        rk_t = at("rk_t", [P, 2, 4, P], F32, A0 + 60 * K)
        nv = at("nv", [P, 2, 4, C], F32, A0 + 64 * K)
        y_sq = at("y_sq", [P, NB, P], F32, H0 + 8 * K)
        y_hi = at("y_hi", [P, 8, T], FR, H0)
        y_lo = at("y_lo", [P, 8, T], FR, H0 + 32768)

        gate_in = at("gate_in", [P, 4, T], F32, A0)
        merged = at("merged", [P, 2, T], F32, A0 + 16 * K)
        gated = at("gated", [P, 2, T], F32, A0 + 24 * K)
        m_hi = at("m_hi", [P, KT, T], FR, X0)
        m_lo = at("m_lo", [P, KT, T], FR, A0 + 32 * K)
        x_back = at("x_back", [P, 2, T], F32, H0)
        x_mid = at("x_mid", [P, KT, T], F32, A0)
        hid = at("hid", [P, 4, T], F32, A0 + 32 * K)
        g_hi = at("g_hi", [P, 2, T], FR, X0)
        g_lo = at("g_lo", [P, 2, T], FR, X0 + 8 * K)
        q_2 = at("q_2", [P, 4, T], F32, X0)
        k_2 = at("k_2", [P, 4, T], F32, X0 + 16 * K)
        v_2 = at("v_2", [P, NB, 512], F32, A0)
        z_a = at("z_a", [P, 4, T], F32, A0 + 16 * K)
        vt_2 = at("vt_2", [P, 4, T], F32, A0 + 32 * K)
        z_b = at("z_b", [P, 4, T], F32, A0 + 32 * K)
        c_q = at("c_q", [P, 2, T], F32, A0 + 48 * K)
        c_kv = at("c_kv", [P, T], F32, A0 + 56 * K)
        k_rope = at("k_rope", [P, T], F32, A0 + 60 * K)
        nsq = at("nsq", [P, 2, T], F32, H0)
        nrt = at("nrt", [P, 2, T], F32, H0 + 8 * K)
        table = at("table", [P, 2, T], F32, H0 + 16 * K)
        buckets = at("buckets", [33, 1152], F32, H0 + 24 * K)
        bias_vec = at("bias_vec", [HEADS_A, 1152], F32, H0 + 48 * K)
        att_s = at("att_s", [P, 2, T], F32, H0 + 32 * K)
        att_pt = at("att_pt", [P, 2, T], F32, H0 + 40 * K)
        o_all = at("o_all", [P, NB, 512], F32, H0 + 48 * K)
        cq_hi = at("cq_hi", [P, 2, T], FR, H0 + 32 * K)
        cq_lo = at("cq_lo", [P, 2, T], FR, H0 + 40 * K)
        ckv_hi = at("ckv_hi", [P, 1, T], FR, H0 + 48 * K)
        ckv_lo = at("ckv_lo", [P, 1, T], FR, H0 + 52 * K)
        cos_t = at("cos_t", [P, T], F32, A0 + 48 * K)
        sin_t = at("sin_t", [P, T], F32, A0 + 52 * K)
        pos_i = at("pos_i", [P, T], I32, A0 + 56 * K)
        vb_t = at("vb_t", [P, T], F32, A0 + 56 * K)
        nsq_b = at("nsq_b", [P, T], F32, H0 + 56 * K)
        hn_root = at("hn_root", [P, T], F32, H0 + 60 * K)
        qh = at("qh", [DQK, HEADS_B, T], F32, X0)
        kh = at("kh", [DQK, HEADS_B, T], F32, H0)
        v_b = at("v_b", [P, NB, 512], F32, A0)
        causal = at("causal", [P, T], F32, H0 + 48 * K)
        o_b = at("o_b", [P, 2, 512], F32, H0 + 52 * K)
        mix_hi = at("mix_hi", [P, KT, T], FR, X0)
        mix_lo = at("mix_lo", [P, KT, T], FR, H0)
        x_back2 = at("x_back2", [P, 2, T], F32, H0 + 32 * K)
        x_out = at("x_out", [P, 2, T], F32, H0 + 40 * K)
        out_tok = at("out_tok", [P, 2, NB, P], F32, H0 + 48 * K)

        gp = ctx.enter_context(nc.psum_tensor("gp", [P, 2, T], F32))
        sm = ctx.enter_context(nc.psum_tensor("sm", [P, 4, HALF], F32))

        s = {name: ctx.enter_context(nc.semaphore(name)) for name in SEMS}
        block = ctx.enter_context(nc.Block())

        def pcol(name, n=0):
            c = ROWS[name] + n
            return col[:, c:c + 1]

        def raw_block(slot, k, a=0, b=None):
            n = 1024 // k
            return w_raw[:, slot, 0:k * n].rearrange("p (k c) -> p k c", k=k)[:, :, a:b]

        def weight_dmas(t):
            def tile(w, c, n=P):
                return w[:, c:c + n].rearrange("(k p) c -> p k c", p=P)
            z = t % 2
            if t < T_BR:
                return [(raw_block(z, 8), tile(w_in[0], P * t))]
            if t < T_WO:
                return [(w_raw[:, z, 256 * n:256 * n + 256].rearrange("p (k c) -> p k c", k=2),
                         tile(w[0], P * (t - T_BR)))
                        for n, w in enumerate((sc_out, sb_out, rw_out, sg_out))]
            if t < T_FFN:
                return [(raw_block(z, 8), tile(w_o[0], P * (t - T_WO)))]
            if t < T_IN2:
                kind, a, *half = ffn_block(t)
                if kind == "up":
                    return [(raw_block(z, 8), tile(w_up[0], a))]
                return [(raw_block(z, 2), tile(w_down[0][P * a:P * a + 2 * P], HALF * half[0], HALF))]
            n = t - T_IN2
            if t < T_UQ and n == 19:
                return [(raw_block(z, 8, 32 * r, 32 * r + 32), tile(w_in_2[0], 19 * P, 32))
                        for r in range(4)]
            if t < T_UQ:
                c = P * n if n < 19 else 19 * P + 32 + P * (n - 20)
                return [(raw_block(z, 8), tile(w_in_2[0], c))]
            if t < T_UKV:
                return [(w_raw[:, z, 0:768].rearrange("p (k c) -> p k c", k=2),
                         tile(w_uq_2[0], 4 * DQK * (t - T_UQ), 4 * DQK))]
            if t < T_OUT:
                return [(w_raw[:, z, :], w_ukv_2[0])]
            return [(raw_block(z, 8), tile(w_out_2[0], P * (t - T_OUT)))]

        class Waits:

            def __init__(self, eng, own):
                self.eng, self.own, self.seen = eng, own, {}

            def __call__(self, name, n=1):
                self.seen[name] = self.seen.get(name, 0) + n
                self.eng.wait_ge(s[name], self.seen[name])

            def after(self, ins):
                ins.then_inc(s[self.own], 1)
                self(self.own)

        def bank(b):
            if b < 4:
                return sm[:, b, :]
            return gp[:, (b - 4) // 2, HALF * (b % 2):HALF * (b % 2) + HALF]

        def o_place(n):
            c = HALF * (n % 2) + C * (n // 2 % 8)
            return gp[:, 1, c:c + C]

        @block.sync
        def _(sp):
            wait = Waits(sp, None)

            def load_weights(t):
                if t >= 2:
                    sp.wait_ge(s["w_split"], t - 1)
                for dst, src in weight_dmas(t):
                    sp.dma_start(dst, src).then_inc(s[f"w_loaded{t % 2}"], 16)

            wait("prm_clear")
            rows = [("mix_g", mix_norm_g[0]), ("gate_b", gate_b[0]), ("sc_w", sc_conv_w[0]),
                    ("mu", rw_mu[0]), ("w0", rw_w0[0]), ("a0", rw_a0[0]), ("k_k", rw_k_k[0]),
                    ("k_a", rw_k_a[0]), ("r_k", rw_r_k[0]), ("ffn_g", ffn_norm_g[0]),
                    ("fin_g", final_norm_g), ("g2", norm_gain_2[0]), ("q_c", q_c_gain_2[0]),
                    ("kv_c", kv_c_gain_2[0])]
            for name, a in rows:
                if name == "sc_w":
                    src = a.rearrange("w (t p) -> (w t) p", p=P)
                elif name == "r_k":
                    src = a.rearrange("(t h) p -> t (h p)", h=2)
                else:
                    src = a.rearrange("(t p) -> t p", p=P)
                r = ROWS[name]
                sp.dma_start(prm[r:r + src.shape[0], 0, :], src).then_inc(s["prm_in"], 16)
            for name, a, c in (("a_q", a_q_gain_2[0], 0), ("a_q", a_q_gain_2[0], C),
                               ("a_k", a_k_gain_2[0], 0), ("a_k", a_k_gain_2[0], C),
                               ("qn", qn_gain_2[0], 0), ("qn", qr_gain_2[0], C),
                               ("kn", kn_gain_2[0], 0), ("kn", kr_gain_2[0], C)):
                r = ROWS[name]
                sp.dma_start(prm[r:r + 1, 0, c:c + a.shape[0]],
                             a.rearrange("(o p) -> o p", o=1)).then_inc(s["prm_in"], 16)
            sp.dma_start(rel_rows[0:32, :], rel_bias_2).then_inc(s["rel_in"], 16)
            sp.dma_start(freq[:, :], rope_freq).then_inc(s["par_in"], 16)
            taps = ffn_conv_w[0].rearrange("w (t p) -> (w t) p", p=P)
            sp.dma_start(prm[:, 1, :], taps[0:P]).then_inc(s["prm_in"], 16)
            sp.dma_start(prm[0:4, 2, :], taps[P:P + 4]).then_inc(s["prm_in"], 16)
            for n, a in enumerate((sg_ln_g[0], sg_ln_b[0], rw_gn_g[0], rw_gn_b[0])):
                sp.dma_start(row_g[:, n, :], a.partition_broadcast(P)).then_inc(s["par_in"], 16)
            sp.dma_start(lora[0:64, 0, :], rw_w2[0]).then_inc(s["par_in"], 16)
            sp.dma_start(lora[64:128, 0, :], rw_a2[0]).then_inc(s["par_in"], 16)
            sp.dma_start(lora[:, 1, :], rw_g2[0]).then_inc(s["par_in"], 16)
            sp.dma_start(sg_bias[:, :], sg_b[0]).then_inc(s["par_in"], 16)
            sp.dma_start(sg_w_raw[:, :, :], sg_w[0].rearrange("g t s -> t g s")).then_inc(s["par_in"], 16)
            for tt in range(NB):
                sp.dma_start(x_tok[:, tt, :], x[0, P * tt:P * tt + P, :]).then_inc(s[f"x_in{tt // 4}"], 16)
            load_weights(0)
            load_weights(1)
            wait("h_ready", KT)
            sp.dma_start(x_spill, x_t[:, :, :]).then_inc(s["x_out"], 16)
            for t in range(2, T_GATE + 2):
                load_weights(t)
            with sp.Fori(0, 15) as i:
                for z in range(2):
                    sp.wait_ge(s["w_split"], 2 * i + (T_GATE + z + 1))
                    c = i * (2 * P) + P * (T_GATE + 2 + z)
                    sp.dma_start(raw_block(z, 8), w_in[0][:, bass.ds(c, P)]
                                 .rearrange("(k p) c -> p k c", p=P)).then_inc(s[f"w_loaded{z}"], 16)
                    sp.wait_ge(s["gate_ready"], 2 * i + (z + 1))
                    sp.dma_start(gates_spill[bass.ds(2 * i + z, 1)].rearrange("a p t -> p (a t)"),
                                 gate_out[:, z, :]).then_inc(s[f"gate_stored{z}"], 16)
            for z in range(2):
                load_weights(T_BR + z)
                sp.wait_ge(s["gate_ready"], 31 + z)
                sp.dma_start(gates_spill[30 + z], gate_out[:, z, :]).then_inc(s[f"gate_stored{z}"], 16)
            sp.wait_ge(s["y_split"], 8)
            for z in range(2):
                sp.wait_ge(s[f"gate_stored{z}"], 16 * 16)
            for d in range(KT):
                for n in range(4):
                    if d:
                        p = P_BR + 4 * (d - 1) + n
                        sp.wait_ge(s[f"p_free{p % 2}"], frees_before(p) + 1)
                    sp.dma_start(gate_in[:, n, :], gates_spill[8 * n + d]).then_inc(s[f"gate_in{n}"], 16)
                load_weights(T_BR + 2 + d)
            sp.wait_ge(s["p_ready"], P_WO)
            for d in range(KT):
                if d >= 2:
                    p = P_WO + d - 2
                    sp.wait_ge(s[f"p_free{p % 2}"], frees_before(p) + 1)
                sp.dma_start(x_back[:, d % 2, :], x_spill[:, d, :]).then_inc(s[f"x_back{d % 2}"], 16)
                load_weights(T_WO + 2 + d)
            load_weights(T_FFN + 2)
            load_weights(T_FFN + 3)
            with sp.Fori(0, FT // 2 - 1) as i:
                for u in range(6):
                    sp.wait_ge(s["w_split"], 6 * i + (T_FFN + 3 + u))
                    kind, a, *half = ffn_block(T_FFN + 4 + u)
                    if kind == "up":
                        dst, src = raw_block(u % 2, 8), w_up[0][:, bass.ds(2 * P * i + a, P)]
                    else:
                        c = HALF * half[0]
                        dst, src = raw_block(u % 2, 2), w_down[0][bass.ds(2 * P * i + P * a, 2 * P), c:c + HALF]
                    sp.dma_start(dst, src.rearrange("(k p) c -> p k c", p=P)).then_inc(s[f"w_loaded{u % 2}"], 16)
            for t in range(T_IN2 - 2, T_IN2 + 2):
                load_weights(t)
            sp.wait_ge(s["h_ready"], 3 * KT)
            sp.dma_start(x_spill, x_mid[:, :, :]).then_inc(s["x_out"], 16)
            for t in range(T_IN2 + 2, T_UKV + 1):
                load_weights(t)
            sp.wait_ge(s["p_ready"], P_UQ)
            sp.dma_start(buckets[:, :], bucket_table).then_inc(s["rel_in"], 16)
            sp.wait_ge(s["bias_rows"], 1)
            sp.dma_start(bias_spill, bias_vec[:, :].unsqueeze(1).to_broadcast([HEADS_A, P, 1152])).then_inc(s["bias_out"], 16)
            sp.wait_ge(s["bias_out"], 16)
            for h in range(HEADS_A):
                if h >= 2:
                    sp.wait_ge(s["at_s"], NB * (h - 1))
                skew = bass.AP(tensor=bias_spill.tensor, offset=1152 * P * h + 127, ap=[[1151, P], [1, T]])
                sp.dma_start(table[:, h % 2, :], skew).then_inc(s[f"table_in{h % 2}"], 16)
            sp.wait_ge(s["q_split"], 2)
            sp.wait_ge(s["kv_split"], 1)
            sp.dma_start(pos_i[C:C + 32, :], positions_2[0].partition_broadcast(32)).then_inc(s["pos_in"], 16)
            load_weights(T_OUT)
            load_weights(T_OUT + 1)
            for d in range(KT):
                if d == 0:
                    sp.wait_ge(s["at_pt_copied"], 2 * UNITS)
                else:
                    wait("out_taken")
                if d >= 2:
                    p = P_OUT + d - 2
                    sp.wait_ge(s[f"p_free{p % 2}"], frees_before(p) + 1)
                if d + 2 < KT:
                    load_weights(T_OUT + 2 + d)
                sp.dma_start(x_back2[:, d % 2, :], x_spill[:, d, :]).then_inc(s[f"x_back{d % 2}"], 16)
                if d:
                    sp.dma_start(out[0][:, P * (d - 1):P * d].rearrange("(n p) c -> p n c", p=P),
                                 out_tok[:, (d - 1) % 2]).then_inc(s[f"stored{(d - 1) % 2}"], 16)
            wait("out_taken")
            d = KT
            sp.dma_start(out[0][:, P * (d - 1):P * d].rearrange("(n p) c -> p n c", p=P),
                         out_tok[:, (d - 1) % 2]).then_inc(s[f"stored{(d - 1) % 2}"], 16)
            for z in range(2):
                sp.wait_ge(s[f"stored{z}"], 16 * KT // 2)

        @block.gpsimd
        def _(pool):
            wait = Waits(pool, "pool_own")

            def select(view, pattern, base, mult, compare=ALU.is_ge, fill=0.0):
                wait.after(pool.affine_select(out=view, in_=view, pattern=pattern, compare_op=compare,
                                              fill=fill, base=base, channel_multiplier=mult))

            wait.after(pool.memset(rel_rows[:, :], 1.0))
            pool.memset(prm[:, :, :], 0.0).then_inc(s["prm_clear"], 1)
            wait.after(pool.memset(ident[:, :], 0.0))
            select(ident[:, :], [[-1, P]], 0, 1, ALU.not_equal, 1.0)
            wait.after(pool.memset(ones[:, :], 1.0))
            wait.after(pool.memset(ones_row[:, :], 1.0))
            wait.after(pool.memset(head_ones[:, :], 1.0))
            select(head_ones[:, 0:C], [[0, C]], C - 1, -1)
            select(head_ones[:, C:P], [[0, C]], -C, 1)
            for m, off in ((mask_s, -1), (mask_i, 0)):
                wait.after(pool.tensor_copy(m[:, :], head_ones[:, :]))
                select(m[:, :], [[1, P]], off, -1)
            for n, m in enumerate(level):
                b = 2 ** n
                wait.after(pool.memset(m[:, :], 0.0))
                view = m[:, :].rearrange("p (k h c) -> p k h c", h=2, c=b)[:, :, 1, :]
                wait.after(pool.memset(view, 1.0))
                select(view, [[-2 * b, P // (2 * b)], [0, b]], 0, 1)
                select(view, [[2 * b, P // (2 * b)], [0, b]], b - 1, -1)
            wait.after(pool.memset(level0_t[:, :], 0.0))
            view = level0_t[:, :].rearrange("p (k h) -> p k h", h=2)[:, :, 0]
            wait.after(pool.memset(view, 1.0))
            select(view, [[-2, P // 2]], -1, 1, ALU.is_equal)
            wait.after(pool.memset(group_sel[:, :, :], 1.0))
            select(group_sel[:, :, :], [[P, 2], [1, P]], 0, -C)
            select(group_sel[:, :, :], [[-P, 2], [-1, P]], C - 1, C)
            wait.after(pool.memset(rope_turn[:, :], 0.0))
            select(rope_turn[:, :], [[-1, 32]], 16 - C, 1, ALU.not_equal, 1.0)
            select(rope_turn[:, :], [[-1, 32]], -16 - C, 1, ALU.not_equal, -1.0)
            pool.drain().then_inc(s["consts"], 1)

            wait("wsg_copied")
            pool.affine_select(out=w_sg[:, :, :], in_=w_sg[:, :, :], pattern=[[0, 4], [1, P]],
                               compare_op=ALU.is_ge, fill=0.0, base=0,
                               channel_multiplier=-1).then_inc(s["wsg_ready"], 1)

            for n in range(4 * NB):
                qb, z = n // 4, n % 2
                for name, buf in (("sb_sp", sb_sp), ("sb_p", sb_p)):
                    wait(name)
                    diag = buf[:, z, P * qb:P * qb + P]
                    pool.affine_select(out=diag, in_=diag, pattern=[[-1, P]], compare_op=ALU.is_gt,
                                       fill=0.0, base=0, channel_multiplier=1).then_inc(s[name + "_cut"], 1)

            for rnd in range(2 * 2):
                for n in range(1, 6):
                    for hh in range(2):
                        if n == 1:
                            wait("rk_m")
                        else:
                            wait("rk_p")
                        pool.tensor_tensor(m_lv[:, hh], m_t[:, hh],
                                           level[n][:, :].unsqueeze(1).to_broadcast([P, 4, P]),
                                           ALU.mult).then_inc(s["rk_lv"], 1)
                for hh in range(2):
                    wait("rk_p")
            for q in range(4 * KT):
                d, n = divmod(q, 4)
                if n == 0:
                    continue
                p = P_BR + q
                pool.wait_ge(s[f"p_free{p % 2}"], frees_before(p) + 1)
                if n == 1:
                    pool.wait_ge(s[f"p_free{(p - 1) % 2}"], frees_before(p - 1) + 1)
                else:
                    pool.wait_ge(s["merge_add"], merge_adds(q - 1))
                pool.tensor_tensor(merged[:, d % 2, :], merged[:, d % 2, :], gated[:, q % 2, :], ALU.add) \
                    .then_inc(s["merge_add"], 1)
            pool.wait_ge(s["at_pt_copied"], UNITS)
            wait.after(pool.memset(mla_ones[:, :], 1.0 / C))
            select(mla_ones[:, 0:C], [[0, C]], C - 1, -1)
            wait.after(pool.memset(mla_ones[:, C:DQK], 1.0 / 32))
            pool.affine_select(out=mla_ones[:, C:DQK], in_=mla_ones[:, C:DQK], pattern=[[0, 32]],
                               compare_op=ALU.is_ge, fill=0.0, base=-C,
                               channel_multiplier=1).then_inc(s["mla_ones"], 1)
            pool.wait_ge(s["p_ready"], P_OUT)
            wait.after(pool.memset(causal[:, :], 0.0))
            pool.affine_select(out=causal[:, :], in_=causal[:, :], pattern=[[-1, T]], compare_op=ALU.is_ge,
                               fill=NEG, base=T - P, channel_multiplier=1).then_inc(s["causal"], 1)

        @block.tensor
        def _(pe):
            wait = Waits(pe, None)

            def product(p, weights, rows, hi, lo, k0=0):
                n = len(weights)
                for half in range(2):
                    c = slice(HALF * half, HALF * half + HALF)
                    o = gp[0:rows, p % 2, c]
                    for k, (wh, wl) in enumerate(weights):
                        pe.matmul(o, wh, hi[:, k0 + k, c], start=(k == 0), stop=False)
                        pe.matmul(o, wh, lo[:, k0 + k, c], start=False, stop=False)
                        mm = pe.matmul(o, wl, hi[:, k0 + k, c], start=False, stop=(k == n - 1))
                return mm

            def ring(t, a, b):
                return w_hi[:, t % 2, a:b], w_lo[:, t % 2, a:b]

            def whole(t, p, hi, lo):
                pe.wait_ge(s["w_split"], t + 1)
                if p >= 2:
                    pe.wait_ge(s[f"p_free{p % 2}"], frees_before(p))
                product(p, [ring(t, P * k, P * k + P) for k in range(8)], P, hi, lo) \
                    .then_inc(s["p_ready"], 1)

            def norm(n):
                for k in range(KT):
                    wait("square")
                    for half in range(2):
                        mm = pe.matmul(sm[:, half, :], ones[:, :], squares[:, k % 2, HALF * half:HALF * half + HALF],
                                       start=(k == 0), stop=(k == KT - 1), skip_group_check=True)
                    mm.then_inc(s["square_used"], 1)

            wait("consts")
            pe.wait_ge(s["prm_in"], 16 * PRM_DMAS)
            for n in range(3):
                r = P if n < 2 else 4
                mm = pe.transpose(sm[:, 0, P * n:P * n + r], prm[0:r, n, :], ident[0:r, 0:r])
            mm.then_inc(s["col_t"], 1)
            pe.wait_ge(s["par_in"], 16 * PAR_DMAS)
            for g in range(4):
                mm = pe.transpose(sm[:, 1, P * g:P * g + P], sg_w_raw[:, g, :], ident[:, :])
            mm.then_inc(s["wsg_t"], 1)
            wait("wsg_copied")
            wait("cols")
            for b in range(16):
                half, k = divmod(b, 8)
                if k == 0:
                    pe.wait_ge(s[f"x_in{half}"], 64)
                if b >= 4:
                    wait(f"x_turned{b % 2}")
                for n in range(4):
                    mm = pe.transpose(sm[:, b % 4, P * n:P * n + P],
                                      x_tok[:, 4 * half + n, P * k:P * k + P], ident[:, :])
                mm.then_inc(s["x_t"], 1)
            for b in range(4):
                wait(f"x_turned{b % 2}")
            norm(0)
            wait("h_split", KT)
            for t in range(T_GATE):
                whole(t, t, h_hi, h_lo)
                if t == 13:
                    for b in range(4):
                        ft, half = divmod(b, 2)
                        for n in range(4):
                            mm = pe.transpose(sm[:, b, P * n:P * n + P],
                                              vt_sb[:, ft, P * (4 * half + n):P * (4 * half + n) + P], ident[:, :])
                        mm.then_inc(s["v_turned"], 1)
            for z in range(2):
                pe.wait_ge(s[f"p_free{z}"], P_GATE // 2)
            wait("v_taken", 4)
            for b in range(4):
                ft, half = divmod(b, 2)
                for n in range(4):
                    mm = pe.transpose(sm[:, b, P * n:P * n + P],
                                      vt_sg[:, ft, P * (4 * half + n):P * (4 * half + n) + P], ident[:, :])
                mm.then_inc(s["v_turned"], 1)
            wait("sg_normed")
            wait("wsg_ready")
            for b in range(4):
                ft, half = divmod(b, 2)
                for n in range(4):
                    tt = 4 * half + n
                    c = slice(P * n, P * n + P)
                    pe.matmul(sm[:, b, c], group_sel[:, ft, :], sg_bias[:, :], start=True, stop=False,
                              skip_group_check=True)
                    for hh in range(2):
                        g = 2 * ft + hh
                        mm = pe.matmul(sm[C * hh:C * hh + C, b, c], v_sg[:, tt, C * g:C * g + C], w_sg[:, g, :],
                                       start=False, stop=True, skip_group_check=True)
                mm.then_inc(s["sg_mixed"], 1)
            for z in range(2):
                pe.wait_ge(s["w_split"], T_GATE + z + 1)
                product(z, [ring(z, P * k, P * k + P) for k in range(8)], P, h_hi, h_lo) \
                    .then_inc(s["p_ready"], 1)
            with pe.Fori(1, 16) as i:
                for z in range(2):
                    pe.wait_ge(s["w_split"], 2 * i + (T_GATE + z + 1))
                    pe.wait_ge(s["gate_ready"], 2 * i + (z - 1))
                    product(z, [ring(z, P * k, P * k + P) for k in range(8)], P, h_hi, h_lo) \
                        .then_inc(s["p_ready"], 1)
            wait("sg_done", 4)
            pe.wait_ge(s["gate_ready"], 32)

            units = [(qb, h) for qb in range(NB) for h in range(4)]

            def sb_scores(n):
                qb, h = units[n]
                hh, ft = h % 2, h // 2
                if n >= 2:
                    wait("sb_z_free")
                w = P * (qb + 1)
                for a in range(0, w, HALF):
                    m = min(HALF, w - a)
                    mm = pe.matmul(sm[:, 2 * (n % 2) + a // HALF, 0:m],
                                   q_sb[C * hh:C * hh + C, ft, P * qb:P * qb + P],
                                   k_sb[C * hh:C * hh + C, ft, a:a + m], start=True, stop=True)
                mm.then_inc(s["sb_z"], 1)

            def sb_values(n):
                qb, h = units[n]
                if n >= 1:
                    wait("sb_pt_copied")
                wait("sb_p_cut")
                for k in range(qb + 1):
                    mm = pe.transpose(gp[:, 0, P * k:P * k + P], sb_p[:, n % 2, P * k:P * k + P], ident[:, :])
                mm.then_inc(s["sb_pt"], 1)

            def sb_output(n):
                qb, h = units[n]
                pe.wait_ge(s["sb_pt_copied"], n + 1)
                for k in range(qb + 1):
                    mm = pe.matmul(gp[:, 1, C * h:C * h + C], sb_pt[:, n % 2, P * k:P * k + P],
                                   v_sb[:, k, C * h:C * h + C], start=(k == 0), stop=(k == qb),
                                   skip_group_check=True)
                if h == 3:
                    mm.then_inc(s["sb_o"], 1)

            def sb_turn(qb):
                wait("sb_o_copied")
                if qb >= 1:
                    wait("sb_y_free")
                for ft in range(2):
                    mm = pe.transpose(gp[:, 1, HALF + P * ft:HALF + P * ft + P],
                                      sb_o[:, qb % 2, P * ft:P * ft + P], ident[:, :])
                mm.then_inc(s["sb_y"], 1)

            sb_scores(0)
            for n in range(len(units)):
                if n + 1 < len(units):
                    sb_scores(n + 1)
                sb_values(n)
                sb_output(n)
                if n % 4 == 3:
                    sb_turn(n // 4)
            wait("sb_y_free")

            for ft in range(2):
                wait("rk_lora")
                if ft:
                    wait("rk_g_free")
                for half in range(2):
                    c = slice(HALF * half, HALF * half + HALF)
                    pe.matmul(gp[:, 0, c], lora[0:C, 0, P * ft:P * ft + P], rk_th[0:C, c], start=True, stop=True)
                    mm = pe.matmul(gp[:, 1, c], lora[C:P, 0, P * ft:P * ft + P], zr[C:P, 6, c], start=True, stop=True)
                mm.then_inc(s["rk_lora_p"], 1)
                wait("rk_kk2")
                for half in range(2):
                    mm = pe.matmul(sm[:, half, :], head_ones[:, :], rk_e[:, HALF * half:HALF * half + HALF],
                                   start=True, stop=True)
                mm.then_inc(s["rk_lora_p"], 1)
                wait("rk_bonus")
                for tt in range(NB):
                    mm = pe.matmul(sm[:, 2, 2 * tt:2 * tt + 2], rk_e[:, P * tt:P * tt + P],
                                   head_ones[:, 0:P:C], start=True, stop=True)
                mm.then_inc(s["rk_bonus_p"], 1)
                wait("rk_bonus_taken")
                wait("rk_prep")
                for b in range(8):
                    src = (rk_a, rk_e, rk_f, zr)[b // 2]
                    for n in range(4):
                        c = slice(P * (4 * (b % 2) + n), P * (4 * (b % 2) + n) + P)
                        mm = pe.transpose(bank(b)[:, P * n:P * n + P],
                                          zr[:, 4 + ft, c] if b >= 6 else src[:, c], ident[:, :])
                    mm.then_inc(s["rk_tok_t"], 1)
                for b in range(8):
                    wait(f"rk_tok{b % 2}")
                for g in range(2):
                    for hh in range(2):
                        rows = slice(C * hh, C * hh + C)
                        for dst, lhs, rhs in ((2 * hh, rk_b, rk_a), (2 * hh + 1, rk_a, rk_b),
                                              (4 + 2 * hh, "k", rk_a), (5 + 2 * hh, rk_b, "r")):
                            for n in range(4):
                                c = slice(P * (4 * g + n), P * (4 * g + n) + P)
                                l = zr[rows, 2 + ft, c] if lhs == "k" else lhs[rows, c]
                                r = zr[rows, ft, c] if rhs == "r" else rhs[rows, c]
                                mm = pe.matmul(bank(dst)[:, P * n:P * n + P], l, r, start=True, stop=True)
                            mm.then_inc(s["rk_mats"], 1)
                    for hh in range(2):
                        rows = slice(C * hh, C * hh + C)
                        wait("rk_m")
                        for n in range(4):
                            c = slice(P * (4 * g + n), P * (4 * g + n) + P)
                            mm = pe.matmul(bank(2 * hh)[:, P * n:P * n + P], zr[rows, 2 + ft, c],
                                           zr[rows, ft, c], start=True, stop=True)
                        mm.then_inc(s["rk_mats"], 1)
                    wait("rk_mats_done", 2)
                    for n in range(1, 6):
                        for hh in range(2):
                            wait("rk_lv")
                            for u in range(4):
                                mm = pe.matmul(bank(2 * hh)[:, P * u:P * u + P], m_lv[:, hh, u, :],
                                               inv[:, hh, u, :], start=True, stop=True)
                            mm.then_inc(s["rk_p"], 1)
                        for hh in range(2):
                            wait("rk_copied")
                            for u in range(4):
                                if n < 5:
                                    pe.matmul(bank(2 * hh + 1)[:, P * u:P * u + P], inv_t[:, hh, u, :],
                                              m_p[:, hh, u, :], start=True, stop=True)
                                mm = pe.matmul(bank(4 + 2 * hh)[:, P * u:P * u + P], m_p[:, hh, u, :],
                                               inv_t[:, hh, u, :], start=True, stop=True)
                            mm.then_inc(s["rk_x"], 1)
                        for hh in range(2):
                            wait("rk_x_added")
                    for hh in range(2):
                        cols = slice(C * hh, C * hh + C)
                        for u in range(4):
                            mm = pe.matmul(bank(2 * hh)[:, C * u:C * u + C], n_t[:, hh, u, :],
                                           v_tok[:, 4 * g + u, cols], start=True, stop=True)
                            mm = pe.matmul(bank(2 * hh)[:, BW + C * u:BW + C * u + C], rk_t[:, hh, u, :],
                                           v_tok[:, 4 * g + u, cols], start=True, stop=True)
                        mm.then_inc(s["rk_nv"], 1)
                        for u in range(4):
                            mm = pe.matmul(bank(5 + 2 * hh)[C * hh:C * hh + C, P * u:P * u + P],
                                           a_tok[:, 4 * g + u, cols], inv_t[:, hh, u, :], start=True, stop=True)
                        mm.then_inc(s["rk_nv"], 1)
                    for hh in range(2):
                        wait("rk_copied")
                        for u in range(4):
                            mm = pe.matmul(bank(2 * hh + 1)[:, C * u:C * u + C], inv_t[:, hh, u, :],
                                           nv[:, hh, u, :], start=True, stop=True)
                        mm.then_inc(s["rk_xnv"], 1)
                    wait("rk_round", 2)
                    wait("rk_round_act", 2)
                for ch in range(NCH):
                    tt, pb = ch // 2, C * (ch % 2)
                    toks = slice(pb, pb + C)
                    wait("rk_state")
                    for hh in range(2):
                        rows = slice(C * hh, C * hh + C)
                        mm = pe.matmul(bank(4 + hh)[toks, 0:C], xa_t[rows, P * tt + pb:P * tt + pb + C],
                                       s_all[rows, ch, :], start=True, stop=True)
                    mm.then_inc(s["rk_chain"], 1)
                    for hh in range(2):
                        cols = slice(C * hh, C * hh + C)
                        pe.matmul(bank(6)[C * hh:C * hh + C, 0:C], k_tok[toks, tt, cols], v_tok[toks, tt, cols],
                                  start=True, stop=False, skip_group_check=True)
                    wait("rk_u_added")
                    for hh in range(2):
                        cols = slice(C * hh, C * hh + C)
                        mm = pe.matmul(bank(6)[C * hh:C * hh + C, 0:C], b_tok[toks, tt, cols], u_tok[toks, tt, cols],
                                       start=False, stop=True, skip_group_check=True)
                    mm.then_inc(s["rk_chain"], 1)
                wait("rk_state")
                for g in range(2):
                    for hh in range(2):
                        cols, rows = slice(C * hh, C * hh + C), slice(C * hh, C * hh + C)
                        for u in range(4):
                            tt = 4 * g + u
                            pe.matmul(bank(2 * g + hh)[:, C * u:C * u + C], rb_t[:, hh, tt, :],
                                      u_tok[:, tt, cols], start=True, stop=False, skip_group_check=True)
                            for q in range(2):
                                mm = pe.matmul(bank(2 * g + hh)[C * q:C * q + C, C * u:C * u + C],
                                               zr[rows, ft, P * tt + C * q:P * tt + C * q + C],
                                               s_all[rows, 2 * tt + q, :], start=False, stop=True,
                                               skip_group_check=True)
                    mm.then_inc(s["rk_y"], 1)
                for b in range(2):
                    for u in range(4):
                        c = slice(P * (4 * b + u), P * (4 * b + u) + P)
                        mm = pe.matmul(bank(4 + b)[:, P * u:P * u + P], rk_sg[:, c],
                                       lora[:, 1, P * ft:P * ft + P], start=True, stop=True)
                    mm.then_inc(s["rk_y"], 1)
                wait("rk_y_ready")
                for b in range(2):
                    for u in range(4):
                        mm = pe.transpose(bank(6 + b)[:, P * u:P * u + P], y_tok[:, 4 * b + u, :], ident[:, :])
                    mm.then_inc(s["rk_y_t"], 1)

            wait("y_split", 8)
            for d in range(KT):
                t = T_BR + d
                pe.wait_ge(s["w_split"], t + 1)
                for n in range(4):
                    p = P_BR + 4 * d + n
                    pe.wait_ge(s[f"p_free{p % 2}"], frees_before(p))
                    product(p, [ring(t, 256 * n + P * k, 256 * n + P * k + P) for k in range(2)], P,
                            y_hi, y_lo, 2 * n).then_inc(s["p_ready"], 1)
            for d in range(KT):
                if d == 0:
                    wait("m_split", KT)
                whole(T_WO + d, P_WO + d, m_hi, m_lo)
            norm(1)
            wait("h_split", KT)
            for n in range(4):
                whole(T_FFN + n, P_FFN + n, h_hi, h_lo)

            def up(i, u, q):
                pe.wait_ge(s["w_split"], 6 * i + (T_FFN + 5 + u))
                pe.wait_ge(s[f"p_free{q % 2}"], 6 * i + frees_before(P_FFN + 4 + q))
                product(q, [ring(u, P * k, P * k + P) for k in range(8)], P, h_hi, h_lo) \
                    .then_inc(s["p_ready"], 1)

            def down(i, u, q):
                pe.wait_ge(s["w_split"], 6 * i + (T_FFN + 5 + u))
                for j in range(4):
                    pe.wait_ge(s[f"p_free{(q + j) % 2}"], 6 * i + frees_before(P_FFN + 4 + q + j))
                    product(q + j, [ring(u, HALF * k + P * j, HALF * k + P * j + P) for k in range(2)], P,
                            g_hi, g_lo).then_inc(s["p_ready"], 1)

            with pe.Fori(0, FT // 2 - 1) as i:
                up(i, 0, 0)
                pe.wait_ge(s["g_split"], 2 * i + 2)
                down(i, 1, 1)
                down(i, 2, 5)
                for u in range(3, 6):
                    up(i, u, 6 + u)
            pe.wait_ge(s["g_split"], FT)
            for u in range(2):
                down(FT // 2 - 1, u, 4 * u)
            norm(2)
            norm(3)
            wait("h_split", KT)
            for t in range(T_IN2, T_UQ):
                whole(t, P_IN2 + t - T_IN2, h_hi, h_lo)
                if t - T_IN2 == 13:
                    for b in range(8):
                        ft, half = divmod(b, 2)
                        if b >= 4:
                            wait("v_taken")
                        for n in range(4):
                            c = P * (4 * half + n)
                            mm = pe.transpose(sm[:, b % 4, P * n:P * n + P], vt_2[:, ft, c:c + P], ident[:, :])
                        mm.then_inc(s["v_turned"], 1)
            wait("v_taken", 4)
            for z in range(2):
                pe.wait_ge(s[f"p_free{z}"], frees_before(P_UQ))
            pe.wait_ge(s["rel_in"], 32)
            for n in range(3):
                mm = pe.matmul(sm[0:HEADS_A, n, 0:384], rel_rows[0:33, :], buckets[0:33, 384 * n:384 * n + 384],
                               start=True, stop=True)
            mm.then_inc(s["bias_p"], 1)
            wait("bias_rows")
            for j in range(8):
                wait("n2_sq")
                for half in range(2):
                    mm = pe.matmul(sm[:, 2 * (j % 2) + half, :], head_ones[:, :],
                                   nsq[:, j % 2, HALF * half:HALF * half + HALF], start=True, stop=True)
                mm.then_inc(s["n2_ss"], 1)
            wait("n2_q", 8)

            def attention(total, block, scores, v, column, turn):
                def z(n):
                    if n >= 2:
                        wait("at_s")
                    w = P * (block(n) + 1)
                    for a in range(0, w, HALF):
                        m = min(HALF, w - a)
                        mm = scores(n, sm[:, 2 * (n % 2) + a // HALF, 0:m], a, m)
                    mm.then_inc(s["at_z"], 1)

                z(0)
                for n in range(total):
                    if n + 1 < total:
                        z(n + 1)
                    qb = block(n)
                    if n >= 1:
                        wait("at_pt_copied")
                    wait("at_p")
                    for k in range(qb + 1):
                        mm = pe.transpose(gp[:, 0, P * k:P * k + P], att_s[:, n % 2, P * k:P * k + P], ident[:, :])
                    mm.then_inc(s["at_pt"], 1)
                    pe.wait_ge(s["at_pt_copied"], wait.seen.get("at_pt_copied", 0) + 1)
                    if n >= 2:
                        wait("at_o_taken")
                    for k in range(qb + 1):
                        mm = pe.matmul(o_place(n), att_pt[:, n % 2, P * k:P * k + P],
                                       v[:, k, column(n):column(n) + C], start=(k == 0), stop=(k == qb),
                                       skip_group_check=True)
                    mm.then_inc(s["at_o"], 1)
                    turn(n)
                wait("at_s", 2)
                wait("at_pt_copied")
                wait("at_o_taken", 2)

            def scores_a(n, o, a, m):
                h, qb = divmod(n, NB)
                rows = slice(C * (h % 2), C * (h % 2) + C)
                return pe.matmul(o, q_2[rows, h // 2, P * qb:P * qb + P], k_2[rows, h // 2, a:a + m],
                                 start=True, stop=True)

            attention(UNITS, lambda n: n % NB, scores_a, v_2, lambda n: C * (n // NB), lambda n: None)
            for qb in range(NB):
                if qb >= 4:
                    wait("z_done")
                for ft in range(4):
                    mm = pe.transpose(sm[:, qb % 4, P * ft:P * ft + P], o_all[:, qb, P * ft:P * ft + P], ident[:, :])
                mm.then_inc(s["z_turned"], 1)
            wait("z_done", 4)

            for j in range(3):
                wait("c_sq")
                for half in range(2):
                    c = slice(HALF * half, HALF * half + HALF)
                    mm = pe.matmul(sm[:, (0, 0, 2)[j] + half, :], ones[:, :], nsq[:, j % 2, c],
                                   start=(j != 1), stop=(j != 0), skip_group_check=True)
                mm.then_inc(s["c_ss"], 1)
            wait("c_sq")
            wait("c_root", 2)
            for half in range(2):
                c = slice(HALF * half, HALF * half + HALF)
                mm = pe.matmul(sm[C:C + 32, half, :], ones[C:C + 32, 0:32], nsq[C:C + 32, 1, c], start=True, stop=True)
            mm.then_inc(s["c_ss"], 1)

            def turn_rope(view, z):
                for half in range(2):
                    c = slice(HALF * half, HALF * half + HALF)
                    mm = pe.matmul(sm[C:C + 32, 2 * z + half, :], rope_turn[C:C + 32, :], view[:, c],
                                   start=True, stop=True)
                mm.then_inc(s["rot"], 1)

            wait("krope_normed")
            turn_rope(k_rope[C:C + 32, :], 1)
            wait("rot_used")
            wait("q_split", 2)
            for h in range(HEADS_B):
                t, p = T_UQ + h // 4, P_UQ + h
                pe.wait_ge(s["w_split"], t + 1)
                pe.wait_ge(s[f"p_free{p % 2}"], frees_before(p))
                product(p, [ring(t, 384 * k + DQK * (h % 4), 384 * k + DQK * (h % 4) + DQK) for k in range(2)],
                        DQK, cq_hi, cq_lo).then_inc(s["p_ready"], 1)
            wait("mla_ones")

            def head_norm(rows, squares_waited=False):
                if not squares_waited:
                    wait("hn_sq")
                for half in range(2):
                    c = slice(HALF * half, HALF * half + HALF)
                    mm = pe.matmul(sm[0:rows, half, :], mla_ones[0:rows, 0:rows], nsq_b[0:rows, c],
                                   start=True, stop=True)
                mm.then_inc(s["hn_ss"], 1)

            for h in range(HEADS_B):
                head_norm(DQK)
                wait("hn_done")
                turn_rope(qh[C:DQK, h, :], 1)
                wait("rot_used")
            wait("kv_split")
            pe.wait_ge(s["w_split"], T_UKV + 1)
            for h in range(HEADS_B):
                p = P_UKV + h
                pe.wait_ge(s[f"p_free{p % 2}"], frees_before(p))
                product(p, [ring(T_UKV, P * h, P * h + P)], P, ckv_hi, ckv_lo).then_inc(s["p_ready"], 1)
                wait("hn_sq")
                for n in range(NB):
                    mm = pe.transpose(sm[:, 2 + n // 4, C * (n % 4):C * (n % 4) + C], vb_t[C:P, P * n:P * n + P],
                                      ident[C:P, C:P])
                mm.then_inc(s["vb_turned"], 1)
                head_norm(C, True)
                wait("hn_done")
                wait("vb_taken")
            for z in range(2):
                pe.wait_ge(s[f"p_free{z}"], frees_before(P_OUT))
            wait("k_rope_spread")

            def scores_b(n, o, a, m):
                qb, h = divmod(n, HEADS_B)
                return pe.matmul(o, qh[:, h, P * qb:P * qb + P], kh[:, h, a:a + m], start=True, stop=True)

            def turn_b(n):
                if n % 8 != 7:
                    return
                qb = n // 8
                pe.wait_ge(s["at_o_taken"], UNITS + n + 1)
                for ft in range(4):
                    mm = pe.transpose(gp[:, 0, P * ft:P * ft + P], o_b[:, qb % 2, P * ft:P * ft + P],
                                      ident[:, :])
                mm.then_inc(s["z_turned"], 1)
                wait("z_done")

            attention(UNITS, lambda n: n // 8, scores_b, v_b, lambda n: C * (n % 8), turn_b)
            wait("mix_split", 8)

            def turn_out(d):
                p = P_OUT + d
                pe.wait_ge(s[f"p_free{p % 2}"], frees_before(p) + 1)
                if d >= 2:
                    wait("out_taken")
                for n in range(NB):
                    mm = pe.transpose(sm[:, 2 * (d % 2) + n // 4, P * (n % 4):P * (n % 4) + P],
                                      x_out[:, d % 2, P * n:P * n + P], ident[:, :])
                mm.then_inc(s["out_t"], 1)

            for d in range(KT):
                whole(T_OUT + d, P_OUT + d, mix_hi, mix_lo)
                if d:
                    turn_out(d - 1)
            turn_out(KT - 1)

        @block.scalar
        def _(act):
            wait = Waits(act, "act_own")

            def split_weights(t):
                act.wait_ge(s[f"w_loaded{t % 2}"], loaded_value(t))
                if t >= 2:
                    act.wait_ge(s["p_ready"], outs_through(t - 2))
                n = block_columns(t)
                act.copy(w_hi[:, t % 2, 0:n], w_raw[:, t % 2, 0:n]).then_inc(s["w_high"], 1)

            def norm(n, src, ready=None):
                for k in range(KT):
                    if ready:
                        wait(ready)
                    if n * KT + k >= 2:
                        act.wait_ge(s["square_used"], n * KT + k - 1)
                    act.activation(squares[:, k % 2, :], src[:, k, :], ACT.Square).then_inc(s["square"], 1)
                act.wait_ge(s["square_used"], KT * (n + 1))
                act.activation(root[:, :], sm[:, 0:2, :].rearrange("p a b -> p (a b)"), ACT.Sqrt,
                               bias=RMS_EPS, scale=1.0 / D).then_inc(s["root"], 1)

            def split_h():
                for k in range(KT):
                    wait("h_ready")
                    act.copy(h_hi[:, k, :], h_tmp[:, k % 2, :]).then_inc(s["high"], 1)

            for b in range(0, 16, 2):
                act.wait_ge(s["x_t"], b + 1)
                half, k = divmod(b, 8)
                act.copy(x_t[:, k, HALF * half:HALF * half + HALF], sm[:, b % 4, :]).then_inc(s["x_turned0"], 1)
            act.wait_ge(s["x_turned1"], 8)
            act.wait_ge(s["x_turned0"], 8)
            norm(0, x_t)
            split_weights(0)
            split_h()
            for t in range(T_GATE):
                split_weights(t + 1)
                if t in (4, 5):
                    continue
                act.wait_ge(s["p_ready"], t + 1)
                ps = gp[:, t % 2, :]
                done = s[f"p_free{t % 2}"]
                if t < 2:
                    act.copy(y_a[:, t, :], ps).then_inc(done, 1)
                elif t < 4:
                    act.copy(sc_c[:, t - 2, :], ps).then_inc(done, 1)
                elif t < 8:
                    act.mul(q_sb[:, t - 6, :], ps, 0.125).then_inc(done, 1)
                elif t < 10:
                    act.copy(k_sb[:, t - 8, :], ps).then_inc(done, 1)
                elif t < 12:
                    if t == 10:
                        wait("sc_done")
                    act.copy(vt_sb[:, t - 10, :], ps).then_inc(done, 1)
                elif t < 20:
                    if t == 12:
                        act.wait_ge(s["x_out"], 16)
                    act.copy(zr[:, t - 12, :], ps).then_inc(done, 1)
                else:
                    dst = y_d[:, t - 20, :] if t < 22 else vt_sg[:, t - 22, :]
                    act.activation(dst, ps, ACT.Gelu_apprx_tanh).then_inc(done, 1)
            wait("sg_var")
            act.activation(small[:, 16:24], small[:, 8:16], ACT.Sqrt, bias=LN_EPS).then_inc(s["sg_root"], 1)
            def gate(i, z, stored=True):
                act.wait_ge(s["p_ready"], 2 * i + (T_GATE + z + 1))
                if stored:
                    act.wait_ge(s[f"gate_stored{z}"], 16 * i)
                act.activation(gate_out[:, z, :], gp[:, z, :], ACT.Sigmoid,
                               bias=col[:, bass.ds(2 * i + (ROWS["gate_b"] + z), 1)]) \
                    .then_inc(s["gate_ready"], 1)

            for z in range(2):
                split_weights(T_GATE + z + 1)
                gate(0, z, stored=False)
            with act.Fori(1, 15) as i:
                for z in range(2):
                    act.wait_ge(s[f"w_loaded{1 - z}"], 16 * i + loaded_value(T_GATE + z + 1))
                    act.wait_ge(s["p_ready"], 2 * i + (T_GATE + z))
                    act.copy(w_hi[:, 1 - z, :], w_raw[:, 1 - z, :]).then_inc(s["w_high"], 1)
                    gate(i, z)
            for z in range(2):
                split_weights(T_BR - 1 + z)
                gate(15, z)

            def sb_log(n):
                z, w = n % 2, P * (n // 4 + 1)
                wait("sb_z")
                l = sb_l[:, z, 0:w]
                sc = sm[:, 2 * z:2 * z + 2, :].rearrange("p a b -> p (a b)")[:, 0:w]
                wait.after(act.activation(l, sc, ACT.Abs))
                wait.after(act.activation(l, l, ACT.Exp, scale=-1.0))
                act.activation(l, l, ACT.Ln, bias=1.0).then_inc(s["sb_l"], 1)

            units = 4 * NB
            sb_log(0)
            for n in range(units):
                if n + 1 < units:
                    sb_log(n + 1)
                z, w = n % 2, P * (n // 4 + 1)
                wait("sb_z_free")
                act.activation(sb_p[:, z, 0:w], sb_p[:, z, 0:w], ACT.Exp).then_inc(s["sb_p"], 1)
                wait("sb_pt")
                act.copy(sb_pt[:, z, 0:w], gp[:, 0, 0:w]).then_inc(s["sb_pt_copied"], 1)
                if n % 4 == 3:
                    qb = n // 4
                    wait("sb_o")
                    act.copy(sb_o[:, qb % 2, :], gp[:, 1, 0:BW]).then_inc(s["sb_o_copied"], 1)
                    wait("sb_y")
                    act.copy(y_b[:, :, P * qb:P * qb + P],
                             gp[:, 1, HALF:HALF + BW].rearrange("p (f t) -> p f t", f=2)) \
                        .then_inc(s["sb_y_free"], 1)

            wait("rk_shift", 8)
            for ft in range(2):
                act.activation(rk_th[0:C, :], zr[0:C, 6, :], ACT.Tanh).then_inc(s["rk_lora"], 1)
                wait.after(act.activation(rk_sg[:, :], zr[:, 7, :], ACT.Sigmoid))
                wait("rk_kk1")
                act.activation(rk_e[:, :], rk_kk[:, :], ACT.Square).then_inc(s["rk_kk2"], 1)
                wait("rk_lora_p")
                act.activation(rk_f[:, :], gp[:, 0, :], ACT.Sigmoid, bias=pcol("w0", ft)).then_inc(s["rk_w"], 1)
                act.activation(rk_a[:, :], gp[:, 1, :], ACT.Sigmoid, bias=pcol("a0", ft)).then_inc(s["rk_w"], 1)
                wait("rk_lora_p")
                act.activation(rk_e[:, :], sm[:, 0:2, :].rearrange("p a b -> p (a b)"), ACT.Sqrt) \
                    .then_inc(s["rk_pow"], 1)
                wait("rk_cum")
                act.activation(rk_f[:, :], rk_l[:, :], ACT.Exp, scale=DECAY).then_inc(s["rk_pow"], 1)
                act.activation(rk_lx[:, :], rk_lx[:, :], ACT.Exp, scale=-DECAY).then_inc(s["rk_pow"], 1)
                act.activation(rk_l[:, :], rk_l[:, :], ACT.Exp, scale=-DECAY).then_inc(s["rk_pow"], 1)
                for b in range(0, 8, 2):
                    wait("rk_tok_t", 1 if b == 0 else 2)
                    act.copy((a_tok, b_tok, k_tok, v_tok)[b // 2][:, 0:4, :],
                             bank(b).rearrange("p (u c) -> p u c", u=4)).then_inc(s["rk_tok0"], 1)
                wait("rk_tok_t")
                for g in range(2):
                    for n in range(1, 6):
                        for hh in range(2):
                            wait("rk_p")
                            act.copy(m_p[:, hh], bank(2 * hh).rearrange("p (u c) -> p u c", u=4)) \
                                .then_inc(s["rk_copied"], 1)
                    for hh in range(2):
                        cols = slice(C * hh, C * hh + C)
                        wait("rk_nv")
                        act.copy(nv[:, hh], bank(2 * hh)[:, 0:BW].rearrange("p (u c) -> p u c", u=4)) \
                            .then_inc(s["rk_copied"], 1)
                        act.copy(y_loc[:, 4 * g:4 * g + 4, cols],
                                 bank(2 * hh)[:, BW:2 * BW].rearrange("p (u c) -> p u c", u=4))
                        wait("rk_nv")
                        act.copy(xa_t[cols, HALF * g:HALF * g + HALF], bank(5 + 2 * hh)[cols, :]) \
                            .then_inc(s["rk_round_act"], 1)
                wait("rk_gvar")
                act.activation(small[:, 80:96], small[:, 64:80], ACT.Sqrt, bias=GN_EPS, scale=1.0 / C) \
                    .then_inc(s["rk_groot"], 1)
                for b in range(2):
                    wait("rk_y_t")
                    ins = act.copy(y_c[:, ft, HALF * b:HALF * b + HALF], bank(6 + b))
                ins.then_inc(s["rk_g_free"], 1)

            for n, y in enumerate((y_a, y_b, y_c, y_d)):
                if n == 0:
                    act.wait_ge(s["rk_g_free"], 2)
                for ft in range(2):
                    act.copy(y_hi[:, 2 * n + ft, :], y[:, ft, :]).then_inc(s["high"], 1)
            for d in range(KT):
                split_weights(T_BR + d + 1)
                act.wait_ge(s["merge_add"], 3 * (d + 1))
                act.copy(m_hi[:, d, :], merged[:, d % 2, :]).then_inc(s["high"], 1)
            for d in range(KT):
                split_weights(T_WO + d + 1)
            for z in range(2):
                act.wait_ge(s[f"p_free{z}"], frees_before(P_FFN))
            norm(1, x_mid)
            split_h()

            def taps(tap, j, i):
                return col[:, bass.ds(2 * i + (ROWS["conv"] + 2 * FT * tap + 2 + j), 1)]

            def first_tap(i, buf, j, p):
                act.wait_ge(s["p_ready"], 12 * i + (p + 1))
                act.activation(hid[:, buf, :], gp[:, p % 2, :], ACT.Copy, scale=taps(2, j, i)) \
                    .then_inc(s["c_first"], 1)

            def gate_silu(i, buf, p):
                act.wait_ge(s[f"p_free{p % 2}"], 6 * i + (frees_before(p) + 1))
                act.activation(hid[:, buf, :], hid[:, buf, :], ACT.Silu).then_inc(s["silu"], 1)

            def g_high(i, k):
                act.wait_ge(s["g_raw"], 2 * i + (3 + k))
                act.copy(g_hi[:, k, :], hid[:, 2 * k + 1, :]).then_inc(s["g_high"], 1)

            for n in range(4):
                split_weights(T_FFN + n + 1)
                if n in (1, 3):
                    gate_silu(-1, n - 1, P_FFN + 12 + n - 1)
                first_tap(-1, n, (0, FT, 1, FT + 1)[n], P_FFN + 12 + n)
                if n in (1, 3):
                    g_high(-1, n // 2)
            p0 = P_FFN + 4
            with act.Fori(0, FT // 2 - 1) as i:
                for u in range(6):
                    t = T_FFN + 4 + u
                    act.wait_ge(s[f"w_loaded{(u + 1) % 2}"], 48 * i + loaded_value(t + 1))
                    act.wait_ge(s["p_ready"], 12 * i + outs_through(t - 1))
                    act.copy(w_hi[:, (u + 1) % 2, :], w_raw[:, (u + 1) % 2, :]).then_inc(s["w_high"], 1)
                    if u == 0:
                        first_tap(i, 0, 0, p0)
                    elif u == 1:
                        gate_silu(i, 0, p0)
                    elif u == 3:
                        act.wait_ge(s["g_split"], 2 * i + 2)
                        first_tap(i, 1, FT, p0 + 9)
                        g_high(i, 0)
                    elif u == 4:
                        first_tap(i, 2, 1, p0 + 10)
                    elif u == 5:
                        gate_silu(i, 2, p0 + 10)
                        first_tap(i, 3, FT + 1, p0 + 11)
                        g_high(i, 1)
            split_weights(T_IN2 - 1)
            split_weights(T_IN2)
            for z in range(2):
                act.wait_ge(s[f"p_free{z}"], frees_before(P_IN2))
            norm(2, x_mid)
            norm(3, x_mid, "x_normed")
            split_h()
            for t in range(T_IN2, T_UQ):
                split_weights(t + 1)
                n = t - T_IN2
                act.wait_ge(s["p_ready"], P_IN2 + n + 1)
                if n == 0:
                    act.wait_ge(s["x_out"], 32)
                ps = gp[:, n % 2, :]
                dst, func = ((q_2[:, n, :], ACT.Copy) if n < 4 else (k_2[:, n - 4, :], ACT.Copy) if n < 8
                             else (vt_2[:, n - 8, :], ACT.Copy) if n < 12
                             else (z_a[:, n - 12, :], ACT.Silu) if n < 16
                             else (c_q[:, n - 16, :], ACT.Copy) if n < 18
                             else (c_kv[:, :], ACT.Copy) if n == 18
                             else (k_rope[:, :], ACT.Copy) if n == 19
                             else (z_b[:, n - 20, :], ACT.Silu))
                act.activation(dst, ps, func).then_inc(s[f"p_free{n % 2}"], 1)

            for z in range(2):
                act.wait_ge(s[f"p_free{z}"], frees_before(P_UQ))

            def root_of(dst, src, n, sem):
                act.activation(dst, src, ACT.Sqrt, bias=RMS_EPS, scale=1.0 / n).then_inc(s[sem], 1)

            def pair(z):
                return sm[:, 2 * z:2 * z + 2, :].rearrange("p a b -> p (a b)")

            def n2_square(j):
                if j >= 2:
                    act.wait_ge(s["n2_ss"], j - 1)
                act.activation(nsq[:, j % 2, :], (q_2, k_2)[j // 4][:, j % 4, :], ACT.Square) \
                    .then_inc(s["n2_sq"], 1)

            wait("bias_rows")
            n2_square(0)
            for j in range(8):
                if j < 7:
                    n2_square(j + 1)
                act.wait_ge(s["n2_ss"], j + 1)
                if j >= 2:
                    wait("n2_q")
                root_of(nrt[:, j % 2, :], pair(j % 2), C, "n2_rt")

            def attention(block, scale):
                def exps(n):
                    w = P * (block(n) + 1)
                    wait("at_m")
                    act.activation(att_s[:, n % 2, 0:w], att_s[:, n % 2, 0:w], ACT.Exp, scale=scale,
                                   bias=small[:, 102 + n % 2:103 + n % 2],
                                   accum_out=small[:, 104 + n % 2:105 + n % 2]).then_inc(s["at_p"], 1)

                exps(0)
                for n in range(UNITS):
                    if n < UNITS - 1:
                        exps(n + 1)
                    w = P * (block(n) + 1)
                    wait("at_pt")
                    act.copy(att_pt[:, n % 2, 0:w], gp[:, 0, 0:w]).then_inc(s["at_pt_copied"], 1)

            attention(lambda n: n % NB, 1.0)
            act.wait_ge(s["n2_q"], 8)
            for j, src in enumerate((c_q[:, 0, :], c_q[:, 1, :], c_kv[:, :])):
                if j == 2:
                    act.wait_ge(s["c_ss"], 1)
                act.activation(nsq[:, j % 2, :], src, ACT.Square).then_inc(s["c_sq"], 1)
            act.wait_ge(s["c_ss"], 2)
            act.activation(nsq[C:C + 32, 1, :], k_rope[C:C + 32, :], ACT.Square).then_inc(s["c_sq"], 1)
            root_of(nrt[:, 0, :], pair(0), BW, "c_root")
            act.wait_ge(s["c_ss"], 3)
            root_of(nrt[:, 1, :], pair(1), P, "c_root")
            act.wait_ge(s["c_ss"], 4)
            act.wait_ge(s["kv_normed"], 1)
            root_of(nrt[C:C + 32, 0, :], pair(0)[C:C + 32, :], 32, "c_root")
            for k in range(2):
                act.wait_ge(s["q_normed"], k + 1)
                act.copy(cq_hi[:, k, :], c_q[:, k, :]).then_inc(s["high"], 1)
            act.copy(ckv_hi[:, 0, :], c_kv[:, :]).then_inc(s["high"], 1)
            wait("angles")
            act.activation(sin_t[C:C + 32, :], sin_t[C:C + 32, :], ACT.Sin).then_inc(s["hn_rt"], 1)
            act.activation(cos_t[C:C + 32, :], cos_t[C:C + 32, :], ACT.Sin).then_inc(s["hn_rt"], 1)
            split_weights(T_UQ + 1)

            for h in range(HEADS_B):
                p = P_UQ + h
                act.wait_ge(s["p_ready"], p + 1)
                act.copy(qh[:, h, :], gp[0:DQK, p % 2, :]).then_inc(s[f"p_free{p % 2}"], 1)
            split_weights(T_UKV)
            for z in range(2):
                act.wait_ge(s[f"p_free{z}"], frees_before(P_UKV))

            def head_norm(view, rows):
                act.activation(nsq_b[0:rows, :], view, ACT.Square).then_inc(s["hn_sq"], 1)
                wait("hn_ss")
                act.activation(hn_root[0:rows, :], pair(0)[0:rows, :], ACT.Sqrt, bias=RMS_EPS) \
                    .then_inc(s["hn_rt"], 1)

            for h in range(HEADS_B):
                if h:
                    act.wait_ge(s["rot_used"], h + 1)
                head_norm(qh[:, h, :], DQK)
            for h in range(HEADS_B):
                p = P_UKV + h
                act.wait_ge(s["p_ready"], p + 1)
                if h == 0:
                    act.wait_ge(s["rot_used"], HEADS_B + 1)
                else:
                    act.wait_ge(s["hn_done"], HEADS_B + h)
                wait.after(act.copy(kh[0:C, h, :], gp[0:C, p % 2, :]))
                if h:
                    wait("vb_turned")
                act.copy(vb_t[C:P, :], gp[C:P, p % 2, :]).then_inc(s[f"p_free{p % 2}"], 1)
                head_norm(kh[0:C, h, :], C)
            split_weights(T_OUT)
            split_weights(T_OUT + 1)
            attention(lambda n: n // 8, DQK ** -0.5)
            act.wait_ge(s["z_done"], 2 * NB)
            for k in range(8):
                act.copy(mix_hi[:, k, :], (z_a, z_b)[k // 4][:, k % 4, :]).then_inc(s["high"], 1)
            for d in range(KT):
                if 1 <= d < KT - 1:
                    split_weights(T_OUT + d + 1)
                wait("out_t")
                if d >= 2:
                    act.wait_ge(s[f"stored{d % 2}"], 16 * (d // 2))
                act.copy(out_tok[:, d % 2], pair(d % 2).rearrange("p (n c) -> p n c", c=P)) \
                    .then_inc(s["out_taken"], 1)

        @block.vector
        def _(dve):
            wait = Waits(dve, "dve_own")

            def split_weights(t):
                n = block_columns(t)
                dve.wait_ge(s["w_high"], t + 1)
                dve.tensor_tensor(w_lo[:, t % 2, 0:n], w_raw[:, t % 2, 0:n], w_hi[:, t % 2, 0:n].bitcast(F32),
                                  ALU.subtract).then_inc(s["w_split"], 1)

            def norm(src, gain, dst=None):
                wait("root")

                wait.after(dve.reciprocal(rstd[:, :], root[:, :]))
                for k in range(KT):
                    o = dst[:, k, :] if dst is not None else h_tmp[:, k % 2, :]
                    if dst is None and k >= 2:
                        wait("h_split")
                    ins = dve.scalar_tensor_tensor(o, src[:, k, :], pcol(gain, k), rstd[:, :], ALU.mult, ALU.mult)
                    ins.then_inc(s["h_ready"] if dst is None else s["x_normed"], 1)
                    if dst is None and k >= 1:
                        h_low(k - 1)
                if dst is None:
                    h_low(KT - 1)
                    wait("h_split", 2)

            def h_low(k):
                wait("high")
                dve.tensor_tensor(h_lo[:, k, :], h_tmp[:, k % 2, :], h_hi[:, k, :].bitcast(F32),
                                  ALU.subtract).then_inc(s["h_split"], 1)

            wait("col_t")
            dve.tensor_copy(col[:, 0:NCOL], sm[:, 0, 0:NCOL]).then_inc(s["cols"], 1)
            wait("wsg_t")
            dve.tensor_copy(w_sg[:, :, :], sm[:, 1, :].rearrange("p (g t) -> p g t", g=4)).then_inc(s["wsg_copied"], 1)
            dve.wait_ge(s["cols"], 1)
            wait.after(dve.tensor_scalar(k_a_rest[:, :], col[:, ROWS["k_a"]:ROWS["k_a"] + 2], -1.0, 1.0,
                                         ALU.mult, ALU.add))
            wait.after(dve.tensor_scalar(a_q_scaled[:, :], pcol("a_q"), 0.125, None, ALU.mult))
            for b in range(1, 16, 2):
                dve.wait_ge(s["x_t"], b + 1)
                half, k = divmod(b, 8)
                dve.tensor_copy(x_t[:, k, HALF * half:HALF * half + HALF], sm[:, b % 4, :]) \
                    .then_inc(s["x_turned1"], 1)
            norm(x_t, "mix_g")
            split_weights(0)
            for t in range(T_GATE):
                split_weights(t + 1)
                if t in (4, 5):
                    n = t - 4
                    dve.wait_ge(s["p_ready"], t + 1)
                    dve.wait_ge(s["p_free0"], 2)
                    dve.wait_ge(s["p_free1"], 2)
                    cx, acc = sc_cx[:, 0, :], sc_c[:, n, :]
                    dve.tensor_tensor(cx, gp[:, t % 2, :], sc_c[:, n, :], ALU.mult).then_inc(s[f"p_free{t % 2}"], 1)
                    dve.wait_ge(s[f"p_free{t % 2}"], 3)
                    wait.after(dve.tensor_scalar(acc, cx, pcol("sc_w", 4 + n), None, ALU.mult))
                    for shift in (1, 2):
                        wait.after(dve.scalar_tensor_tensor(
                            acc[:, shift:T], cx[:, 0:T - shift], pcol("sc_w", 4 - 2 * shift + n),
                            acc[:, shift:T], ALU.mult, ALU.add))
                    ins = dve.tensor_tensor(y_a[:, n, :], y_a[:, n, :], acc, ALU.mult)
                    if n == 1:
                        ins.then_inc(s["sc_done"], 1)
                if t == 13:
                    for b in range(4):
                        ft, half = divmod(b, 2)
                        wait("v_turned")
                        dve.tensor_copy(v_sb[:, 4 * half:4 * half + 4, P * ft:P * ft + P],
                                        sm[:, b, :].rearrange("p (n c) -> p n c", n=4)).then_inc(s["v_taken"], 1)
            for b in range(4):
                ft, half = divmod(b, 2)
                wait("v_turned")
                wait.after(dve.tensor_copy(v_sg[:, 4 * half:4 * half + 4, P * ft:P * ft + P],
                                           sm[:, b, :].rearrange("p (n c) -> p n c", n=4)))
            stats = rstd[:, 0:6 * NB].rearrange("p (n k) -> p n k", n=NB)
            mean_var = rstd[:, 64:64 + 2 * NB].rearrange("p (n k) -> p n k", n=NB)
            for tt in range(NB):
                ins = dve.bn_stats(stats[:, tt, :], v_sg[:, tt, :])
            wait.after(ins)
            for tt in range(NB):
                ins = dve.bn_aggr(mean_var[:, tt, :], stats[:, tt, :])
            wait.after(ins)
            dve.tensor_copy(small[:, 8:16], mean_var[:, :, 1]).then_inc(s["sg_var"], 1)
            wait("sg_root")
            wait.after(dve.reciprocal(small[:, 24:32], small[:, 16:24]))
            for tt in range(NB):
                ins = dve.tensor_scalar(v_sg[:, tt, :], v_sg[:, tt, :], mean_var[:, tt, 0:1],
                                        small[:, 24 + tt:25 + tt], ALU.subtract, ALU.mult)
            wait.after(ins)
            wait.after(dve.tensor_tensor(v_sg[:, :, :], v_sg[:, :, :],
                                         row_g[:, 0, :].unsqueeze(1).to_broadcast([P, NB, BW]), ALU.mult))
            dve.tensor_tensor(v_sg[:, :, :], v_sg[:, :, :],
                              row_g[:, 1, :].unsqueeze(1).to_broadcast([P, NB, BW]), ALU.add) \
                .then_inc(s["sg_normed"], 1)
            dve.wait_ge(s["p_free0"], 11)
            dve.wait_ge(s["p_free1"], 11)
            for b in range(4):
                ft, half = divmod(b, 2)
                c = slice(HALF * half, HALF * half + HALF)
                wait("sg_mixed")
                dve.tensor_tensor(y_d[:, ft, c], sm[:, b, :], y_d[:, ft, c], ALU.mult).then_inc(s["sg_done"], 1)
            with dve.Fori(0, 16) as i:
                for z in range(2):
                    dve.wait_ge(s["w_high"], 2 * i + (T_GATE + z + 2))
                    dve.tensor_tensor(w_lo[:, 1 - z, :], w_raw[:, 1 - z, :], w_hi[:, 1 - z, :].bitcast(F32),
                                      ALU.subtract).then_inc(s["w_split"], 1)

            def sb_soft(n):
                z, w = n % 2, P * (n // 4 + 1)
                sc = sm[:, 2 * z:2 * z + 2, :].rearrange("p a b -> p (a b)")[:, 0:w]
                wait("sb_l")
                dve.scalar_tensor_tensor(sb_sp[:, z, 0:w], sc, 0.0, sb_l[:, z, 0:w], ALU.max, ALU.add) \
                    .then_inc(s["sb_sp"], 1)

            sb_soft(0)
            for n in range(4 * NB):
                z, w = n % 2, P * (n // 4 + 1)
                sc = sm[:, 2 * z:2 * z + 2, :].rearrange("p a b -> p (a b)")[:, 0:w]
                if n >= 2:
                    dve.wait_ge(s["sb_z_free"], n - 1)
                wait("sb_sp_cut")
                wait.after(dve.tensor_tensor_scan(sb_sum[:, z, 0:w][:, ::-1], ones_row[:, 0:w],
                                                  sb_sp[:, z, 0:w][:, ::-1], 0.0, ALU.mult, ALU.add))
                dve.tensor_tensor(sb_p[:, z, 0:w], sc, sb_sum[:, z, 0:w], ALU.subtract) \
                    .then_inc(s["sb_z_free"], 1)
                if n + 1 < 4 * NB:
                    sb_soft(n + 1)

            dve.wait_ge(s["sb_pt_copied"], 4 * NB)
            for z in range(2):
                dve.wait_ge(s[f"gate_stored{z}"], 16 * 16)
            wait.after(dve.memset(ones_row[:, 0:T:C], 0.0))
            for j in range(8):
                d = (rk_l, rk_lx)[j % 2]
                dve.tensor_scalar(d[:, 0:1], zr[:, j, 0:1], -1.0, None, ALU.mult)
                wait.after(dve.tensor_tensor(d[:, 1:T], zr[:, j, 0:T - 1], zr[:, j, 1:T], ALU.subtract))
                dve.scalar_tensor_tensor(zr[:, j, :], d[:, :], pcol("mu", j), zr[:, j, :], ALU.mult, ALU.add) \
                    .then_inc(s["rk_shift"], 1)
                wait("rk_shift")
            bonus, decay_end = small[:, 32:48], small[:, 48:64]
            for ft in range(2):
                zk, zv, zq = zr[:, 2 + ft, :], zr[:, 4 + ft, :], zr[:, ft, :]
                dve.tensor_scalar(rk_kk[:, :], zk, pcol("k_k", ft), None, ALU.mult).then_inc(s["rk_kk1"], 1)
                wait("rk_w")
                wait.after(dve.tensor_tensor_scan(rk_l[:, :], ones_row[:, :], rk_f[:, :], 0.0, ALU.mult, ALU.add))
                dve.tensor_tensor(rk_lx[:, :], rk_l[:, :], rk_f[:, :], ALU.subtract).then_inc(s["rk_cum"], 1)
                wait("rk_pow")
                wait.after(dve.tensor_scalar(rk_e[:, :], rk_e[:, :], 1e-12, None, ALU.max))
                wait.after(dve.reciprocal(rk_e[:, :], rk_e[:, :]))
                wait.after(dve.tensor_tensor(rk_kk[:, :], rk_kk[:, :], rk_e[:, :], ALU.mult))
                wait("rk_w")
                wait.after(dve.tensor_scalar(rk_e[:, :], rk_a[:, :], pcol("k_a", ft), k_a_rest[:, ft:ft + 1],
                                             ALU.mult, ALU.add))
                wait.after(dve.tensor_tensor(zk, zk, rk_e[:, :], ALU.mult))
                wait.after(dve.tensor_tensor(rk_b[:, :], rk_kk[:, :], rk_a[:, :], ALU.mult))
                dve.scalar_tensor_tensor(rk_e[:, :], zq, pcol("r_k", ft), zk, ALU.mult, ALU.mult) \
                    .then_inc(s["rk_bonus"], 1)
                wait("rk_pow")
                wait.after(dve.tensor_tensor(rk_b[:, :], rk_b[:, :], rk_f[:, :], ALU.mult))
                wait.after(dve.tensor_tensor(zk, zk, rk_f[:, :], ALU.mult))
                wait("rk_pow")
                wait.after(dve.scalar_tensor_tensor(rk_a[:, :], rk_kk[:, :], -1.0, rk_lx[:, :], ALU.mult, ALU.mult))
                wait("rk_pow")
                wait.after(dve.tensor_tensor(zq, zq, rk_l[:, :], ALU.mult))
                wait.after(dve.tensor_copy(decay_end, rk_l[:, C - 1:T:C]))
                wait("rk_bonus_p")
                dve.tensor_copy(bonus, sm[:, 2, 0:16]).then_inc(s["rk_bonus_taken"], 1)
                end = decay_end.unsqueeze(2).to_broadcast([P, NCH, C])
                dve.tensor_tensor(rk_e[:, :].rearrange("p (n c) -> p n c", n=NCH),
                                  rk_b[:, :].rearrange("p (n c) -> p n c", n=NCH), end, ALU.mult)
                dve.tensor_tensor(rk_f[:, :].rearrange("p (n c) -> p n c", n=NCH),
                                  zk.rearrange("p (n c) -> p n c", n=NCH), end, ALU.mult).then_inc(s["rk_prep"], 1)
                for b in range(1, 8, 2):
                    wait("rk_tok_t", 2)
                    dve.tensor_copy((a_tok, b_tok, k_tok, v_tok)[b // 2][:, 4:8, :],
                                    bank(b).rearrange("p (u c) -> p u c", u=4)).then_inc(s["rk_tok1"], 1)
                wide = [P, 4, P]

                def four(x):
                    return x.rearrange("p (u c) -> p u c", u=4)

                def spread(m):
                    return m[:, :].unsqueeze(1).to_broadcast(wide)

                for g in range(2):
                    for hh in range(2):
                        wait("rk_mats")
                        dve.tensor_tensor(m_t[:, hh], four(bank(2 * hh)), spread(mask_s), ALU.mult) \
                            .then_inc(s["rk_m"], 1)
                        dve.wait_ge(s["rk_m"], 4 * ft + 2 * g + hh + 1)
                        wait.after(dve.tensor_tensor(inv_t[:, hh], m_t[:, hh], spread(level[0]), ALU.mult))
                        dve.tensor_tensor(inv_t[:, hh], inv_t[:, hh], spread(ident), ALU.add)
                        wait("rk_mats")
                        wait.after(dve.tensor_tensor(inv[:, hh], four(bank(2 * hh + 1)), spread(level0_t), ALU.mult))
                        dve.tensor_tensor(inv[:, hh], inv[:, hh], spread(ident), ALU.add)
                        wait("rk_mats")
                        dve.tensor_tensor(n_t[:, hh], four(bank(4 + 2 * hh)), spread(mask_s), ALU.mult)
                        wait("rk_mats")
                        dve.tensor_tensor(rb_t[:, hh, 4 * g:4 * g + 4, :], four(bank(5 + 2 * hh)), spread(mask_i),
                                          ALU.mult)
                    for hh in range(2):
                        wait("rk_mats")
                        dve.tensor_tensor(rk_t[:, hh], four(bank(2 * hh)), spread(mask_i), ALU.mult) \
                            .then_inc(s["rk_mats_done"], 1)
                    wait("rk_mats_done", 2)
                    for n in range(1, 6):
                        for hh in range(2):
                            wait("rk_x")
                            if n < 5:
                                dve.tensor_tensor(inv[:, hh], inv[:, hh], four(bank(2 * hh + 1)), ALU.add)
                            dve.tensor_tensor(inv_t[:, hh], inv_t[:, hh], four(bank(4 + 2 * hh)), ALU.add) \
                                .then_inc(s["rk_x_added"], 1)
                        wait("rk_x_added", 2)
                    for hh in range(2):
                        wait("rk_xnv")
                        dve.tensor_copy(xnv[:, 4 * g:4 * g + 4, C * hh:C * hh + C],
                                        bank(2 * hh + 1)[:, 0:BW].rearrange("p (u c) -> p u c", u=4)) \
                            .then_inc(s["rk_round"], 1)
                dve.memset(s_all[:, 0, :], 0.0).then_inc(s["rk_state"], 1)
                wait("rk_state")
                for ch in range(NCH):
                    tt, pb = ch // 2, C * (ch % 2)
                    toks = slice(pb, pb + C)
                    wait("rk_chain")
                    dve.tensor_tensor(u_tok[toks, tt, :].rearrange("p (h c) -> p h c", h=2),
                                      gp[toks, 0, :].rearrange("p (h c) -> p h c", h=2)[:, :, 0:C],
                                      xnv[toks, tt, :].rearrange("p (h c) -> p h c", h=2), ALU.add) \
                        .then_inc(s["rk_u_added"], 1)
                    wait("rk_chain")
                    dve.scalar_tensor_tensor(s_all[:, ch + 1, :], s_all[:, ch, :], decay_end[:, ch:ch + 1],
                                             bank(6)[:, 0:C], ALU.mult, ALU.add).then_inc(s["rk_state"], 1)
                    wait("rk_state")
                for g in range(2):
                    wait("rk_y")
                    wait.after(dve.tensor_tensor(
                        y_tok[:, 4 * g:4 * g + 4, :].rearrange("p u (h c) -> p h u c", h=2),
                        sm[:, 2 * g:2 * g + 2, 0:BW].rearrange("p h (u c) -> p h u c", c=C),
                        y_loc[:, 4 * g:4 * g + 4, :].rearrange("p u (h c) -> p h u c", h=2), ALU.add))
                yg = y_tok[:, :, :].rearrange("p t (h c) -> p (t h) c", h=2)
                sq = y_sq[:, :, :].rearrange("p t (h c) -> p (t h) c", h=2)
                vg = v_tok[:, :, :].rearrange("p t (h c) -> p (t h) c", h=2)
                mean, var, root_v = small[:, 96:112], small[:, 64:80], small[:, 80:96]

                def over(v):
                    return v.unsqueeze(2).to_broadcast([P, 16, C])

                def row(n):
                    return row_g[:, n, P * ft:P * ft + P].unsqueeze(1).to_broadcast([P, NB, P])

                wait.after(dve.tensor_reduce(mean, yg, AX, ALU.add))
                wait.after(dve.tensor_scalar(mean, mean, -1.0 / C, None, ALU.mult))
                wait.after(dve.tensor_tensor(yg, yg, over(mean), ALU.add))
                wait.after(dve.tensor_tensor(sq, yg, yg, ALU.mult))
                dve.tensor_reduce(var, sq, AX, ALU.add).then_inc(s["rk_gvar"], 1)
                wait("rk_groot")
                wait.after(dve.reciprocal(root_v, root_v))
                wait.after(dve.tensor_tensor(yg, yg, over(root_v), ALU.mult))
                wait.after(dve.tensor_tensor(y_tok[:, :, :], y_tok[:, :, :], row(2), ALU.mult))
                wait.after(dve.tensor_tensor(y_tok[:, :, :], y_tok[:, :, :], row(3), ALU.add))
                wait.after(dve.tensor_tensor(sq, vg, over(bonus), ALU.mult))
                wait.after(dve.tensor_tensor(yg, yg, sq, ALU.add))
                for b in range(2):
                    wait("rk_y")
                    ins = dve.tensor_tensor(y_tok[:, 4 * b:4 * b + 4, :], y_tok[:, 4 * b:4 * b + 4, :],
                                            four(bank(4 + b)), ALU.mult)
                ins.then_inc(s["rk_y_ready"], 1)

            for n, y in enumerate((y_a, y_b, y_c, y_d)):
                for ft in range(2):
                    wait("high")
                    dve.tensor_tensor(y_lo[:, 2 * n + ft, :], y[:, ft, :], y_hi[:, 2 * n + ft, :].bitcast(F32),
                                      ALU.subtract).then_inc(s["y_split"], 1)
            for d in range(KT):
                split_weights(T_BR + d + 1)
                if d >= 2:
                    wait("m_split")
                for n in range(4):
                    q = 4 * d + n
                    p = P_BR + q
                    dve.wait_ge(s["p_ready"], p + 1)
                    dve.wait_ge(s[f"gate_in{n}"], 16 * (d + 1))
                    o = merged[:, d % 2, :] if n == 0 else gated[:, q % 2, :]
                    if n and q >= 3:
                        dve.wait_ge(s["merge_add"], merge_adds(q - 2))
                    dve.tensor_tensor(o, gp[:, p % 2, :], gate_in[:, n, :], ALU.mult).then_inc(s[f"p_free{p % 2}"], 1)
                wait("high")
                dve.tensor_tensor(m_lo[:, d, :], merged[:, d % 2, :], m_hi[:, d, :].bitcast(F32),
                                  ALU.subtract).then_inc(s["m_split"], 1)
            for d in range(KT):
                split_weights(T_WO + d + 1)
                p = P_WO + d
                dve.wait_ge(s["p_ready"], p + 1)
                dve.wait_ge(s[f"x_back{d % 2}"], 16 * (d // 2 + 1))
                dve.tensor_tensor(x_mid[:, d, :], gp[:, p % 2, :], x_back[:, d % 2, :], ALU.add) \
                    .then_inc(s[f"p_free{p % 2}"], 1)
            norm(x_mid, "ffn_g")

            def taps(tap, j, i):
                return col[:, bass.ds(2 * i + (ROWS["conv"] + 2 * FT * tap + 2 + j), 1)]

            def conv(i, buf, j, p):
                dve.wait_ge(s["c_first"], 4 * i + (5 + buf))
                ps = gp[:, p % 2, :]
                dve.scalar_tensor_tensor(hid[:, buf, 1:T], ps[:, 0:T - 1], taps(1, j, i), hid[:, buf, 1:T],
                                         ALU.mult, ALU.add).then_inc(s["conv_mid"], 1)
                dve.wait_ge(s["conv_mid"], 4 * i + (5 + buf))
                dve.scalar_tensor_tensor(hid[:, buf, 2:T], ps[:, 0:T - 2], taps(0, j, i), hid[:, buf, 2:T],
                                         ALU.mult, ALU.add).then_inc(s[f"p_free{p % 2}"], 1)

            def glu(i, k, p):
                dve.wait_ge(s[f"p_free{p % 2}"], 6 * i + (frees_before(p) + 1))
                dve.wait_ge(s["silu"], 2 * i + (3 + k))
                g = hid[:, 2 * k + 1, :]
                dve.tensor_tensor(g, hid[:, 2 * k, :], g, ALU.mult).then_inc(s["g_raw"], 1)
                dve.wait_ge(s["g_high"], 2 * i + (3 + k))
                dve.tensor_tensor(g_lo[:, k, :], g, g_hi[:, k, :].bitcast(F32), ALU.subtract) \
                    .then_inc(s["g_split"], 1)

            def add_down(i, u, p):
                for j in range(4):
                    d = 4 * u + j
                    dve.wait_ge(s["p_ready"], 12 * i + (p + j + 1))
                    for z in range(2):
                        dve.wait_ge(s[f"p_free{z}"], 6 * i + (frees_before(p) - 2))
                    dve.tensor_tensor(x_mid[:, d, :], x_mid[:, d, :], gp[:, (p + j) % 2, :], ALU.add) \
                        .then_inc(s[f"p_free{(p + j) % 2}"], 1)

            for n in range(4):
                split_weights(T_FFN + n + 1)
                conv(-1, n, (0, FT, 1, FT + 1)[n], P_FFN + 12 + n)
                if n % 2:
                    glu(-1, n // 2, P_FFN + 12 + n)
            p0 = P_FFN + 4
            with dve.Fori(0, FT // 2 - 1) as i:
                for u in range(6):
                    dve.wait_ge(s["w_high"], 6 * i + (T_FFN + 6 + u))
                    z = (u + 1) % 2
                    dve.tensor_tensor(w_lo[:, z, :], w_raw[:, z, :], w_hi[:, z, :].bitcast(F32),
                                      ALU.subtract).then_inc(s["w_split"], 1)
                    if u == 0:
                        conv(i, 0, 0, p0)
                    elif u < 3:
                        add_down(i, u - 1, p0 + 1 + 4 * (u - 1))
                    elif u == 3:
                        conv(i, 1, FT, p0 + 9)
                        glu(i, 0, p0 + 9)
                    elif u == 4:
                        conv(i, 2, 1, p0 + 10)
                    else:
                        conv(i, 3, FT + 1, p0 + 11)
                        glu(i, 1, p0 + 11)
            split_weights(T_IN2 - 1)
            add_down(FT // 2 - 1, 0, p0)
            split_weights(T_IN2)
            add_down(FT // 2 - 1, 1, p0 + 4)
            norm(x_mid, "fin_g", x_mid)
            norm(x_mid, "g2")
            for t in range(T_IN2, T_UQ):
                split_weights(t + 1)
                if t - T_IN2 == 13:
                    for b in range(8):
                        ft, half = divmod(b, 2)
                        wait("v_turned")
                        dve.tensor_copy(v_2[:, 4 * half:4 * half + 4, P * ft:P * ft + P],
                                        sm[:, b % 4, :].rearrange("p (n c) -> p n c", n=4)).then_inc(s["v_taken"], 1)
            wait("bias_p")
            dve.tensor_copy(bias_vec[:, :].rearrange("p (n c) -> p n c", n=3), sm[0:HEADS_A, 0:3, 0:384]) \
                .then_inc(s["bias_rows"], 1)
            for j in range(8):
                t = (q_2, k_2)[j // 4][:, j % 4, :]
                wait("n2_rt")
                wait.after(dve.reciprocal(nrt[:, j % 2, :], nrt[:, j % 2, :]))
                dve.scalar_tensor_tensor(t, t, a_q_scaled[:, :] if j < 4 else pcol("a_k"), nrt[:, j % 2, :],
                                         ALU.mult, ALU.mult).then_inc(s["n2_q"], 1)

            def attention(block, table_of, scale, out_of):
                def scores(n):
                    z, w = n % 2, P * (block(n) + 1)
                    wait("at_z")
                    tab = table_of(n)
                    dve.tensor_tensor_reduce(
                        out=att_s[:, z, 0:w], in0=sm[:, 2 * z:2 * z + 2, :].rearrange("p a b -> p (a b)")[:, 0:w],
                        in1=tab[:, T - w:T], scale=1.0, scalar=-3e38, op0=ALU.add, op1=ALU.max,
                        accum_out=small[:, 100 + z:101 + z]).then_inc(s["at_s"], 1)
                    wait("at_s")
                    dve.tensor_scalar(small[:, 102 + z:103 + z], small[:, 100 + z:101 + z], -scale, None,
                                      ALU.mult).then_inc(s["at_m"], 1)

                scores(0)
                for n in range(UNITS):
                    if n < UNITS - 1:
                        scores(n + 1)
                    z = n % 2
                    wait("at_p")
                    wait.after(dve.reciprocal(small[:, 106 + z:107 + z], small[:, 104 + z:105 + z]))
                    wait("at_o")
                    dve.tensor_scalar(out_of(n), o_place(n),
                                      small[:, 106 + z:107 + z], None, ALU.mult).then_inc(s["at_o_taken"], 1)
                    after_unit(n, block)

            def after_unit(n, block):
                if block(8) == 1 and n % 8 == 7:
                    qb = n // 8
                    wait("z_turned")
                    zb = z_b[:, :, P * qb:P * qb + P]
                    dve.tensor_tensor(zb, zb, gp[:, 0, 0:HALF].rearrange("p (f t) -> p f t", f=4), ALU.mult) \
                        .then_inc(s["z_done"], 1)

            def bias_table(n):
                h = n // NB
                if n % NB == 0:
                    dve.wait_ge(s[f"table_in{h % 2}"], 16 * (h // 2 + 1))
                return table[:, h % 2, :]

            attention(lambda n: n % NB, bias_table, 1.0,
                      lambda n: o_all[:, n % NB, C * (n // NB):C * (n // NB) + C])
            for qb in range(NB):
                wait("z_turned")
                za = z_a[:, :, P * qb:P * qb + P]
                dve.tensor_tensor(za, za, sm[:, qb % 4, :].rearrange("p (f t) -> p f t", f=4), ALU.mult) \
                    .then_inc(s["z_done"], 1)
            wait("c_root")
            wait.after(dve.reciprocal(nrt[:, 0, :], nrt[:, 0, :]))
            for k in range(2):
                dve.scalar_tensor_tensor(c_q[:, k, :], c_q[:, k, :], pcol("q_c", k), nrt[:, 0, :],
                                         ALU.mult, ALU.mult).then_inc(s["q_normed"], 1)
            wait("c_root")
            wait.after(dve.reciprocal(nrt[:, 1, :], nrt[:, 1, :]))
            dve.wait_ge(s["q_normed"], 2)
            dve.scalar_tensor_tensor(c_kv[:, :], c_kv[:, :], pcol("kv_c"), nrt[:, 1, :], ALU.mult, ALU.mult) \
                .then_inc(s["kv_normed"], 1)
            rope = slice(C, C + 32)
            wait("c_root")
            wait.after(dve.reciprocal(nrt[rope, 0, :], nrt[rope, 0, :]))
            dve.scalar_tensor_tensor(k_rope[rope, :], k_rope[rope, :], col[rope, ROWS["kn"]:ROWS["kn"] + 1],
                                     nrt[rope, 0, :], ALU.mult, ALU.mult).then_inc(s["krope_normed"], 1)
            for k in range(2):
                wait("high")
                dve.tensor_tensor(cq_lo[:, k, :], c_q[:, k, :], cq_hi[:, k, :].bitcast(F32),
                                  ALU.subtract).then_inc(s["q_split"], 1)
            wait("high")
            dve.tensor_tensor(ckv_lo[:, 0, :], c_kv[:, :], ckv_hi[:, 0, :].bitcast(F32), ALU.subtract) \
                .then_inc(s["kv_split"], 1)
            wait("pos_in", 16)
            dve.wait_ge(s["q_split"], 2)
            dve.wait_ge(s["krope_normed"], 1)
            ang, turns = nrt[rope, 0, :], nrt[rope, 1, :]
            wait.after(dve.tensor_copy(ang, pos_i[rope, :]))
            wait.after(dve.tensor_scalar(ang, ang, freq[rope, :], None, ALU.mult))
            wait.after(dve.tensor_scalar(turns, ang, 1.0 / (2 * math.pi), ROUND, ALU.mult, ALU.add))
            wait.after(dve.tensor_scalar(turns, turns, -ROUND, None, ALU.add))
            for part in TURN:
                wait.after(dve.scalar_tensor_tensor(ang, turns, -part, ang, ALU.mult, ALU.add))
            wait.after(dve.tensor_scalar(sin_t[rope, :], ang, -PI_IN, PI_IN, ALU.max, ALU.min))
            wait.after(dve.tensor_scalar(ang, ang, math.pi / 2, None, ALU.add))
            wait.after(dve.tensor_scalar(turns, ang, math.pi, -2 * math.pi, ALU.is_gt, ALU.mult))
            wait.after(dve.tensor_tensor(ang, ang, turns, ALU.add))
            dve.tensor_scalar(cos_t[rope, :], ang, -PI_IN, PI_IN, ALU.max, ALU.min).then_inc(s["angles"], 1)

            def add_rope(view):
                wait("rot")
                t = hn_root[rope, :]
                wait.after(dve.tensor_tensor(t, sm[rope, 2:4, :].rearrange("p a b -> p (a b)"), sin_t[rope, :],
                                             ALU.mult))
                wait.after(dve.tensor_tensor(view, view, cos_t[rope, :], ALU.mult))
                dve.tensor_tensor(view, view, t, ALU.add).then_inc(s["rot_used"], 1)

            wait("hn_rt", 2)
            add_rope(k_rope[rope, :])
            dve.wait_ge(s["rot_used"], 1)
            split_weights(T_UQ + 1)
            split_weights(T_UKV)
            for h in range(HEADS_B):
                wait("hn_rt")
                wait.after(dve.reciprocal(hn_root[0:DQK, :], hn_root[0:DQK, :]))
                dve.scalar_tensor_tensor(qh[:, h, :], qh[:, h, :], col[0:DQK, ROWS["qn"]:ROWS["qn"] + 1],
                                         hn_root[0:DQK, :], ALU.mult, ALU.mult).then_inc(s["hn_done"], 1)
                dve.wait_ge(s["hn_done"], h + 1)
                add_rope(qh[rope, h, :])
            for h in range(HEADS_B):
                ins = dve.tensor_copy(kh[rope, h, :], k_rope[rope, :])
            ins.then_inc(s["k_rope_spread"], 1)
            for h in range(HEADS_B):
                for half in range(2):
                    if half == 0:
                        wait("vb_turned")
                    ins = dve.tensor_copy(v_b[:, 4 * half:4 * half + 4, C * h:C * h + C],
                                          sm[:, 2 + half, 0:BW].rearrange("p (n c) -> p n c", n=4))
                ins.then_inc(s["vb_taken"], 1)
                wait("hn_rt")
                wait.after(dve.reciprocal(hn_root[0:C, :], hn_root[0:C, :]))
                dve.scalar_tensor_tensor(kh[0:C, h, :], kh[0:C, h, :], col[0:C, ROWS["kn"]:ROWS["kn"] + 1],
                                         hn_root[0:C, :], ALU.mult, ALU.mult).then_inc(s["hn_done"], 1)
                dve.wait_ge(s["hn_done"], HEADS_B + h + 1)
            split_weights(T_OUT)
            split_weights(T_OUT + 1)
            wait("causal")
            attention(lambda n: n // 8, lambda n: causal, DQK ** -0.5,
                      lambda n: o_b[:, (n // 8) % 2, C * (n % 8):C * (n % 8) + C])
            for k in range(8):
                wait("high")
                dve.tensor_tensor(mix_lo[:, k, :], (z_a, z_b)[k // 4][:, k % 4, :], mix_hi[:, k, :].bitcast(F32),
                                  ALU.subtract).then_inc(s["mix_split"], 1)
            for d in range(KT):
                if 1 <= d < KT - 1:
                    split_weights(T_OUT + d + 1)
                p = P_OUT + d
                dve.wait_ge(s["p_ready"], p + 1)
                dve.wait_ge(s[f"x_back{d % 2}"], 16 * (KT // 2 + d // 2 + 1))
                if d >= 2:
                    dve.wait_ge(s["out_t"], d - 1)
                dve.tensor_tensor(x_out[:, d % 2, :], gp[:, p % 2, :], x_back2[:, d % 2, :], ALU.add) \
                    .then_inc(s[f"p_free{p % 2}"], 1)


_INS = ["x", "mix_norm_g", "w_in", "gate_b", "sc_conv_w", "sc_out", "sb_out", "rw_mu", "rw_w0", "rw_w2",
        "rw_a0", "rw_a2", "rw_g2", "rw_k_k", "rw_k_a", "rw_r_k", "rw_gn_g", "rw_gn_b", "rw_out", "sg_ln_g",
        "sg_ln_b", "sg_w", "sg_b", "sg_out", "w_o", "ffn_norm_g", "w_up", "ffn_conv_w", "w_down",
        "final_norm_g", "positions_2", "rel_bias_2", "norm_gain_2", "w_in_2", "a_q_gain_2", "a_k_gain_2",
        "q_c_gain_2", "w_uq_2", "kv_c_gain_2", "w_ukv_2", "qn_gain_2", "qr_gain_2", "kn_gain_2",
        "kr_gain_2", "w_out_2"]


def shape_tables():
    dist = 1023 - np.arange(1152)
    safe = np.maximum(dist, 0)
    large = 16 + (np.log(np.maximum(safe, 1).astype(np.float32) / np.float32(16))
                  / np.float32(math.log(2048 / 16)) * 16).astype(np.int32)
    bucket = np.where(safe < 16, safe, np.minimum(large, 31))
    count = sum(((dist >= 0) & (dist % d == 0) & (dist <= w)).astype(int)
                for w, d in ((128, 1), (512, 4), (2048, 16)))
    table = np.zeros((33, 1152), np.float32)
    table[bucket, np.arange(1152)] = 1.0
    table[32] = np.where(count > 0, np.log(np.maximum(count, 1)), NEG)
    freq = (np.float32(10000.0) ** (-np.arange(0, 32, 2, dtype=np.float32) / np.float32(32)))
    return table, np.tile(freq, 8).astype(np.float32).reshape(P, 1)


def kernel(**inputs):
    import concourse.bacc as _bacc
    from concourse.bass_utils import run_bass_kernel_spmd as _run

    nc = _bacc.Bacc("TRN2", target_bir_lowering=False, num_devices=1)
    arrays, args = {}, []
    table, freq = shape_tables()
    for name in _INS + ["bucket_table", "rope_freq"]:
        a = {"bucket_table": table, "rope_freq": freq}.get(name)
        a = np.ascontiguousarray(inputs[name] if a is None else a)
        arrays[f"in_{name}"] = a
        args.append(nc.dram_tensor(f"in_{name}", a.shape, mybir.dt.from_np(a.dtype), kind="ExternalInput").ap())
    args.append(nc.dram_tensor("out_0", (1, T, D), F32, kind="ExternalOutput").ap())
    hybrid_layers(nc, *args)
    r = _run(nc, [arrays], core_ids=[0])
    return r.results[0]["out_0"]
```

```python
import math
from contextlib import ExitStack

import numpy as np
import concourse.bass as bass
from concourse import mybir

P = 128
T = 1024
D = 1024
KT = D // P
HALF = 512
NB = T // P
BW = 256
BT = BW // P
C = 64
NCH = T // C
FT = 22
HEADS_A = 8
HEADS_B = 8
DQK = 96
RMS_EPS = 1e-6
LN_EPS = 1e-5
GN_EPS = 64e-5
DECAY = math.exp(-0.5)
NEG = -1e30
UNITS = 64
ROUND = 1.5 * 2.0 ** 23
TURN = (6.28125, 0.0019350051879882812, 3.0198944141e-07)
PI_IN = 3.1415925

ALU = mybir.AluOpType
ACT = mybir.ActivationFunctionType
F32 = mybir.dt.float32
FR = mybir.dt.float32r
I32 = mybir.dt.int32
AX = mybir.AxisListType.X

ROWS = {}
_n = 0
for _name, _count in (("mix_g", 8), ("gate_b", 32), ("sc_w", 6), ("mu", 8), ("w0", 2), ("a0", 2),
                      ("k_k", 2), ("k_a", 2), ("r_k", 2), ("ffn_g", 8), ("fin_g", 8), ("g2", 8),
                      ("q_c", 2), ("kv_c", 1), ("a_q", 1), ("a_k", 1), ("qn", 1), ("kn", 1)):
    ROWS[_name] = _n
    _n += _count
assert _n <= P
ROWS["conv"] = P
NCOL = P + 3 * 2 * FT

T_IN = 0
T_GATE = 24
T_BR = 56
T_WO = 64
T_FFN = 72
T_IN2 = T_FFN + 6 * (FT // 2)
T_UQ = T_IN2 + 24
T_UKV = T_UQ + 2
T_OUT = T_UKV + 1
T_END = T_OUT + 8
P_IN = 0
P_GATE = 24
P_BR = 56
P_WO = P_BR + 32
P_FFN = P_WO + 8
P_IN2 = P_FFN + 12 * (FT // 2)
P_UQ = P_IN2 + 24
P_UKV = P_UQ + 8
P_OUT = P_UKV + 8
P_END = P_OUT + 8


def outs_through(t):
    if t < T_BR:
        return t + 1
    if t < T_WO:
        return P_BR + 4 * (t - T_BR + 1)
    if t < T_FFN:
        return P_WO + (t - T_WO + 1)
    if t < T_IN2:
        n = t - T_FFN
        if n < 4:
            return P_FFN + n + 1
        f, u = divmod(n - 4, 6)
        if f == FT // 2 - 1:
            return P_FFN + 4 + 12 * f + 4 * (u + 1)
        return P_FFN + 4 + 12 * f + (1, 5, 9, 10, 11, 12)[u]
    if t < T_UQ:
        return P_IN2 + (t - T_IN2 + 1)
    if t < T_UKV:
        return P_UQ + 4 * (t - T_UQ + 1)
    if t < T_OUT:
        return P_UKV + 8
    return P_OUT + (t - T_OUT + 1)


def ffn_block(t):
    n = t - T_FFN
    if n < 4:
        f, u = 0, (0, 3, 4, 5)[n]
    else:
        f, u = 1 + (n - 4) // 6, (n - 4) % 6
        if f == FT // 2:
            u += 1
    if u in (1, 2):
        return "down", 2 * (f - 1), u - 1
    j = 2 * f + (u > 3)
    return "up", P * j + (P * FT if u in (3, 5) else 0)


def block_dmas(t):
    if T_BR <= t < T_WO or t == T_IN2 + 19:
        return 4
    return 1


def loaded_value(t):
    return 16 * sum(block_dmas(s) for s in range(t % 2, t + 1, 2))


def block_columns(t):
    return 768 if T_UQ <= t < T_UKV else 1024


def frees_before(p):
    return p // 2 if p < P_GATE else P_GATE // 2 + (p - P_BR) // 2


def merge_adds(q):
    return 3 * (q // 4) + q % 4


PRM_DMAS = 14 + 8 + 2
PAR_DMAS = 4 + 6

SEMS = (
    "w_split", "prm_clear", "prm_in", "rel_in", "par_in", "h_ready", "x_out", "gate_ready",
    "y_split", "p_ready", "bias_rows", "bias_out", "at_s", "q_split", "kv_split", "pos_in",
    "at_pt_copied", "out_taken", "consts", "wsg_copied", "wsg_ready", "rk_m", "rk_p", "rk_lv",
    "merge_add", "mla_ones", "causal", "square", "square_used", "col_t", "wsg_t", "cols", "x_t",
    "v_turned", "v_taken", "sg_normed", "sg_mixed", "sg_done", "sb_zc", "sb_z", "sb_pt_copied",
    "sb_p_cut", "sb_pt", "sb_o", "sb_o_copied", "sb_y_free", "sb_y", "rk_lora", "rk_g_free",
    "rk_lora_p", "rk_kk2", "rk_bonus", "rk_bonus_p", "rk_bonus_taken", "rk_prep", "rk_tok_t",
    "rk_mats", "rk_mats_done", "rk_x_added", "rk_copied", "rk_x", "rk_nv", "rk_xnv", "rk_round",
    "rk_round_act", "rk_state", "rk_chain", "rk_u_added", "rk_y", "rk_y_ready", "rk_y_t",
    "g_split", "h_split", "bias_p", "n2_sq", "n2_ss", "n2_q", "at_z", "at_o_taken", "at_o",
    "at_p", "at_pt", "z_done", "z_turned", "c_sq", "c_ss", "c_root", "rot", "krope_normed",
    "hn_sq", "hn_ss", "rot_used", "hn_rt", "hn_done", "vb_taken", "vb_turned", "k_rope_spread",
    "out_t", "w_high", "root", "high", "x_turned0", "x_turned1", "sc_done", "sg_var", "sg_root",
    "sb_e", "sb_l", "sb_p", "rk_shift", "rk_kk1", "rk_w", "rk_pow", "rk_cum", "rk_tok0",
    "rk_gvar", "rk_groot", "c_first", "silu", "g_raw", "g_high", "at_m", "kv_normed",
    "q_normed", "angles", "x_normed", "p_free0", "p_free1", "sb_sp", "sb_sp_cut", "rk_tok1",
    "m_split", "conv_mid", "n2_rt", "mix_split", "w_loaded0", "w_loaded1", "x_in0", "x_in1",
    "gate_stored0", "gate_stored1", "gate_in0", "gate_in1", "gate_in2", "gate_in3", "x_back0",
    "x_back1", "table_in0", "table_in1", "stored0", "stored1", "pool_own", "act_own", "dve_own",
)


def hybrid_layers(nc, x, mix_norm_g, w_in, gate_b, sc_conv_w, sc_out, sb_out, rw_mu, rw_w0, rw_w2,
                  rw_a0, rw_a2, rw_g2, rw_k_k, rw_k_a, rw_r_k, rw_gn_g, rw_gn_b, rw_out, sg_ln_g,
                  sg_ln_b, sg_w, sg_b, sg_out, w_o, ffn_norm_g, w_up, ffn_conv_w, w_down,
                  final_norm_g, positions_2, rel_bias_2, norm_gain_2, w_in_2, a_q_gain_2,
                  a_k_gain_2, q_c_gain_2, w_uq_2, kv_c_gain_2, w_ukv_2, qn_gain_2, qr_gain_2,
                  kn_gain_2, kr_gain_2, w_out_2, bucket_table, rope_freq, out):
    x_spill = nc.dram_tensor("x_spill", [P, KT, T], F32, kind="Internal").ap()
    gates_spill = nc.dram_tensor("gates_spill", [32, P, T], F32, kind="Internal").ap()
    bias_spill = nc.dram_tensor("bias_spill", [HEADS_A, P, 1152], F32, kind="Internal").ap()

    with ExitStack() as ctx:
        base = [-(-nc.sbuf_base // 32) * 32]

        def at(name, shape, dtype, offset):
            return nc.alloc_sbuf_tensor_at(name, shape, dtype, offset=offset)

        def fixed(name, shape, dtype=F32):
            size = int(np.prod(shape[1:])) * 4
            h = at(name, shape, dtype, base[0])
            base[0] += -(-size // 32) * 32
            return h

        ident = fixed("ident", [P, P])
        ones = fixed("ones", [P, P])
        head_ones = fixed("head_ones", [P, P])
        rope_turn = fixed("rope_turn", [P, 32])
        mask_s = fixed("mask_s", [P, P])
        mask_i = fixed("mask_i", [P, P])
        level = [fixed(f"level{n}", [P, P]) for n in range(6)]
        level0_t = fixed("level0_t", [P, P])
        group_sel = fixed("group_sel", [4, 2, P])
        col = fixed("col", [P, NCOL])
        k_a_rest = fixed("k_a_rest", [P, 2])
        a_q_scaled = fixed("a_q_scaled", [P, 1])
        row_g = fixed("row_g", [P, 4, BW])
        lora = fixed("lora", [P, 2, BW])
        sg_bias = fixed("sg_bias", [4, P])
        rel_rows = fixed("rel_rows", [33, HEADS_A])
        small = fixed("small", [P, 128])
        ones_row = fixed("ones_row", [P, T])
        mla_ones = fixed("mla_ones", [DQK, DQK])
        freq = fixed("freq", [P, 1])

        X0 = base[0]
        x_t = at("x_t", [P, KT, T], F32, X0)
        W0 = X0 + 32768
        w_raw = at("w_raw", [P, 2, 1024], F32, W0)
        w_hi = at("w_hi", [P, 2, 1024], FR, W0 + 8192)
        w_lo = at("w_lo", [P, 2, 1024], FR, W0 + 16384)
        H0 = W0 + 24576
        h_hi = at("h_hi", [P, KT, T], FR, H0)
        h_lo = at("h_lo", [P, KT, T], FR, H0 + 32768)
        A0 = H0 + 65536
        K = 1024

        x_tok = at("x_tok", [P, NB, D], F32, A0)
        squares = at("squares", [P, 2, T], F32, A0 + 40 * K)
        root = at("root", [P, T], F32, A0 + 48 * K)
        rstd = at("rstd", [P, T], F32, A0 + 52 * K)
        h_tmp = at("h_tmp", [P, 2, T], F32, A0 + 56 * K)
        prm = at("prm", [P, 3, P], F32, A0 + 32 * K)
        sg_w_raw = at("sg_w_raw", [P, 4, P], F32, A0 + 36 * K)
        y_a = at("y_a", [P, BT, T], F32, A0)
        y_d = at("y_d", [P, BT, T], F32, A0 + 8 * K)
        q_sb = at("q_sb", [P, BT, T], F32, A0 + 16 * K)
        k_sb = at("k_sb", [P, BT, T], F32, A0 + 24 * K)
        v_sb = at("v_sb", [P, NB, BW], F32, A0 + 32 * K)
        y_b = at("y_b", [P, BT, T], F32, A0 + 40 * K)
        y_c = at("y_c", [P, BT, T], F32, A0 + 48 * K)
        zr = at("zr", [P, 8, T], F32, X0)
        sc_c = at("sc_c", [P, BT, T], F32, A0 + 48 * K)
        sc_cx = at("sc_cx", [P, BT, T], F32, A0 + 56 * K)
        vt_sb = at("vt_sb", [P, BT, T], F32, A0 + 56 * K)
        vt_sg = at("vt_sg", [P, BT, T], F32, A0 + 56 * K)
        v_sg = at("v_sg", [P, NB, BW], F32, A0 + 40 * K)
        w_sg = at("w_sg", [P, 4, P], F32, A0 + 64 * K)
        gate_out = at("gate_out", [P, 2, T], F32, A0 + 56 * K)
        sb_zc = at("sb_zc", [P, 2, 2, T], F32, H0)
        sb_l = at("sb_l", [P, 2, 2, T], F32, H0 + 16 * K)
        sb_sp = at("sb_sp", [P, 2, 2, T], F32, H0 + 32 * K)
        sb_pt = at("sb_pt", [P, 2, T], F32, H0 + 48 * K)
        sb_o = at("sb_o", [P, 2, BW], F32, H0 + 56 * K)
        rk_a = at("rk_a", [P, T], F32, H0)
        rk_b = at("rk_b", [P, T], F32, H0 + 4 * K)
        rk_kk = at("rk_kk", [P, T], F32, H0 + 8 * K)
        rk_l = at("rk_l", [P, T], F32, H0 + 12 * K)
        rk_lx = at("rk_lx", [P, T], F32, H0 + 16 * K)
        rk_e = at("rk_e", [P, T], F32, H0 + 20 * K)
        rk_f = at("rk_f", [P, T], F32, H0 + 24 * K)
        rk_sg = at("rk_sg", [P, T], F32, H0 + 28 * K)
        rk_th = at("rk_th", [P, T], F32, H0 + 32 * K)
        a_tok = at("a_tok", [P, NB, P], F32, H0 + 36 * K)
        b_tok = at("b_tok", [P, NB, P], F32, H0 + 40 * K)
        k_tok = at("k_tok", [P, NB, P], F32, H0 + 44 * K)
        v_tok = at("v_tok", [P, NB, P], F32, H0 + 48 * K)
        xa_t = at("xa_t", [P, T], F32, H0 + 52 * K)
        xnv = at("xnv", [P, NB, P], F32, H0 + 56 * K)
        y_loc = at("y_loc", [P, NB, P], F32, H0 + 60 * K)
        rb_t = at("rb_t", [P, 2, NB, P], F32, A0 + 16 * K)
        y_tok = at("y_tok", [P, NB, P], F32, A0 + 24 * K)
        u_tok = at("u_tok", [P, NB, P], F32, A0 + 28 * K)
        s_all = at("s_all", [P, NCH + 1, C], F32, A0 + 32 * K)
        m_t = at("m_t", [P, 2, 4, P], F32, H0 + 8 * K)
        m_lv = at("m_lv", [P, 2, 4, P], F32, H0 + 12 * K)
        inv = at("inv", [P, 2, 4, P], F32, H0 + 16 * K)
        inv_t = at("inv_t", [P, 2, 4, P], F32, H0 + 20 * K)
        m_p = at("m_p", [P, 2, 4, P], F32, H0 + 24 * K)
        n_t = at("n_t", [P, 2, 4, P], F32, A0 + 56 * K)
        rk_t = at("rk_t", [P, 2, 4, P], F32, A0 + 60 * K)
        nv = at("nv", [P, 2, 4, C], F32, A0 + 64 * K)
        y_sq = at("y_sq", [P, NB, P], F32, H0 + 8 * K)
        y_hi = at("y_hi", [P, 8, T], FR, H0)
        y_lo = at("y_lo", [P, 8, T], FR, H0 + 32768)

        gate_in = at("gate_in", [P, 4, T], F32, A0)
        merged = at("merged", [P, 2, T], F32, A0 + 16 * K)
        gated = at("gated", [P, 2, T], F32, A0 + 24 * K)
        m_hi = at("m_hi", [P, KT, T], FR, X0)
        m_lo = at("m_lo", [P, KT, T], FR, A0 + 32 * K)
        x_back = at("x_back", [P, 2, T], F32, H0)
        x_mid = at("x_mid", [P, KT, T], F32, A0)
        hid = at("hid", [P, 4, T], F32, A0 + 32 * K)
        g_hi = at("g_hi", [P, 2, T], FR, X0)
        g_lo = at("g_lo", [P, 2, T], FR, X0 + 8 * K)
        q_2 = at("q_2", [P, 4, T], F32, X0)
        k_2 = at("k_2", [P, 4, T], F32, X0 + 16 * K)
        v_2 = at("v_2", [P, NB, 512], F32, A0)
        z_a = at("z_a", [P, 4, T], F32, A0 + 16 * K)
        vt_2 = at("vt_2", [P, 4, T], F32, A0 + 32 * K)
        z_b = at("z_b", [P, 4, T], F32, A0 + 32 * K)
        c_q = at("c_q", [P, 2, T], F32, A0 + 48 * K)
        c_kv = at("c_kv", [P, T], F32, A0 + 56 * K)
        k_rope = at("k_rope", [P, T], F32, A0 + 60 * K)
        nsq = at("nsq", [P, 2, T], F32, H0)
        nrt = at("nrt", [P, 2, T], F32, H0 + 8 * K)
        table = at("table", [P, 2, T], F32, H0 + 16 * K)
        buckets = at("buckets", [33, 1152], F32, H0 + 24 * K)
        bias_vec = at("bias_vec", [HEADS_A, 1152], F32, H0 + 48 * K)
        att_s = at("att_s", [P, 2, T], F32, H0 + 32 * K)
        att_pt = at("att_pt", [P, 2, T], F32, H0 + 40 * K)
        o_all = at("o_all", [P, NB, 512], F32, H0 + 48 * K)
        cq_hi = at("cq_hi", [P, 2, T], FR, H0 + 32 * K)
        cq_lo = at("cq_lo", [P, 2, T], FR, H0 + 40 * K)
        ckv_hi = at("ckv_hi", [P, 1, T], FR, H0 + 48 * K)
        ckv_lo = at("ckv_lo", [P, 1, T], FR, H0 + 52 * K)
        cos_t = at("cos_t", [P, T], F32, A0 + 48 * K)
        sin_t = at("sin_t", [P, T], F32, A0 + 52 * K)
        pos_i = at("pos_i", [P, T], I32, A0 + 56 * K)
        vb_t = at("vb_t", [P, T], F32, A0 + 56 * K)
        nsq_b = at("nsq_b", [P, 2, T], F32, H0 + 56 * K)
        rt_q = at("rt_q", [P, 2, T], F32, H0 + 16 * K)
        rt_k = at("rt_k", [P, 2, T], F32, H0 + 32 * K)
        rope_tmp = at("rope_tmp", [P, T], F32, H0 + 24 * K)
        qh = at("qh", [DQK, HEADS_B, T], F32, X0)
        kh = at("kh", [DQK, HEADS_B, T], F32, H0)
        v_b = at("v_b", [P, NB, 512], F32, A0)
        causal = at("causal", [P, T], F32, H0 + 48 * K)
        o_b = at("o_b", [P, NB, 512], F32, A0 + 48 * K)
        mix_hi = at("mix_hi", [P, KT, T], FR, X0)
        mix_lo = at("mix_lo", [P, KT, T], FR, H0)
        x_back2 = at("x_back2", [P, 2, T], F32, H0 + 32 * K)
        x_out = at("x_out", [P, 2, T], F32, H0 + 40 * K)
        out_tok = at("out_tok", [P, 2, NB, P], F32, H0 + 48 * K)

        gp = ctx.enter_context(nc.psum_tensor("gp", [P, 2, T], F32))
        sm = ctx.enter_context(nc.psum_tensor("sm", [P, 4, HALF], F32))

        s = {name: ctx.enter_context(nc.semaphore(name)) for name in SEMS}
        block = ctx.enter_context(nc.Block())

        def pcol(name, n=0):
            c = ROWS[name] + n
            return col[:, c:c + 1]

        def raw_block(slot, k, a=0, b=None):
            n = 1024 // k
            return w_raw[:, slot, 0:k * n].rearrange("p (k c) -> p k c", k=k)[:, :, a:b]

        def weight_dmas(t):
            def tile(w, c, n=P):
                return w[:, c:c + n].rearrange("(k p) c -> p k c", p=P)
            z = t % 2
            if t < T_BR:
                return [(raw_block(z, 8), tile(w_in[0], P * t))]
            if t < T_WO:
                return [(w_raw[:, z, 256 * n:256 * n + 256].rearrange("p (k c) -> p k c", k=2),
                         tile(w[0], P * (t - T_BR)))
                        for n, w in enumerate((sc_out, sb_out, rw_out, sg_out))]
            if t < T_FFN:
                return [(raw_block(z, 8), tile(w_o[0], P * (t - T_WO)))]
            if t < T_IN2:
                kind, a, *half = ffn_block(t)
                if kind == "up":
                    return [(raw_block(z, 8), tile(w_up[0], a))]
                return [(raw_block(z, 2), tile(w_down[0][P * a:P * a + 2 * P], HALF * half[0], HALF))]
            n = t - T_IN2
            if t < T_UQ and n == 19:
                return [(raw_block(z, 8, 32 * r, 32 * r + 32), tile(w_in_2[0], 19 * P, 32))
                        for r in range(4)]
            if t < T_UQ:
                c = P * n if n < 19 else 19 * P + 32 + P * (n - 20)
                return [(raw_block(z, 8), tile(w_in_2[0], c))]
            if t < T_UKV:
                return [(w_raw[:, z, 0:768].rearrange("p (k c) -> p k c", k=2),
                         tile(w_uq_2[0], 4 * DQK * (t - T_UQ), 4 * DQK))]
            if t < T_OUT:
                return [(w_raw[:, z, :], w_ukv_2[0])]
            return [(raw_block(z, 8), tile(w_out_2[0], P * (t - T_OUT)))]

        class Waits:

            def __init__(self, eng, own):
                self.eng, self.own, self.seen = eng, own, {}

            def __call__(self, name, n=1):
                self.seen[name] = self.seen.get(name, 0) + n
                self.eng.wait_ge(s[name], self.seen[name])

            def after(self, ins):
                ins.then_inc(s[self.own], 1)
                self(self.own)

        def bank(b):
            if b < 4:
                return sm[:, b, :]
            return gp[:, (b - 4) // 2, HALF * (b % 2):HALF * (b % 2) + HALF]

        PAIRS = 2 * NB

        def sb_wide(buf, m):
            return buf[:, m % 2, :, 0:P * (m // 2 + 1)]

        def o_place(n):
            c = HALF * (n % 2) + C * (n // 2 % 8)
            return gp[:, 1, c:c + C]

        def at_small(kind, n):
            c = 96 + 4 * kind + n % 4
            return small[:, c:c + 1]

        @block.sync
        def _(sp):
            wait = Waits(sp, None)

            def load_weights(t):
                if t >= 2:
                    sp.wait_ge(s["w_split"], t - 1)
                for dst, src in weight_dmas(t):
                    sp.dma_start(dst, src).then_inc(s[f"w_loaded{t % 2}"], 16)

            wait("prm_clear")
            rows = [("mix_g", mix_norm_g[0]), ("gate_b", gate_b[0]), ("sc_w", sc_conv_w[0]),
                    ("mu", rw_mu[0]), ("w0", rw_w0[0]), ("a0", rw_a0[0]), ("k_k", rw_k_k[0]),
                    ("k_a", rw_k_a[0]), ("r_k", rw_r_k[0]), ("ffn_g", ffn_norm_g[0]),
                    ("fin_g", final_norm_g), ("g2", norm_gain_2[0]), ("q_c", q_c_gain_2[0]),
                    ("kv_c", kv_c_gain_2[0])]
            for name, a in rows:
                if name == "sc_w":
                    src = a.rearrange("w (t p) -> (w t) p", p=P)
                elif name == "r_k":
                    src = a.rearrange("(t h) p -> t (h p)", h=2)
                else:
                    src = a.rearrange("(t p) -> t p", p=P)
                r = ROWS[name]
                sp.dma_start(prm[r:r + src.shape[0], 0, :], src).then_inc(s["prm_in"], 16)
            for name, a, c in (("a_q", a_q_gain_2[0], 0), ("a_q", a_q_gain_2[0], C),
                               ("a_k", a_k_gain_2[0], 0), ("a_k", a_k_gain_2[0], C),
                               ("qn", qn_gain_2[0], 0), ("qn", qr_gain_2[0], C),
                               ("kn", kn_gain_2[0], 0), ("kn", kr_gain_2[0], C)):
                r = ROWS[name]
                sp.dma_start(prm[r:r + 1, 0, c:c + a.shape[0]],
                             a.rearrange("(o p) -> o p", o=1)).then_inc(s["prm_in"], 16)
            sp.dma_start(rel_rows[0:32, :], rel_bias_2).then_inc(s["rel_in"], 16)
            sp.dma_start(freq[:, :], rope_freq).then_inc(s["par_in"], 16)
            taps = ffn_conv_w[0].rearrange("w (t p) -> (w t) p", p=P)
            sp.dma_start(prm[:, 1, :], taps[0:P]).then_inc(s["prm_in"], 16)
            sp.dma_start(prm[0:4, 2, :], taps[P:P + 4]).then_inc(s["prm_in"], 16)
            for n, a in enumerate((sg_ln_g[0], sg_ln_b[0], rw_gn_g[0], rw_gn_b[0])):
                sp.dma_start(row_g[:, n, :], a.partition_broadcast(P)).then_inc(s["par_in"], 16)
            sp.dma_start(lora[0:64, 0, :], rw_w2[0]).then_inc(s["par_in"], 16)
            sp.dma_start(lora[64:128, 0, :], rw_a2[0]).then_inc(s["par_in"], 16)
            sp.dma_start(lora[:, 1, :], rw_g2[0]).then_inc(s["par_in"], 16)
            sp.dma_start(sg_bias[:, :], sg_b[0]).then_inc(s["par_in"], 16)
            sp.dma_start(sg_w_raw[:, :, :], sg_w[0].rearrange("g t s -> t g s")).then_inc(s["par_in"], 16)
            for tt in range(NB):
                sp.dma_start(x_tok[:, tt, :], x[0, P * tt:P * tt + P, :]).then_inc(s[f"x_in{tt // 4}"], 16)
            load_weights(0)
            load_weights(1)
            wait("h_ready", KT)
            sp.dma_start(x_spill, x_t[:, :, :]).then_inc(s["x_out"], 16)
            for t in range(2, T_GATE + 2):
                load_weights(t)
            with sp.Fori(0, 15) as i:
                for z in range(2):
                    sp.wait_ge(s["w_split"], 2 * i + (T_GATE + z + 1))
                    c = i * (2 * P) + P * (T_GATE + 2 + z)
                    sp.dma_start(raw_block(z, 8), w_in[0][:, bass.ds(c, P)]
                                 .rearrange("(k p) c -> p k c", p=P)).then_inc(s[f"w_loaded{z}"], 16)
                    sp.wait_ge(s["gate_ready"], 2 * i + (z + 1))
                    sp.dma_start(gates_spill[bass.ds(2 * i + z, 1)].rearrange("a p t -> p (a t)"),
                                 gate_out[:, z, :]).then_inc(s[f"gate_stored{z}"], 16)
            for z in range(2):
                load_weights(T_BR + z)
                sp.wait_ge(s["gate_ready"], 31 + z)
                sp.dma_start(gates_spill[30 + z], gate_out[:, z, :]).then_inc(s[f"gate_stored{z}"], 16)
            sp.wait_ge(s["y_split"], 8)
            for z in range(2):
                sp.wait_ge(s[f"gate_stored{z}"], 16 * 16)
            for d in range(KT):
                for n in range(4):
                    if d:
                        p = P_BR + 4 * (d - 1) + n
                        sp.wait_ge(s[f"p_free{p % 2}"], frees_before(p) + 1)
                    sp.dma_start(gate_in[:, n, :], gates_spill[8 * n + d]).then_inc(s[f"gate_in{n}"], 16)
                load_weights(T_BR + 2 + d)
            sp.wait_ge(s["p_ready"], P_WO)
            for d in range(KT):
                if d >= 2:
                    p = P_WO + d - 2
                    sp.wait_ge(s[f"p_free{p % 2}"], frees_before(p) + 1)
                sp.dma_start(x_back[:, d % 2, :], x_spill[:, d, :]).then_inc(s[f"x_back{d % 2}"], 16)
                load_weights(T_WO + 2 + d)
            load_weights(T_FFN + 2)
            load_weights(T_FFN + 3)
            with sp.Fori(0, FT // 2 - 1) as i:
                for u in range(6):
                    sp.wait_ge(s["w_split"], 6 * i + (T_FFN + 3 + u))
                    kind, a, *half = ffn_block(T_FFN + 4 + u)
                    if kind == "up":
                        dst, src = raw_block(u % 2, 8), w_up[0][:, bass.ds(2 * P * i + a, P)]
                    else:
                        c = HALF * half[0]
                        dst, src = raw_block(u % 2, 2), w_down[0][bass.ds(2 * P * i + P * a, 2 * P), c:c + HALF]
                    sp.dma_start(dst, src.rearrange("(k p) c -> p k c", p=P)).then_inc(s[f"w_loaded{u % 2}"], 16)
            for t in range(T_IN2 - 2, T_IN2 + 2):
                load_weights(t)
            sp.wait_ge(s["h_ready"], 3 * KT)
            sp.dma_start(x_spill, x_mid[:, :, :]).then_inc(s["x_out"], 16)
            for t in range(T_IN2 + 2, T_UKV + 1):
                load_weights(t)
            sp.wait_ge(s["p_ready"], P_UQ)
            sp.dma_start(buckets[:, :], bucket_table).then_inc(s["rel_in"], 16)
            sp.wait_ge(s["bias_rows"], 1)
            sp.dma_start(bias_spill, bias_vec[:, :].unsqueeze(1).to_broadcast([HEADS_A, P, 1152])).then_inc(s["bias_out"], 16)
            sp.wait_ge(s["bias_out"], 16)
            for h in range(HEADS_A):
                if h >= 2:
                    sp.wait_ge(s["at_s"], NB * (h - 1))
                skew = bass.AP(tensor=bias_spill.tensor, offset=1152 * P * h + 127, ap=[[1151, P], [1, T]])
                sp.dma_start(table[:, h % 2, :], skew).then_inc(s[f"table_in{h % 2}"], 16)
            sp.wait_ge(s["q_split"], 2)
            sp.wait_ge(s["kv_split"], 1)
            sp.dma_start(pos_i[C:C + 32, :], positions_2[0].partition_broadcast(32)).then_inc(s["pos_in"], 16)
            load_weights(T_OUT)
            load_weights(T_OUT + 1)
            for d in range(KT):
                if d == 0:
                    sp.wait_ge(s["at_pt_copied"], 2 * UNITS)
                else:
                    wait("out_taken")
                if d >= 2:
                    p = P_OUT + d - 2
                    sp.wait_ge(s[f"p_free{p % 2}"], frees_before(p) + 1)
                if d + 2 < KT:
                    load_weights(T_OUT + 2 + d)
                sp.dma_start(x_back2[:, d % 2, :], x_spill[:, d, :]).then_inc(s[f"x_back{d % 2}"], 16)
                if d:
                    sp.dma_start(out[0][:, P * (d - 1):P * d].rearrange("(n p) c -> p n c", p=P),
                                 out_tok[:, (d - 1) % 2]).then_inc(s[f"stored{(d - 1) % 2}"], 16)
            wait("out_taken")
            d = KT
            sp.dma_start(out[0][:, P * (d - 1):P * d].rearrange("(n p) c -> p n c", p=P),
                         out_tok[:, (d - 1) % 2]).then_inc(s[f"stored{(d - 1) % 2}"], 16)
            for z in range(2):
                sp.wait_ge(s[f"stored{z}"], 16 * KT // 2)

        @block.gpsimd
        def _(pool):
            wait = Waits(pool, "pool_own")

            def select(view, pattern, base, mult, compare=ALU.is_ge, fill=0.0):
                wait.after(pool.affine_select(out=view, in_=view, pattern=pattern, compare_op=compare,
                                              fill=fill, base=base, channel_multiplier=mult))

            wait.after(pool.memset(rel_rows[:, :], 1.0))
            pool.memset(prm[:, :, :], 0.0).then_inc(s["prm_clear"], 1)
            wait.after(pool.memset(ident[:, :], 0.0))
            select(ident[:, :], [[-1, P]], 0, 1, ALU.not_equal, 1.0)
            wait.after(pool.memset(ones[:, :], 1.0))
            wait.after(pool.memset(ones_row[:, :], 1.0))
            wait.after(pool.memset(head_ones[:, :], 1.0))
            select(head_ones[:, 0:C], [[0, C]], C - 1, -1)
            select(head_ones[:, C:P], [[0, C]], -C, 1)
            for m, off in ((mask_s, -1), (mask_i, 0)):
                wait.after(pool.tensor_copy(m[:, :], head_ones[:, :]))
                select(m[:, :], [[1, P]], off, -1)
            for n, m in enumerate(level):
                b = 2 ** n
                wait.after(pool.memset(m[:, :], 0.0))
                view = m[:, :].rearrange("p (k h c) -> p k h c", h=2, c=b)[:, :, 1, :]
                wait.after(pool.memset(view, 1.0))
                select(view, [[-2 * b, P // (2 * b)], [0, b]], 0, 1)
                select(view, [[2 * b, P // (2 * b)], [0, b]], b - 1, -1)
            wait.after(pool.memset(level0_t[:, :], 0.0))
            view = level0_t[:, :].rearrange("p (k h) -> p k h", h=2)[:, :, 0]
            wait.after(pool.memset(view, 1.0))
            select(view, [[-2, P // 2]], -1, 1, ALU.is_equal)
            wait.after(pool.memset(group_sel[:, :, :], 1.0))
            select(group_sel[:, :, :], [[P, 2], [1, P]], 0, -C)
            select(group_sel[:, :, :], [[-P, 2], [-1, P]], C - 1, C)
            wait.after(pool.memset(rope_turn[:, :], 0.0))
            select(rope_turn[:, :], [[-1, 32]], 16 - C, 1, ALU.not_equal, 1.0)
            select(rope_turn[:, :], [[-1, 32]], -16 - C, 1, ALU.not_equal, -1.0)
            pool.drain().then_inc(s["consts"], 1)

            wait("wsg_copied")
            pool.affine_select(out=w_sg[:, :, :], in_=w_sg[:, :, :], pattern=[[0, 4], [1, P]],
                               compare_op=ALU.is_ge, fill=0.0, base=0,
                               channel_multiplier=-1).then_inc(s["wsg_ready"], 1)

            def sb_cut(m, signal):
                wait(signal)
                qb = m // 2
                diag = sb_sp[:, m % 2, :, P * qb:P * qb + P]
                pool.affine_select(out=diag, in_=diag, pattern=[[0, 2], [-1, P]], compare_op=ALU.is_gt,
                                   fill=0.0, base=0, channel_multiplier=1).then_inc(s[signal + "_cut"], 1)

            sb_cut(0, "sb_sp")
            for m in range(PAIRS):
                if m + 1 < PAIRS:
                    sb_cut(m + 1, "sb_sp")
                sb_cut(m, "sb_p")

            for rnd in range(2 * 2):
                for n in range(1, 6):
                    for hh in range(2):
                        if n == 1:
                            wait("rk_m")
                        else:
                            wait("rk_p")
                        pool.tensor_tensor(m_lv[:, hh], m_t[:, hh],
                                           level[n][:, :].unsqueeze(1).to_broadcast([P, 4, P]),
                                           ALU.mult).then_inc(s["rk_lv"], 1)
                for hh in range(2):
                    wait("rk_p")
            for q in range(4 * KT):
                d, n = divmod(q, 4)
                if n == 0:
                    continue
                p = P_BR + q
                pool.wait_ge(s[f"p_free{p % 2}"], frees_before(p) + 1)
                if n == 1:
                    pool.wait_ge(s[f"p_free{(p - 1) % 2}"], frees_before(p - 1) + 1)
                else:
                    pool.wait_ge(s["merge_add"], merge_adds(q - 1))
                pool.tensor_tensor(merged[:, d % 2, :], merged[:, d % 2, :], gated[:, q % 2, :], ALU.add) \
                    .then_inc(s["merge_add"], 1)
            pool.wait_ge(s["at_pt_copied"], UNITS)
            wait.after(pool.memset(mla_ones[:, :], 1.0 / C))
            select(mla_ones[:, 0:C], [[0, C]], C - 1, -1)
            wait.after(pool.memset(mla_ones[:, C:DQK], 1.0 / 32))
            pool.affine_select(out=mla_ones[:, C:DQK], in_=mla_ones[:, C:DQK], pattern=[[0, 32]],
                               compare_op=ALU.is_ge, fill=0.0, base=-C,
                               channel_multiplier=1).then_inc(s["mla_ones"], 1)
            pool.wait_ge(s["p_ready"], P_OUT)
            wait.after(pool.memset(causal[:, :], 0.0))
            pool.affine_select(out=causal[:, :], in_=causal[:, :], pattern=[[-1, T]], compare_op=ALU.is_ge,
                               fill=NEG, base=T - P, channel_multiplier=1).then_inc(s["causal"], 1)

        @block.tensor
        def _(pe):
            wait = Waits(pe, None)

            def product(p, weights, rows, hi, lo, k0=0, split=None):
                n = len(weights)
                for half in range(2):
                    c = slice(HALF * half, HALF * half + HALF)
                    o = gp[0:rows, p % 2, c]
                    for k, (wh, wl) in enumerate(weights):
                        if split and half == 0:
                            wait(split)
                        pe.matmul(o, wh, hi[:, k0 + k, c], start=(k == 0), stop=False)
                        pe.matmul(o, wh, lo[:, k0 + k, c], start=False, stop=False)
                        mm = pe.matmul(o, wl, hi[:, k0 + k, c], start=False, stop=(k == n - 1))
                return mm

            def ring(t, a, b):
                return w_hi[:, t % 2, a:b], w_lo[:, t % 2, a:b]

            def whole(t, p, hi, lo, split=None):
                pe.wait_ge(s["w_split"], t + 1)
                if p >= 2:
                    pe.wait_ge(s[f"p_free{p % 2}"], frees_before(p))
                product(p, [ring(t, P * k, P * k + P) for k in range(8)], P, hi, lo, split=split) \
                    .then_inc(s["p_ready"], 1)

            def norm(n):
                for k in range(KT):
                    wait("square")
                    for half in range(2):
                        mm = pe.matmul(sm[:, half, :], ones[:, :], squares[:, k % 2, HALF * half:HALF * half + HALF],
                                       start=(k == 0), stop=(k == KT - 1), skip_group_check=True)
                    mm.then_inc(s["square_used"], 1)

            wait("consts")
            pe.wait_ge(s["prm_in"], 16 * PRM_DMAS)
            for n in range(3):
                r = P if n < 2 else 4
                mm = pe.transpose(sm[:, 0, P * n:P * n + r], prm[0:r, n, :], ident[0:r, 0:r])
            mm.then_inc(s["col_t"], 1)
            pe.wait_ge(s["par_in"], 16 * PAR_DMAS)
            for g in range(4):
                mm = pe.transpose(sm[:, 1, P * g:P * g + P], sg_w_raw[:, g, :], ident[:, :])
            mm.then_inc(s["wsg_t"], 1)
            wait("wsg_copied")
            wait("cols")
            for b in range(16):
                half, k = divmod(b, 8)
                if k == 0:
                    pe.wait_ge(s[f"x_in{half}"], 64)
                if b >= 4:
                    wait(f"x_turned{b % 2}")
                for n in range(4):
                    mm = pe.transpose(sm[:, b % 4, P * n:P * n + P],
                                      x_tok[:, 4 * half + n, P * k:P * k + P], ident[:, :])
                mm.then_inc(s["x_t"], 1)
            for b in range(4):
                wait(f"x_turned{b % 2}")
            norm(0)
            for t in range(T_GATE):
                whole(t, t, h_hi, h_lo, "h_split" if t == 0 else None)
                if t == 13:
                    for b in range(4):
                        ft, half = divmod(b, 2)
                        for n in range(4):
                            mm = pe.transpose(sm[:, b, P * n:P * n + P],
                                              vt_sb[:, ft, P * (4 * half + n):P * (4 * half + n) + P], ident[:, :])
                        mm.then_inc(s["v_turned"], 1)
            for z in range(2):
                pe.wait_ge(s[f"p_free{z}"], P_GATE // 2)
            wait("v_taken", 4)
            for b in range(4):
                ft, half = divmod(b, 2)
                for n in range(4):
                    mm = pe.transpose(sm[:, b, P * n:P * n + P],
                                      vt_sg[:, ft, P * (4 * half + n):P * (4 * half + n) + P], ident[:, :])
                mm.then_inc(s["v_turned"], 1)
            wait("sg_normed")
            wait("wsg_ready")
            for b in range(4):
                ft, half = divmod(b, 2)
                for n in range(4):
                    tt = 4 * half + n
                    c = slice(P * n, P * n + P)
                    pe.matmul(sm[:, b, c], group_sel[:, ft, :], sg_bias[:, :], start=True, stop=False,
                              skip_group_check=True)
                    for hh in range(2):
                        g = 2 * ft + hh
                        mm = pe.matmul(sm[C * hh:C * hh + C, b, c], v_sg[:, tt, C * g:C * g + C], w_sg[:, g, :],
                                       start=False, stop=True, skip_group_check=True)
                mm.then_inc(s["sg_mixed"], 1)
            for z in range(2):
                pe.wait_ge(s["w_split"], T_GATE + z + 1)
                product(z, [ring(z, P * k, P * k + P) for k in range(8)], P, h_hi, h_lo) \
                    .then_inc(s["p_ready"], 1)
            with pe.Fori(1, 16) as i:
                for z in range(2):
                    pe.wait_ge(s["w_split"], 2 * i + (T_GATE + z + 1))
                    pe.wait_ge(s["gate_ready"], 2 * i + (z - 1))
                    product(z, [ring(z, P * k, P * k + P) for k in range(8)], P, h_hi, h_lo) \
                        .then_inc(s["p_ready"], 1)
            wait("sg_done", 4)
            pe.wait_ge(s["gate_ready"], 32)

            def sb_scores(m):
                qb, ft = divmod(m, 2)
                if m >= 1:
                    wait("sb_zc")
                w = P * (qb + 1)
                for hh in range(2):
                    for a in range(0, w, HALF):
                        n = min(HALF, w - a)
                        mm = pe.matmul(sm[:, 2 * hh + a // HALF, 0:n],
                                       q_sb[C * hh:C * hh + C, ft, P * qb:P * qb + P],
                                       k_sb[C * hh:C * hh + C, ft, a:a + n], start=True, stop=True)
                mm.then_inc(s["sb_z"], 1)

            def sb_values(n):
                qb = n // 4
                if n >= 1:
                    wait("sb_pt_copied")
                if n % 2 == 0:
                    wait("sb_p_cut")
                for k in range(qb + 1):
                    mm = pe.transpose(gp[:, 0, P * k:P * k + P],
                                      sb_sp[:, n // 2 % 2, n % 2, P * k:P * k + P], ident[:, :])
                mm.then_inc(s["sb_pt"], 1)

            def sb_output(n):
                qb, h = divmod(n, 4)
                for k in range(qb + 1):
                    mm = pe.matmul(gp[:, 1, C * h:C * h + C], sb_pt[:, n % 2, P * k:P * k + P],
                                   v_sb[:, k, C * h:C * h + C], start=(k == 0), stop=(k == qb),
                                   skip_group_check=True)
                if h == 3:
                    mm.then_inc(s["sb_o"], 1)

            def sb_turn(qb):
                wait("sb_o_copied")
                if qb >= 1:
                    wait("sb_y_free")
                for ft in range(2):
                    mm = pe.transpose(gp[:, 1, HALF + P * ft:HALF + P * ft + P],
                                      sb_o[:, qb % 2, P * ft:P * ft + P], ident[:, :])
                mm.then_inc(s["sb_y"], 1)

            sb_scores(0)
            for m in range(PAIRS + 1):
                if m + 1 < PAIRS:
                    sb_scores(m + 1)
                if m >= 1:
                    for n in (2 * m - 2, 2 * m - 1):
                        sb_values(n)
                        if n % 4 == 1 and n > 4:
                            sb_turn(n // 4 - 1)
                        if n >= 1:
                            sb_output(n - 1)
            wait("sb_pt_copied")
            sb_output(4 * NB - 1)
            sb_turn(NB - 1)
            wait("sb_y_free")

            for ft in range(2):
                wait("rk_lora")
                if ft:
                    wait("rk_g_free")
                for half in range(2):
                    c = slice(HALF * half, HALF * half + HALF)
                    pe.matmul(gp[:, 0, c], lora[0:C, 0, P * ft:P * ft + P], rk_th[0:C, c], start=True, stop=True)
                    mm = pe.matmul(gp[:, 1, c], lora[C:P, 0, P * ft:P * ft + P], zr[C:P, 6, c], start=True, stop=True)
                mm.then_inc(s["rk_lora_p"], 1)
                wait("rk_kk2")
                for half in range(2):
                    mm = pe.matmul(sm[:, half, :], head_ones[:, :], rk_e[:, HALF * half:HALF * half + HALF],
                                   start=True, stop=True)
                mm.then_inc(s["rk_lora_p"], 1)
                wait("rk_bonus")
                for tt in range(NB):
                    mm = pe.matmul(sm[:, 2, 2 * tt:2 * tt + 2], rk_e[:, P * tt:P * tt + P],
                                   head_ones[:, 0:P:C], start=True, stop=True)
                mm.then_inc(s["rk_bonus_p"], 1)
                wait("rk_bonus_taken")
                wait("rk_prep")
                for b in range(8):
                    src = (rk_a, rk_e, rk_f, zr)[b // 2]
                    for n in range(4):
                        c = slice(P * (4 * (b % 2) + n), P * (4 * (b % 2) + n) + P)
                        mm = pe.transpose(bank(b)[:, P * n:P * n + P],
                                          zr[:, 4 + ft, c] if b >= 6 else src[:, c], ident[:, :])
                    mm.then_inc(s["rk_tok_t"], 1)
                for b in range(8):
                    wait(f"rk_tok{b % 2}")
                for g in range(2):
                    for hh in range(2):
                        rows = slice(C * hh, C * hh + C)
                        for dst, lhs, rhs in ((2 * hh, rk_b, rk_a), (2 * hh + 1, rk_a, rk_b),
                                              (4 + 2 * hh, "k", rk_a), (5 + 2 * hh, rk_b, "r")):
                            for n in range(4):
                                c = slice(P * (4 * g + n), P * (4 * g + n) + P)
                                l = zr[rows, 2 + ft, c] if lhs == "k" else lhs[rows, c]
                                r = zr[rows, ft, c] if rhs == "r" else rhs[rows, c]
                                mm = pe.matmul(bank(dst)[:, P * n:P * n + P], l, r, start=True, stop=True)
                            mm.then_inc(s["rk_mats"], 1)
                    for hh in range(2):
                        rows = slice(C * hh, C * hh + C)
                        wait("rk_m")
                        for n in range(4):
                            c = slice(P * (4 * g + n), P * (4 * g + n) + P)
                            mm = pe.matmul(bank(2 * hh)[:, P * n:P * n + P], zr[rows, 2 + ft, c],
                                           zr[rows, ft, c], start=True, stop=True)
                        mm.then_inc(s["rk_mats"], 1)
                    wait("rk_mats_done", 2)
                    for n in range(1, 6):
                        for hh in range(2):
                            wait("rk_lv")
                            if n > 1:
                                wait("rk_x_added")
                            for u in range(4):
                                mm = pe.matmul(bank(2 * hh)[:, P * u:P * u + P], m_lv[:, hh, u, :],
                                               inv[:, hh, u, :], start=True, stop=True)
                            mm.then_inc(s["rk_p"], 1)
                        for hh in range(2):
                            wait("rk_copied")
                            for u in range(4):
                                if n < 5:
                                    pe.matmul(bank(2 * hh + 1)[:, P * u:P * u + P], inv_t[:, hh, u, :],
                                              m_p[:, hh, u, :], start=True, stop=True)
                                mm = pe.matmul(bank(4 + 2 * hh)[:, P * u:P * u + P], m_p[:, hh, u, :],
                                               inv_t[:, hh, u, :], start=True, stop=True)
                            mm.then_inc(s["rk_x"], 1)
                    wait("rk_x_added", 2)
                    for hh in range(2):
                        cols = slice(C * hh, C * hh + C)
                        for u in range(4):
                            mm = pe.matmul(bank(2 * hh)[:, C * u:C * u + C], n_t[:, hh, u, :],
                                           v_tok[:, 4 * g + u, cols], start=True, stop=True)
                            mm = pe.matmul(bank(2 * hh)[:, BW + C * u:BW + C * u + C], rk_t[:, hh, u, :],
                                           v_tok[:, 4 * g + u, cols], start=True, stop=True)
                        mm.then_inc(s["rk_nv"], 1)
                        for u in range(4):
                            mm = pe.matmul(bank(5 + 2 * hh)[C * hh:C * hh + C, P * u:P * u + P],
                                           a_tok[:, 4 * g + u, cols], inv_t[:, hh, u, :], start=True, stop=True)
                        mm.then_inc(s["rk_nv"], 1)
                    for hh in range(2):
                        wait("rk_copied")
                        for u in range(4):
                            mm = pe.matmul(bank(2 * hh + 1)[:, C * u:C * u + C], inv_t[:, hh, u, :],
                                           nv[:, hh, u, :], start=True, stop=True)
                        mm.then_inc(s["rk_xnv"], 1)
                    wait("rk_round", 2)
                    wait("rk_round_act", 2)
                for ch in range(NCH):
                    tt, pb = ch // 2, C * (ch % 2)
                    toks = slice(pb, pb + C)
                    wait("rk_state")
                    for hh in range(2):
                        rows = slice(C * hh, C * hh + C)
                        mm = pe.matmul(bank(4 + hh)[toks, 0:C], xa_t[rows, P * tt + pb:P * tt + pb + C],
                                       s_all[rows, ch, :], start=True, stop=True)
                    mm.then_inc(s["rk_chain"], 1)
                    for hh in range(2):
                        cols = slice(C * hh, C * hh + C)
                        pe.matmul(bank(6)[C * hh:C * hh + C, 0:C], k_tok[toks, tt, cols], v_tok[toks, tt, cols],
                                  start=True, stop=False, skip_group_check=True)
                    wait("rk_u_added")
                    for hh in range(2):
                        cols = slice(C * hh, C * hh + C)
                        mm = pe.matmul(bank(6)[C * hh:C * hh + C, 0:C], b_tok[toks, tt, cols], u_tok[toks, tt, cols],
                                       start=False, stop=True, skip_group_check=True)
                    mm.then_inc(s["rk_chain"], 1)
                wait("rk_state")
                for g in range(2):
                    for hh in range(2):
                        cols, rows = slice(C * hh, C * hh + C), slice(C * hh, C * hh + C)
                        for u in range(4):
                            tt = 4 * g + u
                            pe.matmul(bank(2 * g + hh)[:, C * u:C * u + C], rb_t[:, hh, tt, :],
                                      u_tok[:, tt, cols], start=True, stop=False, skip_group_check=True)
                            for q in range(2):
                                mm = pe.matmul(bank(2 * g + hh)[C * q:C * q + C, C * u:C * u + C],
                                               zr[rows, ft, P * tt + C * q:P * tt + C * q + C],
                                               s_all[rows, 2 * tt + q, :], start=False, stop=True,
                                               skip_group_check=True)
                    mm.then_inc(s["rk_y"], 1)
                for b in range(2):
                    for u in range(4):
                        c = slice(P * (4 * b + u), P * (4 * b + u) + P)
                        mm = pe.matmul(bank(4 + b)[:, P * u:P * u + P], rk_sg[:, c],
                                       lora[:, 1, P * ft:P * ft + P], start=True, stop=True)
                    mm.then_inc(s["rk_y"], 1)
                wait("rk_y_ready")
                for b in range(2):
                    for u in range(4):
                        mm = pe.transpose(bank(6 + b)[:, P * u:P * u + P], y_tok[:, 4 * b + u, :], ident[:, :])
                    mm.then_inc(s["rk_y_t"], 1)

            for d in range(KT):
                t = T_BR + d
                pe.wait_ge(s["w_split"], t + 1)
                for n in range(4):
                    p = P_BR + 4 * d + n
                    pe.wait_ge(s[f"p_free{p % 2}"], frees_before(p))
                    product(p, [ring(t, 256 * n + P * k, 256 * n + P * k + P) for k in range(2)], P,
                            y_hi, y_lo, 2 * n, "y_split" if d == 0 else None).then_inc(s["p_ready"], 1)
            for d in range(KT):
                whole(T_WO + d, P_WO + d, m_hi, m_lo, "m_split" if d == 0 else None)
            norm(1)
            for n in range(4):
                whole(T_FFN + n, P_FFN + n, h_hi, h_lo, "h_split" if n == 0 else None)

            def up(i, u, q):
                pe.wait_ge(s["w_split"], 6 * i + (T_FFN + 5 + u))
                pe.wait_ge(s[f"p_free{q % 2}"], 6 * i + frees_before(P_FFN + 4 + q))
                product(q, [ring(u, P * k, P * k + P) for k in range(8)], P, h_hi, h_lo) \
                    .then_inc(s["p_ready"], 1)

            def down(i, u, q):
                pe.wait_ge(s["w_split"], 6 * i + (T_FFN + 5 + u))
                for j in range(4):
                    pe.wait_ge(s[f"p_free{(q + j) % 2}"], 6 * i + frees_before(P_FFN + 4 + q + j))
                    product(q + j, [ring(u, HALF * k + P * j, HALF * k + P * j + P) for k in range(2)], P,
                            g_hi, g_lo).then_inc(s["p_ready"], 1)

            with pe.Fori(0, FT // 2 - 1) as i:
                up(i, 0, 0)
                pe.wait_ge(s["g_split"], 2 * i + 2)
                down(i, 1, 1)
                down(i, 2, 5)
                for u in range(3, 6):
                    up(i, u, 6 + u)
            pe.wait_ge(s["g_split"], FT)
            for u in range(2):
                down(FT // 2 - 1, u, 4 * u)
            norm(2)
            norm(3)
            wait("h_split", KT)
            for t in range(T_IN2, T_UQ):
                whole(t, P_IN2 + t - T_IN2, h_hi, h_lo)
                if t - T_IN2 == 13:
                    for b in range(8):
                        ft, half = divmod(b, 2)
                        if b >= 4:
                            wait("v_taken")
                        for n in range(4):
                            c = P * (4 * half + n)
                            mm = pe.transpose(sm[:, b % 4, P * n:P * n + P], vt_2[:, ft, c:c + P], ident[:, :])
                        mm.then_inc(s["v_turned"], 1)
            wait("v_taken", 4)
            for z in range(2):
                pe.wait_ge(s[f"p_free{z}"], frees_before(P_UQ))
            pe.wait_ge(s["rel_in"], 32)
            for n in range(3):
                mm = pe.matmul(sm[0:HEADS_A, n, 0:384], rel_rows[0:33, :], buckets[0:33, 384 * n:384 * n + 384],
                               start=True, stop=True)
            mm.then_inc(s["bias_p"], 1)
            wait("bias_rows")
            for j in range(8):
                wait("n2_sq")
                for half in range(2):
                    mm = pe.matmul(sm[:, 2 * (j % 2) + half, :], head_ones[:, :],
                                   nsq[:, j % 2, HALF * half:HALF * half + HALF], start=True, stop=True)
                mm.then_inc(s["n2_ss"], 1)
            wait("n2_q", 8)

            def attention(block, scores, v, column):
                def z(n):
                    if n >= 2:
                        wait("at_s")
                    w = P * (block(n) + 1)
                    for a in range(0, w, HALF):
                        m = min(HALF, w - a)
                        mm = scores(n, sm[:, 2 * (n % 2) + a // HALF, 0:m], a, m)
                    mm.then_inc(s["at_z"], 1)

                def output(n):
                    if n >= 2:
                        wait("at_o_taken")
                    qb = block(n)
                    for k in range(qb + 1):
                        mm = pe.matmul(o_place(n), att_pt[:, n % 2, P * k:P * k + P],
                                       v[:, k, column(n):column(n) + C], start=(k == 0), stop=(k == qb),
                                       skip_group_check=True)
                    mm.then_inc(s["at_o"], 1)

                z(0)
                z(1)
                for n in range(UNITS):
                    if n >= 1:
                        wait("at_pt_copied")
                    wait("at_p")
                    for k in range(block(n) + 1):
                        mm = pe.transpose(gp[:, 0, P * k:P * k + P], att_s[:, n % 2, P * k:P * k + P], ident[:, :])
                    mm.then_inc(s["at_pt"], 1)
                    if n + 2 < UNITS:
                        z(n + 2)
                    if n >= 1:
                        output(n - 1)
                wait("at_pt_copied")
                output(UNITS - 1)
                wait("at_s", 2)
                wait("at_o_taken", 2)

            def turn_outputs(o):
                for qb in range(NB):
                    if qb >= 4:
                        wait("z_done")
                    for ft in range(4):
                        mm = pe.transpose(sm[:, qb % 4, P * ft:P * ft + P], o[:, qb, P * ft:P * ft + P], ident[:, :])
                    mm.then_inc(s["z_turned"], 1)
                wait("z_done", 4)

            def scores_a(n, o, a, m):
                h, qb = divmod(n, NB)
                rows = slice(C * (h % 2), C * (h % 2) + C)
                return pe.matmul(o, q_2[rows, h // 2, P * qb:P * qb + P], k_2[rows, h // 2, a:a + m],
                                 start=True, stop=True)

            attention(lambda n: n % NB, scores_a, v_2, lambda n: C * (n // NB))
            turn_outputs(o_all)

            for j in range(3):
                wait("c_sq")
                for half in range(2):
                    c = slice(HALF * half, HALF * half + HALF)
                    mm = pe.matmul(sm[:, (0, 0, 2)[j] + half, :], ones[:, :], nsq[:, j % 2, c],
                                   start=(j != 1), stop=(j != 0), skip_group_check=True)
                mm.then_inc(s["c_ss"], 1)
            wait("c_sq")
            wait("c_root", 2)
            for half in range(2):
                c = slice(HALF * half, HALF * half + HALF)
                mm = pe.matmul(sm[C:C + 32, half, :], ones[C:C + 32, 0:32], nsq[C:C + 32, 1, c], start=True, stop=True)
            mm.then_inc(s["c_ss"], 1)

            def turn_rope(view, place):
                for half in range(2):
                    c = slice(HALF * half, HALF * half + HALF)
                    mm = pe.matmul(place[C:C + 32, c], rope_turn[C:C + 32, :], view[:, c],
                                   start=True, stop=True)
                mm.then_inc(s["rot"], 1)

            wait("krope_normed")
            turn_rope(k_rope[C:C + 32, :], sm[:, 2:4, :].rearrange("p a b -> p (a b)"))
            wait("q_split", 2)
            for h in range(HEADS_B):
                t, p = T_UQ + h // 4, P_UQ + h
                pe.wait_ge(s["w_split"], t + 1)
                pe.wait_ge(s[f"p_free{p % 2}"], frees_before(p))
                product(p, [ring(t, 384 * k + DQK * (h % 4), 384 * k + DQK * (h % 4) + DQK) for k in range(2)],
                        DQK, cq_hi, cq_lo).then_inc(s["p_ready"], 1)
            wait("mla_ones")

            def head_norm(rows, h, place):
                wait("hn_sq")
                for half in range(2):
                    c = slice(HALF * half, HALF * half + HALF)
                    mm = pe.matmul(sm[0:rows, place + half, :], mla_ones[0:rows, 0:rows], nsq_b[0:rows, h % 2, c],
                                   start=True, stop=True)
                mm.then_inc(s["hn_ss"], 1)

            for z in range(2):
                pe.wait_ge(s[f"p_free{z}"], frees_before(P_UKV))
            wait("rot_used")
            for h in range(HEADS_B + 1):
                if h < HEADS_B:
                    if h >= 2:
                        pe.wait_ge(s["hn_rt"], 2 + h - 1)
                    head_norm(DQK, h, 2 * (h % 2))
                if h:
                    wait("hn_done")
                    if h >= 3:
                        wait("rot_used")
                    turn_rope(qh[C:DQK, h - 1, :], gp[:, (h - 1) % 2, :])
            wait("rot_used", 2)
            wait("kv_split")
            pe.wait_ge(s["w_split"], T_UKV + 1)
            pe.wait_ge(s["hn_rt"], 2 + HEADS_B)

            def head_kv(h):
                p = P_UKV + h
                pe.wait_ge(s[f"p_free{p % 2}"], frees_before(p))
                product(p, [ring(T_UKV, P * h, P * h + P)], P, ckv_hi, ckv_lo).then_inc(s["p_ready"], 1)

            head_kv(0)
            for h in range(HEADS_B):
                if h < HEADS_B - 1:
                    head_kv(h + 1)
                p = P_UKV + h
                pe.wait_ge(s[f"p_free{p % 2}"], frees_before(p) + 1)
                if h >= 2:
                    wait("vb_taken")
                for n in range(NB):
                    mm = pe.transpose(sm[:, 2 + h % 2, C * n:C * n + C], vb_t[C:P, P * n:P * n + P], ident[C:P, C:P])
                mm.then_inc(s["vb_turned"], 1)
                if h:
                    pe.wait_ge(s["hn_rt"], 2 + HEADS_B + h)
                head_norm(C, h, 0)
            wait("hn_done", HEADS_B)
            wait("vb_taken", 2)
            for z in range(2):
                pe.wait_ge(s[f"p_free{z}"], frees_before(P_OUT))
            wait("k_rope_spread")

            def scores_b(n, o, a, m):
                qb, h = divmod(n, HEADS_B)
                return pe.matmul(o, qh[:, h, P * qb:P * qb + P], kh[:, h, a:a + m], start=True, stop=True)

            attention(lambda n: n // 8, scores_b, v_b, lambda n: C * (n % 8))
            turn_outputs(o_b)

            def turn_out(d):
                p = P_OUT + d
                pe.wait_ge(s[f"p_free{p % 2}"], frees_before(p) + 1)
                if d >= 2:
                    wait("out_taken")
                for n in range(NB):
                    mm = pe.transpose(sm[:, 2 * (d % 2) + n // 4, P * (n % 4):P * (n % 4) + P],
                                      x_out[:, d % 2, P * n:P * n + P], ident[:, :])
                mm.then_inc(s["out_t"], 1)

            for d in range(KT):
                whole(T_OUT + d, P_OUT + d, mix_hi, mix_lo, "mix_split" if d == 0 else None)
                if d:
                    turn_out(d - 1)
            turn_out(KT - 1)

        @block.scalar
        def _(act):
            wait = Waits(act, "act_own")

            def split_weights(t):
                act.wait_ge(s[f"w_loaded{t % 2}"], loaded_value(t))
                if t >= 2:
                    act.wait_ge(s["p_ready"], outs_through(t - 2))
                n = block_columns(t)
                act.copy(w_hi[:, t % 2, 0:n], w_raw[:, t % 2, 0:n]).then_inc(s["w_high"], 1)

            def logs_and_exps():
                act.preload_act_table_set("natural_log_exp_and_others")

            def norm(n, src, ready=None):
                logs_and_exps()
                for k in range(KT):
                    if ready:
                        wait(ready)
                    if n * KT + k >= 2:
                        act.wait_ge(s["square_used"], n * KT + k - 1)
                    act.activation(squares[:, k % 2, :], src[:, k, :], ACT.Square).then_inc(s["square"], 1)
                act.wait_ge(s["square_used"], KT * (n + 1))
                wait.after(act.activation(root[:, :], sm[:, 0:2, :].rearrange("p a b -> p (a b)"), ACT.Ln,
                                          bias=RMS_EPS, scale=1.0 / D))
                act.activation(rstd[:, :], root[:, :], ACT.Exp, scale=-0.5).then_inc(s["root"], 1)

            def split_h():
                for k in range(KT):
                    wait("h_ready")
                    act.copy(h_hi[:, k, :], h_tmp[:, k % 2, :]).then_inc(s["high"], 1)

            for b in range(0, 16, 2):
                act.wait_ge(s["x_t"], b + 1)
                half, k = divmod(b, 8)
                act.copy(x_t[:, k, HALF * half:HALF * half + HALF], sm[:, b % 4, :]).then_inc(s["x_turned0"], 1)
            act.wait_ge(s["x_turned1"], 8)
            act.wait_ge(s["x_turned0"], 8)
            split_weights(0)
            norm(0, x_t)
            split_h()
            for t in range(T_GATE):
                split_weights(t + 1)
                if t in (4, 5):
                    continue
                act.wait_ge(s["p_ready"], t + 1)
                ps = gp[:, t % 2, :]
                done = s[f"p_free{t % 2}"]
                if t < 2:
                    act.copy(y_a[:, t, :], ps).then_inc(done, 1)
                elif t < 4:
                    act.copy(sc_c[:, t - 2, :], ps).then_inc(done, 1)
                elif t < 8:
                    act.mul(q_sb[:, t - 6, :], ps, 0.125).then_inc(done, 1)
                elif t < 10:
                    act.copy(k_sb[:, t - 8, :], ps).then_inc(done, 1)
                elif t < 12:
                    if t == 10:
                        wait("sc_done")
                    act.copy(vt_sb[:, t - 10, :], ps).then_inc(done, 1)
                elif t < 20:
                    if t == 12:
                        act.wait_ge(s["x_out"], 16)
                    act.copy(zr[:, t - 12, :], ps).then_inc(done, 1)
                else:
                    dst = y_d[:, t - 20, :] if t < 22 else vt_sg[:, t - 22, :]
                    act.activation(dst, ps, ACT.Gelu_apprx_tanh).then_inc(done, 1)
            wait("sg_var")
            act.activation(small[:, 16:24], small[:, 8:16], ACT.Sqrt, bias=LN_EPS).then_inc(s["sg_root"], 1)
            def gate(i, z, stored=True):
                act.wait_ge(s["p_ready"], 2 * i + (T_GATE + z + 1))
                if stored:
                    act.wait_ge(s[f"gate_stored{z}"], 16 * i)
                act.activation(gate_out[:, z, :], gp[:, z, :], ACT.Sigmoid,
                               bias=col[:, bass.ds(2 * i + (ROWS["gate_b"] + z), 1)]) \
                    .then_inc(s["gate_ready"], 1)

            for z in range(2):
                split_weights(T_GATE + z + 1)
                gate(0, z, stored=False)
            with act.Fori(1, 15) as i:
                for z in range(2):
                    act.wait_ge(s[f"w_loaded{1 - z}"], 16 * i + loaded_value(T_GATE + z + 1))
                    act.wait_ge(s["p_ready"], 2 * i + (T_GATE + z))
                    act.copy(w_hi[:, 1 - z, :], w_raw[:, 1 - z, :]).then_inc(s["w_high"], 1)
                    gate(i, z)
            for z in range(2):
                split_weights(T_BR - 1 + z)
                gate(15, z)

            def sb_log(m):
                wait("sb_zc")
                if m >= 2:
                    act.wait_ge(s["sb_e"], m - 1)
                l = sb_wide(sb_l, m)
                wait.after(act.activation(l, sb_wide(sb_zc, m), ACT.Abs))
                wait.after(act.activation(l, l, ACT.Exp, scale=-1.0))
                act.activation(l, l, ACT.Ln, bias=1.0).then_inc(s["sb_l"], 1)

            def sb_o_out(qb):
                wait("sb_o")
                act.copy(sb_o[:, qb % 2, :], gp[:, 1, 0:BW]).then_inc(s["sb_o_copied"], 1)

            def sb_y_out(qb):
                wait("sb_y")
                act.copy(y_b[:, :, P * qb:P * qb + P],
                         gp[:, 1, HALF:HALF + BW].rearrange("p (f t) -> p f t", f=2)) \
                    .then_inc(s["sb_y_free"], 1)

            logs_and_exps()
            sb_log(0)
            for m in range(PAIRS + 1):
                if m + 1 < PAIRS:
                    sb_log(m + 1)
                if m >= 1:
                    for n in (2 * m - 2, 2 * m - 1):
                        w = P * (n // 4 + 1)
                        wait("sb_pt")
                        act.copy(sb_pt[:, n % 2, 0:w], gp[:, 0, 0:w]).then_inc(s["sb_pt_copied"], 1)
                        if n >= 4 and n % 4 == 0:
                            sb_o_out(n // 4 - 1)
                        if n >= 4 and n % 4 == 2:
                            sb_y_out(n // 4 - 1)
                if m < PAIRS:
                    wait("sb_e")
                    act.activation(sb_wide(sb_sp, m), sb_wide(sb_sp, m), ACT.Exp).then_inc(s["sb_p"], 1)
            sb_o_out(NB - 1)
            sb_y_out(NB - 1)

            wait("rk_shift", 8)
            for ft in range(2):
                act.activation(rk_th[0:C, :], zr[0:C, 6, :], ACT.Tanh).then_inc(s["rk_lora"], 1)
                wait.after(act.activation(rk_sg[:, :], zr[:, 7, :], ACT.Sigmoid))
                wait("rk_kk1")
                act.activation(rk_e[:, :], rk_kk[:, :], ACT.Square).then_inc(s["rk_kk2"], 1)
                wait("rk_lora_p")
                act.activation(rk_f[:, :], gp[:, 0, :], ACT.Sigmoid, bias=pcol("w0", ft)).then_inc(s["rk_w"], 1)
                act.activation(rk_a[:, :], gp[:, 1, :], ACT.Sigmoid, bias=pcol("a0", ft)).then_inc(s["rk_w"], 1)
                wait("rk_lora_p")
                act.activation(rk_e[:, :], sm[:, 0:2, :].rearrange("p a b -> p (a b)"), ACT.Sqrt) \
                    .then_inc(s["rk_pow"], 1)
                wait("rk_cum")
                act.activation(rk_f[:, :], rk_l[:, :], ACT.Exp, scale=DECAY).then_inc(s["rk_pow"], 1)
                act.activation(rk_lx[:, :], rk_lx[:, :], ACT.Exp, scale=-DECAY).then_inc(s["rk_pow"], 1)
                act.activation(rk_l[:, :], rk_l[:, :], ACT.Exp, scale=-DECAY).then_inc(s["rk_pow"], 1)
                for b in range(0, 8, 2):
                    wait("rk_tok_t", 1 if b == 0 else 2)
                    act.copy((a_tok, b_tok, k_tok, v_tok)[b // 2][:, 0:4, :],
                             bank(b).rearrange("p (u c) -> p u c", u=4)).then_inc(s["rk_tok0"], 1)
                wait("rk_tok_t")
                for g in range(2):
                    for n in range(1, 6):
                        for hh in range(2):
                            wait("rk_p")
                            act.copy(m_p[:, hh], bank(2 * hh).rearrange("p (u c) -> p u c", u=4)) \
                                .then_inc(s["rk_copied"], 1)
                    for hh in range(2):
                        cols = slice(C * hh, C * hh + C)
                        wait("rk_nv")
                        act.copy(nv[:, hh], bank(2 * hh)[:, 0:BW].rearrange("p (u c) -> p u c", u=4)) \
                            .then_inc(s["rk_copied"], 1)
                        act.copy(y_loc[:, 4 * g:4 * g + 4, cols],
                                 bank(2 * hh)[:, BW:2 * BW].rearrange("p (u c) -> p u c", u=4))
                        wait("rk_nv")
                        act.copy(xa_t[cols, HALF * g:HALF * g + HALF], bank(5 + 2 * hh)[cols, :]) \
                            .then_inc(s["rk_round_act"], 1)
                wait("rk_gvar")
                act.activation(small[:, 80:96], small[:, 64:80], ACT.Sqrt, bias=GN_EPS, scale=1.0 / C) \
                    .then_inc(s["rk_groot"], 1)
                for b in range(2):
                    wait("rk_y_t")
                    ins = act.copy(y_c[:, ft, HALF * b:HALF * b + HALF], bank(6 + b))
                ins.then_inc(s["rk_g_free"], 1)

            for n, y in enumerate((y_a, y_b, y_c, y_d)):
                if n == 0:
                    act.wait_ge(s["rk_g_free"], 2)
                for ft in range(2):
                    act.copy(y_hi[:, 2 * n + ft, :], y[:, ft, :]).then_inc(s["high"], 1)
            for d in range(KT):
                split_weights(T_BR + d + 1)
                act.wait_ge(s["merge_add"], 3 * (d + 1))
                act.copy(m_hi[:, d, :], merged[:, d % 2, :]).then_inc(s["high"], 1)
            for d in range(KT):
                split_weights(T_WO + d + 1)
            for z in range(2):
                act.wait_ge(s[f"p_free{z}"], frees_before(P_FFN))
            norm(1, x_mid)
            split_h()

            def taps(tap, j, i):
                return col[:, bass.ds(2 * i + (ROWS["conv"] + 2 * FT * tap + 2 + j), 1)]

            def first_tap(i, buf, j, p):
                act.wait_ge(s["p_ready"], 12 * i + (p + 1))
                act.activation(hid[:, buf, :], gp[:, p % 2, :], ACT.Copy, scale=taps(2, j, i)) \
                    .then_inc(s["c_first"], 1)

            def gate_silu(i, buf, p):
                act.wait_ge(s[f"p_free{p % 2}"], 6 * i + (frees_before(p) + 1))
                act.activation(hid[:, buf, :], hid[:, buf, :], ACT.Silu).then_inc(s["silu"], 1)

            def g_high(i, k):
                act.wait_ge(s["g_raw"], 2 * i + (3 + k))
                act.copy(g_hi[:, k, :], hid[:, 2 * k + 1, :]).then_inc(s["g_high"], 1)

            for n in range(4):
                split_weights(T_FFN + n + 1)
                if n in (1, 3):
                    gate_silu(-1, n - 1, P_FFN + 12 + n - 1)
                first_tap(-1, n, (0, FT, 1, FT + 1)[n], P_FFN + 12 + n)
                if n in (1, 3):
                    g_high(-1, n // 2)
            p0 = P_FFN + 4
            with act.Fori(0, FT // 2 - 1) as i:
                for u in range(6):
                    t = T_FFN + 4 + u
                    act.wait_ge(s[f"w_loaded{(u + 1) % 2}"], 48 * i + loaded_value(t + 1))
                    act.wait_ge(s["p_ready"], 12 * i + outs_through(t - 1))
                    act.copy(w_hi[:, (u + 1) % 2, :], w_raw[:, (u + 1) % 2, :]).then_inc(s["w_high"], 1)
                    if u == 0:
                        first_tap(i, 0, 0, p0)
                    elif u == 1:
                        gate_silu(i, 0, p0)
                    elif u == 3:
                        act.wait_ge(s["g_split"], 2 * i + 2)
                        first_tap(i, 1, FT, p0 + 9)
                        g_high(i, 0)
                    elif u == 4:
                        first_tap(i, 2, 1, p0 + 10)
                    elif u == 5:
                        gate_silu(i, 2, p0 + 10)
                        first_tap(i, 3, FT + 1, p0 + 11)
                        g_high(i, 1)
            split_weights(T_IN2 - 1)
            split_weights(T_IN2)
            for z in range(2):
                act.wait_ge(s[f"p_free{z}"], frees_before(P_IN2))
            norm(2, x_mid)
            norm(3, x_mid, "x_normed")
            split_h()
            for t in range(T_IN2, T_UQ):
                split_weights(t + 1)
                n = t - T_IN2
                act.wait_ge(s["p_ready"], P_IN2 + n + 1)
                if n == 0:
                    act.wait_ge(s["x_out"], 32)
                ps = gp[:, n % 2, :]
                dst, func = ((q_2[:, n, :], ACT.Copy) if n < 4 else (k_2[:, n - 4, :], ACT.Copy) if n < 8
                             else (vt_2[:, n - 8, :], ACT.Copy) if n < 12
                             else (z_a[:, n - 12, :], ACT.Silu) if n < 16
                             else (c_q[:, n - 16, :], ACT.Copy) if n < 18
                             else (c_kv[:, :], ACT.Copy) if n == 18
                             else (k_rope[:, :], ACT.Copy) if n == 19
                             else (z_b[:, n - 20, :], ACT.Silu))
                act.activation(dst, ps, func).then_inc(s[f"p_free{n % 2}"], 1)

            for z in range(2):
                act.wait_ge(s[f"p_free{z}"], frees_before(P_UQ))

            def root_of(dst, src, n, sem):
                wait.after(act.activation(dst, src, ACT.Ln, bias=RMS_EPS, scale=1.0 / n))
                act.activation(dst, dst, ACT.Exp, scale=-0.5).then_inc(s[sem], 1)

            def pair(z):
                return sm[:, 2 * z:2 * z + 2, :].rearrange("p a b -> p (a b)")

            def n2_square(j):
                if j >= 2:
                    act.wait_ge(s["n2_ss"], j - 1)
                act.activation(nsq[:, j % 2, :], (q_2, k_2)[j // 4][:, j % 4, :], ACT.Square) \
                    .then_inc(s["n2_sq"], 1)

            wait("bias_rows")
            logs_and_exps()
            n2_square(0)
            for j in range(8):
                if j < 7:
                    n2_square(j + 1)
                act.wait_ge(s["n2_ss"], j + 1)
                if j >= 2:
                    wait("n2_q")
                root_of(nrt[:, j % 2, :], pair(j % 2), C, "n2_rt")

            def attention(block, scale):
                def exps(n):
                    w = P * (block(n) + 1)
                    wait("at_m")
                    act.activation(att_s[:, n % 2, 0:w], att_s[:, n % 2, 0:w], ACT.Exp, scale=scale,
                                   bias=at_small(1, n), accum_out=at_small(2, n)).then_inc(s["at_p"], 1)

                exps(0)
                for n in range(UNITS):
                    if n < UNITS - 1:
                        exps(n + 1)
                    w = P * (block(n) + 1)
                    wait("at_pt")
                    act.copy(att_pt[:, n % 2, 0:w], gp[:, 0, 0:w]).then_inc(s["at_pt_copied"], 1)

            attention(lambda n: n % NB, 1.0)
            act.wait_ge(s["n2_q"], 8)
            for j, src in enumerate((c_q[:, 0, :], c_q[:, 1, :], c_kv[:, :])):
                if j == 2:
                    act.wait_ge(s["c_ss"], 1)
                act.activation(nsq[:, j % 2, :], src, ACT.Square).then_inc(s["c_sq"], 1)
            act.wait_ge(s["c_ss"], 2)
            act.activation(nsq[C:C + 32, 1, :], k_rope[C:C + 32, :], ACT.Square).then_inc(s["c_sq"], 1)
            root_of(nrt[:, 0, :], pair(0), BW, "c_root")
            act.wait_ge(s["c_ss"], 3)
            root_of(nrt[:, 1, :], pair(1), P, "c_root")
            act.wait_ge(s["c_ss"], 4)
            act.wait_ge(s["kv_normed"], 1)
            root_of(nrt[C:C + 32, 0, :], pair(0)[C:C + 32, :], 32, "c_root")
            for k in range(2):
                act.wait_ge(s["q_normed"], k + 1)
                act.copy(cq_hi[:, k, :], c_q[:, k, :]).then_inc(s["high"], 1)
            act.copy(ckv_hi[:, 0, :], c_kv[:, :]).then_inc(s["high"], 1)
            split_weights(T_UQ + 1)

            for h in range(HEADS_B):
                p = P_UQ + h
                act.wait_ge(s["p_ready"], p + 1)
                act.copy(qh[:, h, :], gp[0:DQK, p % 2, :]).then_inc(s[f"p_free{p % 2}"], 1)
            split_weights(T_UKV)
            for z in range(2):
                act.wait_ge(s[f"p_free{z}"], frees_before(P_UKV))
            wait("angles")
            act.activation(sin_t[C:C + 32, :], sin_t[C:C + 32, :], ACT.Sin).then_inc(s["hn_rt"], 1)
            act.activation(cos_t[C:C + 32, :], cos_t[C:C + 32, :], ACT.Sin).then_inc(s["hn_rt"], 1)

            def head_square(h, view, rows):
                act.activation(nsq_b[0:rows, h % 2, :], view, ACT.Square).then_inc(s["hn_sq"], 1)

            logs_and_exps()
            head_square(0, qh[:, 0, :], DQK)
            for h in range(HEADS_B):
                if h < HEADS_B - 1:
                    head_square(h + 1, qh[:, h + 1, :], DQK)
                wait("hn_ss")
                if h >= 2:
                    act.wait_ge(s["hn_done"], h - 1)
                root_of(rt_q[0:DQK, h % 2, :], pair(h % 2)[0:DQK, :], 1, "hn_rt")
            act.wait_ge(s["rot_used"], HEADS_B + 1)
            for h in range(HEADS_B + 1):
                if h < HEADS_B:
                    p = P_UKV + h
                    act.wait_ge(s["p_ready"], p + 1)
                    wait.after(act.copy(kh[0:C, h, :], gp[0:C, p % 2, :]))
                    head_square(h, kh[0:C, h, :], C)
                if h:
                    wait("hn_ss")
                    if h >= 3:
                        act.wait_ge(s["hn_done"], HEADS_B + h - 2)
                    root_of(rt_k[0:C, (h - 1) % 2, :], pair(0)[0:C, :], 1, "hn_rt")
            split_weights(T_OUT)
            split_weights(T_OUT + 1)
            attention(lambda n: n // 8, DQK ** -0.5)
            act.wait_ge(s["z_done"], 2 * NB)
            for k in range(8):
                act.copy(mix_hi[:, k, :], (z_a, z_b)[k // 4][:, k % 4, :]).then_inc(s["high"], 1)
            for d in range(KT):
                if 1 <= d < KT - 1:
                    split_weights(T_OUT + d + 1)
                wait("out_t")
                if d >= 2:
                    act.wait_ge(s[f"stored{d % 2}"], 16 * (d // 2))
                act.copy(out_tok[:, d % 2], pair(d % 2).rearrange("p (n c) -> p n c", c=P)) \
                    .then_inc(s["out_taken"], 1)

        @block.vector
        def _(dve):
            wait = Waits(dve, "dve_own")

            def split_weights(t):
                n = block_columns(t)
                dve.wait_ge(s["w_high"], t + 1)
                dve.tensor_tensor(w_lo[:, t % 2, 0:n], w_raw[:, t % 2, 0:n], w_hi[:, t % 2, 0:n].bitcast(F32),
                                  ALU.subtract).then_inc(s["w_split"], 1)

            def norm(src, gain, dst=None):
                wait("root")
                for k in range(KT):
                    o = dst[:, k, :] if dst is not None else h_tmp[:, k % 2, :]
                    if dst is None and k >= 2:
                        wait("h_split")
                    ins = dve.scalar_tensor_tensor(o, src[:, k, :], pcol(gain, k), rstd[:, :], ALU.mult, ALU.mult)
                    ins.then_inc(s["h_ready"] if dst is None else s["x_normed"], 1)
                    if dst is None and k >= 1:
                        h_low(k - 1)
                if dst is None:
                    h_low(KT - 1)
                    wait("h_split", 2)

            def h_low(k):
                wait("high")
                dve.tensor_tensor(h_lo[:, k, :], h_tmp[:, k % 2, :], h_hi[:, k, :].bitcast(F32),
                                  ALU.subtract).then_inc(s["h_split"], 1)

            wait("col_t")
            dve.tensor_copy(col[:, 0:NCOL], sm[:, 0, 0:NCOL]).then_inc(s["cols"], 1)
            wait("wsg_t")
            dve.tensor_copy(w_sg[:, :, :], sm[:, 1, :].rearrange("p (g t) -> p g t", g=4)).then_inc(s["wsg_copied"], 1)
            dve.wait_ge(s["cols"], 1)
            wait.after(dve.tensor_scalar(k_a_rest[:, :], col[:, ROWS["k_a"]:ROWS["k_a"] + 2], -1.0, 1.0,
                                         ALU.mult, ALU.add))
            wait.after(dve.tensor_scalar(a_q_scaled[:, :], pcol("a_q"), 0.125, None, ALU.mult))
            for b in range(1, 16, 2):
                dve.wait_ge(s["x_t"], b + 1)
                half, k = divmod(b, 8)
                dve.tensor_copy(x_t[:, k, HALF * half:HALF * half + HALF], sm[:, b % 4, :]) \
                    .then_inc(s["x_turned1"], 1)
            split_weights(0)
            norm(x_t, "mix_g")
            for t in range(T_GATE):
                split_weights(t + 1)
                if t in (4, 5):
                    n = t - 4
                    dve.wait_ge(s["p_ready"], t + 1)
                    dve.wait_ge(s["p_free0"], 2)
                    dve.wait_ge(s["p_free1"], 2)
                    cx, acc = sc_cx[:, 0, :], sc_c[:, n, :]
                    dve.tensor_tensor(cx, gp[:, t % 2, :], sc_c[:, n, :], ALU.mult).then_inc(s[f"p_free{t % 2}"], 1)
                    dve.wait_ge(s[f"p_free{t % 2}"], 3)
                    wait.after(dve.tensor_scalar(acc, cx, pcol("sc_w", 4 + n), None, ALU.mult))
                    for shift in (1, 2):
                        wait.after(dve.scalar_tensor_tensor(
                            acc[:, shift:T], cx[:, 0:T - shift], pcol("sc_w", 4 - 2 * shift + n),
                            acc[:, shift:T], ALU.mult, ALU.add))
                    ins = dve.tensor_tensor(y_a[:, n, :], y_a[:, n, :], acc, ALU.mult)
                    if n == 1:
                        ins.then_inc(s["sc_done"], 1)
                if t == 13:
                    for b in range(4):
                        ft, half = divmod(b, 2)
                        wait("v_turned")
                        dve.tensor_copy(v_sb[:, 4 * half:4 * half + 4, P * ft:P * ft + P],
                                        sm[:, b, :].rearrange("p (n c) -> p n c", n=4)).then_inc(s["v_taken"], 1)
            for b in range(4):
                ft, half = divmod(b, 2)
                wait("v_turned")
                wait.after(dve.tensor_copy(v_sg[:, 4 * half:4 * half + 4, P * ft:P * ft + P],
                                           sm[:, b, :].rearrange("p (n c) -> p n c", n=4)))
            stats = rstd[:, 0:6 * NB].rearrange("p (n k) -> p n k", n=NB)
            mean_var = rstd[:, 64:64 + 2 * NB].rearrange("p (n k) -> p n k", n=NB)
            for tt in range(NB):
                ins = dve.bn_stats(stats[:, tt, :], v_sg[:, tt, :])
            wait.after(ins)
            for tt in range(NB):
                ins = dve.bn_aggr(mean_var[:, tt, :], stats[:, tt, :])
            wait.after(ins)
            dve.tensor_copy(small[:, 8:16], mean_var[:, :, 1]).then_inc(s["sg_var"], 1)
            wait("sg_root")
            wait.after(dve.reciprocal(small[:, 24:32], small[:, 16:24]))
            for tt in range(NB):
                ins = dve.tensor_scalar(v_sg[:, tt, :], v_sg[:, tt, :], mean_var[:, tt, 0:1],
                                        small[:, 24 + tt:25 + tt], ALU.subtract, ALU.mult)
            wait.after(ins)
            wait.after(dve.tensor_tensor(v_sg[:, :, :], v_sg[:, :, :],
                                         row_g[:, 0, :].unsqueeze(1).to_broadcast([P, NB, BW]), ALU.mult))
            dve.tensor_tensor(v_sg[:, :, :], v_sg[:, :, :],
                              row_g[:, 1, :].unsqueeze(1).to_broadcast([P, NB, BW]), ALU.add) \
                .then_inc(s["sg_normed"], 1)
            dve.wait_ge(s["p_free0"], 11)
            dve.wait_ge(s["p_free1"], 11)
            for b in range(4):
                ft, half = divmod(b, 2)
                c = slice(HALF * half, HALF * half + HALF)
                wait("sg_mixed")
                dve.tensor_tensor(y_d[:, ft, c], sm[:, b, :], y_d[:, ft, c], ALU.mult).then_inc(s["sg_done"], 1)
            with dve.Fori(0, 16) as i:
                for z in range(2):
                    dve.wait_ge(s["w_high"], 2 * i + (T_GATE + z + 2))
                    dve.tensor_tensor(w_lo[:, 1 - z, :], w_raw[:, 1 - z, :], w_hi[:, 1 - z, :].bitcast(F32),
                                      ALU.subtract).then_inc(s["w_split"], 1)

            both = sm[:, :, :].rearrange("p (h b) c -> p h (b c)", h=2)

            def sb_keep(m):
                wait("sb_z")
                if m >= 2:
                    dve.wait_ge(s["sb_e"], m - 1)
                dve.tensor_copy(sb_wide(sb_zc, m), both[:, :, 0:P * (m // 2 + 1)]).then_inc(s["sb_zc"], 1)

            def sb_soft(m):
                wait("sb_l")
                dve.wait_ge(s["sb_zc"], m + 1)
                if m >= 2:
                    dve.wait_ge(s["sb_pt"], 2 * (m - 1))
                dve.scalar_tensor_tensor(sb_wide(sb_sp, m), sb_wide(sb_zc, m), 0.0, sb_wide(sb_l, m),
                                         ALU.max, ALU.add).then_inc(s["sb_sp"], 1)

            sb_keep(0)
            sb_soft(0)
            for m in range(PAIRS):
                if m + 1 < PAIRS:
                    sb_keep(m + 1)
                wait("sb_sp_cut")
                w = P * (m // 2 + 1)
                for hh in range(2):
                    ins = dve.tensor_tensor_scan(sb_l[:, m % 2, hh, 0:w][:, ::-1], ones_row[:, 0:w],
                                                 sb_sp[:, m % 2, hh, 0:w][:, ::-1], 0.0, ALU.mult, ALU.add)
                wait.after(ins)
                dve.tensor_tensor(sb_wide(sb_sp, m), sb_wide(sb_zc, m), sb_wide(sb_l, m), ALU.subtract) \
                    .then_inc(s["sb_e"], 1)
                if m + 1 < PAIRS:
                    sb_soft(m + 1)

            dve.wait_ge(s["sb_pt_copied"], 4 * NB)
            dve.wait_ge(s["sb_e"], PAIRS)
            for z in range(2):
                dve.wait_ge(s[f"gate_stored{z}"], 16 * 16)
            wait.after(dve.memset(ones_row[:, 0:T:C], 0.0))
            for j in range(8):
                d = (rk_l, rk_lx)[j % 2]
                dve.tensor_scalar(d[:, 0:1], zr[:, j, 0:1], -1.0, None, ALU.mult)
                wait.after(dve.tensor_tensor(d[:, 1:T], zr[:, j, 0:T - 1], zr[:, j, 1:T], ALU.subtract))
                dve.scalar_tensor_tensor(zr[:, j, :], d[:, :], pcol("mu", j), zr[:, j, :], ALU.mult, ALU.add) \
                    .then_inc(s["rk_shift"], 1)
                wait("rk_shift")
            bonus, decay_end = small[:, 32:48], small[:, 48:64]
            for ft in range(2):
                zk, zv, zq = zr[:, 2 + ft, :], zr[:, 4 + ft, :], zr[:, ft, :]
                dve.tensor_scalar(rk_kk[:, :], zk, pcol("k_k", ft), None, ALU.mult).then_inc(s["rk_kk1"], 1)
                wait("rk_w")
                wait.after(dve.tensor_tensor_scan(rk_l[:, :], ones_row[:, :], rk_f[:, :], 0.0, ALU.mult, ALU.add))
                dve.tensor_tensor(rk_lx[:, :], rk_l[:, :], rk_f[:, :], ALU.subtract).then_inc(s["rk_cum"], 1)
                wait("rk_pow")
                wait.after(dve.tensor_scalar(rk_e[:, :], rk_e[:, :], 1e-12, None, ALU.max))
                wait.after(dve.reciprocal(rk_e[:, :], rk_e[:, :]))
                wait.after(dve.tensor_tensor(rk_kk[:, :], rk_kk[:, :], rk_e[:, :], ALU.mult))
                wait("rk_w")
                wait.after(dve.tensor_scalar(rk_e[:, :], rk_a[:, :], pcol("k_a", ft), k_a_rest[:, ft:ft + 1],
                                             ALU.mult, ALU.add))
                wait.after(dve.tensor_tensor(zk, zk, rk_e[:, :], ALU.mult))
                wait.after(dve.tensor_tensor(rk_b[:, :], rk_kk[:, :], rk_a[:, :], ALU.mult))
                dve.scalar_tensor_tensor(rk_e[:, :], zq, pcol("r_k", ft), zk, ALU.mult, ALU.mult) \
                    .then_inc(s["rk_bonus"], 1)
                wait("rk_pow")
                wait.after(dve.tensor_tensor(rk_b[:, :], rk_b[:, :], rk_f[:, :], ALU.mult))
                wait.after(dve.tensor_tensor(zk, zk, rk_f[:, :], ALU.mult))
                wait("rk_pow")
                wait.after(dve.scalar_tensor_tensor(rk_a[:, :], rk_kk[:, :], -1.0, rk_lx[:, :], ALU.mult, ALU.mult))
                wait("rk_pow")
                wait.after(dve.tensor_tensor(zq, zq, rk_l[:, :], ALU.mult))
                wait.after(dve.tensor_copy(decay_end, rk_l[:, C - 1:T:C]))
                wait("rk_bonus_p")
                dve.tensor_copy(bonus, sm[:, 2, 0:16]).then_inc(s["rk_bonus_taken"], 1)
                end = decay_end.unsqueeze(2).to_broadcast([P, NCH, C])
                dve.tensor_tensor(rk_e[:, :].rearrange("p (n c) -> p n c", n=NCH),
                                  rk_b[:, :].rearrange("p (n c) -> p n c", n=NCH), end, ALU.mult)
                dve.tensor_tensor(rk_f[:, :].rearrange("p (n c) -> p n c", n=NCH),
                                  zk.rearrange("p (n c) -> p n c", n=NCH), end, ALU.mult).then_inc(s["rk_prep"], 1)
                for b in range(1, 8, 2):
                    wait("rk_tok_t", 2)
                    dve.tensor_copy((a_tok, b_tok, k_tok, v_tok)[b // 2][:, 4:8, :],
                                    bank(b).rearrange("p (u c) -> p u c", u=4)).then_inc(s["rk_tok1"], 1)
                wide = [P, 4, P]

                def four(x):
                    return x.rearrange("p (u c) -> p u c", u=4)

                def spread(m):
                    return m[:, :].unsqueeze(1).to_broadcast(wide)

                for g in range(2):
                    for hh in range(2):
                        wait("rk_mats")
                        dve.tensor_tensor(m_t[:, hh], four(bank(2 * hh)), spread(mask_s), ALU.mult) \
                            .then_inc(s["rk_m"], 1)
                        dve.wait_ge(s["rk_m"], 4 * ft + 2 * g + hh + 1)
                        wait.after(dve.tensor_tensor(inv_t[:, hh], m_t[:, hh], spread(level[0]), ALU.mult))
                        dve.tensor_tensor(inv_t[:, hh], inv_t[:, hh], spread(ident), ALU.add)
                        wait("rk_mats")
                        wait.after(dve.tensor_tensor(inv[:, hh], four(bank(2 * hh + 1)), spread(level0_t), ALU.mult))
                        dve.tensor_tensor(inv[:, hh], inv[:, hh], spread(ident), ALU.add)
                        wait("rk_mats")
                        dve.tensor_tensor(n_t[:, hh], four(bank(4 + 2 * hh)), spread(mask_s), ALU.mult)
                        wait("rk_mats")
                        dve.tensor_tensor(rb_t[:, hh, 4 * g:4 * g + 4, :], four(bank(5 + 2 * hh)), spread(mask_i),
                                          ALU.mult)
                    for hh in range(2):
                        wait("rk_mats")
                        dve.tensor_tensor(rk_t[:, hh], four(bank(2 * hh)), spread(mask_i), ALU.mult) \
                            .then_inc(s["rk_mats_done"], 1)
                    wait("rk_mats_done", 2)
                    for n in range(1, 6):
                        for hh in range(2):
                            wait("rk_x")
                            if n < 5:
                                dve.tensor_tensor(inv[:, hh], inv[:, hh], four(bank(2 * hh + 1)), ALU.add)
                            dve.tensor_tensor(inv_t[:, hh], inv_t[:, hh], four(bank(4 + 2 * hh)), ALU.add) \
                                .then_inc(s["rk_x_added"], 1)
                        wait("rk_x_added", 2)
                    for hh in range(2):
                        wait("rk_xnv")
                        dve.tensor_copy(xnv[:, 4 * g:4 * g + 4, C * hh:C * hh + C],
                                        bank(2 * hh + 1)[:, 0:BW].rearrange("p (u c) -> p u c", u=4)) \
                            .then_inc(s["rk_round"], 1)
                dve.memset(s_all[:, 0, :], 0.0).then_inc(s["rk_state"], 1)
                wait("rk_state")
                for ch in range(NCH):
                    tt, pb = ch // 2, C * (ch % 2)
                    toks = slice(pb, pb + C)
                    wait("rk_chain")
                    dve.tensor_tensor(u_tok[toks, tt, :].rearrange("p (h c) -> p h c", h=2),
                                      gp[toks, 0, :].rearrange("p (h c) -> p h c", h=2)[:, :, 0:C],
                                      xnv[toks, tt, :].rearrange("p (h c) -> p h c", h=2), ALU.add) \
                        .then_inc(s["rk_u_added"], 1)
                    wait("rk_chain")
                    dve.scalar_tensor_tensor(s_all[:, ch + 1, :], s_all[:, ch, :], decay_end[:, ch:ch + 1],
                                             bank(6)[:, 0:C], ALU.mult, ALU.add).then_inc(s["rk_state"], 1)
                    wait("rk_state")
                for g in range(2):
                    wait("rk_y")
                    wait.after(dve.tensor_tensor(
                        y_tok[:, 4 * g:4 * g + 4, :].rearrange("p u (h c) -> p h u c", h=2),
                        sm[:, 2 * g:2 * g + 2, 0:BW].rearrange("p h (u c) -> p h u c", c=C),
                        y_loc[:, 4 * g:4 * g + 4, :].rearrange("p u (h c) -> p h u c", h=2), ALU.add))
                yg = y_tok[:, :, :].rearrange("p t (h c) -> p (t h) c", h=2)
                sq = y_sq[:, :, :].rearrange("p t (h c) -> p (t h) c", h=2)
                vg = v_tok[:, :, :].rearrange("p t (h c) -> p (t h) c", h=2)
                mean, var, root_v = small[:, 96:112], small[:, 64:80], small[:, 80:96]

                def over(v):
                    return v.unsqueeze(2).to_broadcast([P, 16, C])

                def row(n):
                    return row_g[:, n, P * ft:P * ft + P].unsqueeze(1).to_broadcast([P, NB, P])

                wait.after(dve.tensor_reduce(mean, yg, AX, ALU.add))
                wait.after(dve.tensor_scalar(mean, mean, -1.0 / C, None, ALU.mult))
                wait.after(dve.tensor_tensor(yg, yg, over(mean), ALU.add))
                wait.after(dve.tensor_tensor(sq, yg, yg, ALU.mult))
                dve.tensor_reduce(var, sq, AX, ALU.add).then_inc(s["rk_gvar"], 1)
                wait("rk_groot")
                wait.after(dve.reciprocal(root_v, root_v))
                wait.after(dve.tensor_tensor(yg, yg, over(root_v), ALU.mult))
                wait.after(dve.tensor_tensor(y_tok[:, :, :], y_tok[:, :, :], row(2), ALU.mult))
                wait.after(dve.tensor_tensor(y_tok[:, :, :], y_tok[:, :, :], row(3), ALU.add))
                wait.after(dve.tensor_tensor(sq, vg, over(bonus), ALU.mult))
                wait.after(dve.tensor_tensor(yg, yg, sq, ALU.add))
                for b in range(2):
                    wait("rk_y")
                    ins = dve.tensor_tensor(y_tok[:, 4 * b:4 * b + 4, :], y_tok[:, 4 * b:4 * b + 4, :],
                                            four(bank(4 + b)), ALU.mult)
                ins.then_inc(s["rk_y_ready"], 1)

            for n, y in enumerate((y_a, y_b, y_c, y_d)):
                for ft in range(2):
                    wait("high")
                    dve.tensor_tensor(y_lo[:, 2 * n + ft, :], y[:, ft, :], y_hi[:, 2 * n + ft, :].bitcast(F32),
                                      ALU.subtract).then_inc(s["y_split"], 1)
            for d in range(KT):
                split_weights(T_BR + d + 1)
                if d >= 2:
                    wait("m_split")
                for n in range(4):
                    q = 4 * d + n
                    p = P_BR + q
                    dve.wait_ge(s["p_ready"], p + 1)
                    dve.wait_ge(s[f"gate_in{n}"], 16 * (d + 1))
                    o = merged[:, d % 2, :] if n == 0 else gated[:, q % 2, :]
                    if n and q >= 3:
                        dve.wait_ge(s["merge_add"], merge_adds(q - 2))
                    dve.tensor_tensor(o, gp[:, p % 2, :], gate_in[:, n, :], ALU.mult).then_inc(s[f"p_free{p % 2}"], 1)
                wait("high")
                dve.tensor_tensor(m_lo[:, d, :], merged[:, d % 2, :], m_hi[:, d, :].bitcast(F32),
                                  ALU.subtract).then_inc(s["m_split"], 1)
            for d in range(KT):
                split_weights(T_WO + d + 1)
                p = P_WO + d
                dve.wait_ge(s["p_ready"], p + 1)
                dve.wait_ge(s[f"x_back{d % 2}"], 16 * (d // 2 + 1))
                dve.tensor_tensor(x_mid[:, d, :], gp[:, p % 2, :], x_back[:, d % 2, :], ALU.add) \
                    .then_inc(s[f"p_free{p % 2}"], 1)
            norm(x_mid, "ffn_g")

            def taps(tap, j, i):
                return col[:, bass.ds(2 * i + (ROWS["conv"] + 2 * FT * tap + 2 + j), 1)]

            def conv(i, buf, j, p):
                dve.wait_ge(s["c_first"], 4 * i + (5 + buf))
                ps = gp[:, p % 2, :]
                dve.scalar_tensor_tensor(hid[:, buf, 1:T], ps[:, 0:T - 1], taps(1, j, i), hid[:, buf, 1:T],
                                         ALU.mult, ALU.add).then_inc(s["conv_mid"], 1)
                dve.wait_ge(s["conv_mid"], 4 * i + (5 + buf))
                dve.scalar_tensor_tensor(hid[:, buf, 2:T], ps[:, 0:T - 2], taps(0, j, i), hid[:, buf, 2:T],
                                         ALU.mult, ALU.add).then_inc(s[f"p_free{p % 2}"], 1)

            def glu(i, k, p):
                dve.wait_ge(s[f"p_free{p % 2}"], 6 * i + (frees_before(p) + 1))
                dve.wait_ge(s["silu"], 2 * i + (3 + k))
                g = hid[:, 2 * k + 1, :]
                dve.tensor_tensor(g, hid[:, 2 * k, :], g, ALU.mult).then_inc(s["g_raw"], 1)
                dve.wait_ge(s["g_high"], 2 * i + (3 + k))
                dve.tensor_tensor(g_lo[:, k, :], g, g_hi[:, k, :].bitcast(F32), ALU.subtract) \
                    .then_inc(s["g_split"], 1)

            def add_down(i, u, p):
                for j in range(4):
                    d = 4 * u + j
                    dve.wait_ge(s["p_ready"], 12 * i + (p + j + 1))
                    for z in range(2):
                        dve.wait_ge(s[f"p_free{z}"], 6 * i + (frees_before(p) - 2))
                    dve.tensor_tensor(x_mid[:, d, :], x_mid[:, d, :], gp[:, (p + j) % 2, :], ALU.add) \
                        .then_inc(s[f"p_free{(p + j) % 2}"], 1)

            for n in range(4):
                split_weights(T_FFN + n + 1)
                conv(-1, n, (0, FT, 1, FT + 1)[n], P_FFN + 12 + n)
                if n % 2:
                    glu(-1, n // 2, P_FFN + 12 + n)
            p0 = P_FFN + 4
            with dve.Fori(0, FT // 2 - 1) as i:
                for u in range(6):
                    dve.wait_ge(s["w_high"], 6 * i + (T_FFN + 6 + u))
                    z = (u + 1) % 2
                    dve.tensor_tensor(w_lo[:, z, :], w_raw[:, z, :], w_hi[:, z, :].bitcast(F32),
                                      ALU.subtract).then_inc(s["w_split"], 1)
                    if u == 0:
                        conv(i, 0, 0, p0)
                    elif u < 3:
                        add_down(i, u - 1, p0 + 1 + 4 * (u - 1))
                    elif u == 3:
                        conv(i, 1, FT, p0 + 9)
                        glu(i, 0, p0 + 9)
                    elif u == 4:
                        conv(i, 2, 1, p0 + 10)
                    else:
                        conv(i, 3, FT + 1, p0 + 11)
                        glu(i, 1, p0 + 11)
            split_weights(T_IN2 - 1)
            add_down(FT // 2 - 1, 0, p0)
            split_weights(T_IN2)
            add_down(FT // 2 - 1, 1, p0 + 4)
            norm(x_mid, "fin_g", x_mid)
            norm(x_mid, "g2")
            for t in range(T_IN2, T_UQ):
                split_weights(t + 1)
                if t - T_IN2 == 13:
                    for b in range(8):
                        ft, half = divmod(b, 2)
                        wait("v_turned")
                        dve.tensor_copy(v_2[:, 4 * half:4 * half + 4, P * ft:P * ft + P],
                                        sm[:, b % 4, :].rearrange("p (n c) -> p n c", n=4)).then_inc(s["v_taken"], 1)
            wait("bias_p")
            dve.tensor_copy(bias_vec[:, :].rearrange("p (n c) -> p n c", n=3), sm[0:HEADS_A, 0:3, 0:384]) \
                .then_inc(s["bias_rows"], 1)
            for j in range(8):
                t = (q_2, k_2)[j // 4][:, j % 4, :]
                wait("n2_rt")
                dve.scalar_tensor_tensor(t, t, a_q_scaled[:, :] if j < 4 else pcol("a_k"), nrt[:, j % 2, :],
                                         ALU.mult, ALU.mult).then_inc(s["n2_q"], 1)

            def attention(block, table_of, scale, out_of):
                def scores(n):
                    z, w = n % 2, P * (block(n) + 1)
                    wait("at_z")
                    tab = table_of(n)
                    dve.tensor_tensor_reduce(
                        out=att_s[:, z, 0:w], in0=sm[:, 2 * z:2 * z + 2, :].rearrange("p a b -> p (a b)")[:, 0:w],
                        in1=tab[:, T - w:T], scale=1.0, scalar=-3e38, op0=ALU.add, op1=ALU.max,
                        accum_out=at_small(0, n)).then_inc(s["at_s"], 1)
                    wait("at_s")
                    dve.tensor_scalar(at_small(1, n), at_small(0, n), -scale, None,
                                      ALU.mult).then_inc(s["at_m"], 1)

                scores(0)
                scores(1)
                for n in range(UNITS):
                    if n < UNITS - 2:
                        scores(n + 2)
                    wait("at_p")
                    wait.after(dve.reciprocal(at_small(3, n), at_small(2, n)))
                    wait("at_o")
                    dve.tensor_scalar(out_of(n), o_place(n), at_small(3, n), None,
                                      ALU.mult).then_inc(s["at_o_taken"], 1)

            def gate_outputs(z):
                for qb in range(NB):
                    wait("z_turned")
                    zq = z[:, :, P * qb:P * qb + P]
                    dve.tensor_tensor(zq, zq, sm[:, qb % 4, :].rearrange("p (f t) -> p f t", f=4), ALU.mult) \
                        .then_inc(s["z_done"], 1)

            def bias_table(n):
                h = n // NB
                if n % NB == 0:
                    dve.wait_ge(s[f"table_in{h % 2}"], 16 * (h // 2 + 1))
                return table[:, h % 2, :]

            attention(lambda n: n % NB, bias_table, 1.0,
                      lambda n: o_all[:, n % NB, C * (n // NB):C * (n // NB) + C])
            gate_outputs(z_a)
            wait("c_root")
            for k in range(2):
                dve.scalar_tensor_tensor(c_q[:, k, :], c_q[:, k, :], pcol("q_c", k), nrt[:, 0, :],
                                         ALU.mult, ALU.mult).then_inc(s["q_normed"], 1)
            wait("c_root")
            dve.wait_ge(s["q_normed"], 2)
            dve.scalar_tensor_tensor(c_kv[:, :], c_kv[:, :], pcol("kv_c"), nrt[:, 1, :], ALU.mult, ALU.mult) \
                .then_inc(s["kv_normed"], 1)
            rope = slice(C, C + 32)
            wait("c_root")
            dve.scalar_tensor_tensor(k_rope[rope, :], k_rope[rope, :], col[rope, ROWS["kn"]:ROWS["kn"] + 1],
                                     nrt[rope, 0, :], ALU.mult, ALU.mult).then_inc(s["krope_normed"], 1)
            for k in range(2):
                wait("high")
                dve.tensor_tensor(cq_lo[:, k, :], c_q[:, k, :], cq_hi[:, k, :].bitcast(F32),
                                  ALU.subtract).then_inc(s["q_split"], 1)
            wait("high")
            dve.tensor_tensor(ckv_lo[:, 0, :], c_kv[:, :], ckv_hi[:, 0, :].bitcast(F32), ALU.subtract) \
                .then_inc(s["kv_split"], 1)
            split_weights(T_UQ + 1)
            wait("pos_in", 16)
            dve.wait_ge(s["q_split"], 2)
            dve.wait_ge(s["krope_normed"], 1)
            ang, turns = nrt[rope, 0, :], nrt[rope, 1, :]
            wait.after(dve.tensor_copy(ang, pos_i[rope, :]))
            wait.after(dve.tensor_scalar(ang, ang, freq[rope, :], None, ALU.mult))
            wait.after(dve.tensor_scalar(turns, ang, 1.0 / (2 * math.pi), ROUND, ALU.mult, ALU.add))
            wait.after(dve.tensor_scalar(turns, turns, -ROUND, None, ALU.add))
            for part in TURN:
                wait.after(dve.scalar_tensor_tensor(ang, turns, -part, ang, ALU.mult, ALU.add))
            wait.after(dve.tensor_scalar(sin_t[rope, :], ang, -PI_IN, PI_IN, ALU.max, ALU.min))
            wait.after(dve.tensor_scalar(ang, ang, math.pi / 2, None, ALU.add))
            wait.after(dve.tensor_scalar(turns, ang, math.pi, -2 * math.pi, ALU.is_gt, ALU.mult))
            wait.after(dve.tensor_tensor(ang, ang, turns, ALU.add))
            dve.tensor_scalar(cos_t[rope, :], ang, -PI_IN, PI_IN, ALU.max, ALU.min).then_inc(s["angles"], 1)

            def add_rope(view, place):
                wait("rot")
                wait.after(dve.tensor_tensor(rope_tmp[rope, :], place[rope, :], sin_t[rope, :], ALU.mult))
                wait.after(dve.tensor_tensor(view, view, cos_t[rope, :], ALU.mult))
                dve.tensor_tensor(view, view, rope_tmp[rope, :], ALU.add).then_inc(s["rot_used"], 1)

            split_weights(T_UKV)
            wait("hn_rt", 2)
            add_rope(k_rope[rope, :], sm[:, 2:4, :].rearrange("p a b -> p (a b)"))
            dve.wait_ge(s["rot_used"], 1)
            for h in range(HEADS_B + 1):
                if h < HEADS_B:
                    wait("hn_rt")
                    dve.scalar_tensor_tensor(qh[:, h, :], qh[:, h, :], col[0:DQK, ROWS["qn"]:ROWS["qn"] + 1],
                                             rt_q[0:DQK, h % 2, :], ALU.mult, ALU.mult).then_inc(s["hn_done"], 1)
                if h:
                    dve.wait_ge(s["hn_done"], h)
                    dve.wait_ge(s["rot_used"], h)
                    add_rope(qh[rope, h - 1, :], gp[:, (h - 1) % 2, :])
            dve.wait_ge(s["rot_used"], HEADS_B + 1)
            for h in range(HEADS_B):
                ins = dve.tensor_copy(kh[rope, h, :], k_rope[rope, :])
            ins.then_inc(s["k_rope_spread"], 1)
            for h in range(HEADS_B + 1):
                if h < HEADS_B:
                    p = P_UKV + h
                    dve.wait_ge(s["p_ready"], p + 1)
                    if h:
                        wait("vb_turned")
                    dve.tensor_copy(vb_t[C:P, :], gp[C:P, p % 2, :]).then_inc(s[f"p_free{p % 2}"], 1)
                if h:
                    if h == HEADS_B:
                        wait("vb_turned")
                    dve.tensor_copy(v_b[:, :, C * (h - 1):C * h],
                                    sm[:, 2 + (h - 1) % 2, :].rearrange("p (n c) -> p n c", n=NB)) \
                        .then_inc(s["vb_taken"], 1)
                    wait("hn_rt")
                    dve.scalar_tensor_tensor(kh[0:C, h - 1, :], kh[0:C, h - 1, :],
                                             col[0:C, ROWS["kn"]:ROWS["kn"] + 1],
                                             rt_k[0:C, (h - 1) % 2, :], ALU.mult, ALU.mult) \
                        .then_inc(s["hn_done"], 1)
            dve.wait_ge(s["hn_done"], 2 * HEADS_B)
            split_weights(T_OUT)
            split_weights(T_OUT + 1)
            wait("causal")
            attention(lambda n: n // 8, lambda n: causal, DQK ** -0.5,
                      lambda n: o_b[:, n // 8, C * (n % 8):C * (n % 8) + C])
            gate_outputs(z_b)
            for k in range(8):
                wait("high")
                dve.tensor_tensor(mix_lo[:, k, :], (z_a, z_b)[k // 4][:, k % 4, :], mix_hi[:, k, :].bitcast(F32),
                                  ALU.subtract).then_inc(s["mix_split"], 1)
            for d in range(KT):
                if 1 <= d < KT - 1:
                    split_weights(T_OUT + d + 1)
                p = P_OUT + d
                dve.wait_ge(s["p_ready"], p + 1)
                dve.wait_ge(s[f"x_back{d % 2}"], 16 * (KT // 2 + d // 2 + 1))
                if d >= 2:
                    dve.wait_ge(s["out_t"], d - 1)
                dve.tensor_tensor(x_out[:, d % 2, :], gp[:, p % 2, :], x_back2[:, d % 2, :], ALU.add) \
                    .then_inc(s[f"p_free{p % 2}"], 1)


_INS = ["x", "mix_norm_g", "w_in", "gate_b", "sc_conv_w", "sc_out", "sb_out", "rw_mu", "rw_w0", "rw_w2",
        "rw_a0", "rw_a2", "rw_g2", "rw_k_k", "rw_k_a", "rw_r_k", "rw_gn_g", "rw_gn_b", "rw_out", "sg_ln_g",
        "sg_ln_b", "sg_w", "sg_b", "sg_out", "w_o", "ffn_norm_g", "w_up", "ffn_conv_w", "w_down",
        "final_norm_g", "positions_2", "rel_bias_2", "norm_gain_2", "w_in_2", "a_q_gain_2", "a_k_gain_2",
        "q_c_gain_2", "w_uq_2", "kv_c_gain_2", "w_ukv_2", "qn_gain_2", "qr_gain_2", "kn_gain_2",
        "kr_gain_2", "w_out_2"]


def shape_tables():
    dist = 1023 - np.arange(1152)
    safe = np.maximum(dist, 0)
    large = 16 + (np.log(np.maximum(safe, 1).astype(np.float32) / np.float32(16))
                  / np.float32(math.log(2048 / 16)) * 16).astype(np.int32)
    bucket = np.where(safe < 16, safe, np.minimum(large, 31))
    count = sum(((dist >= 0) & (dist % d == 0) & (dist <= w)).astype(int)
                for w, d in ((128, 1), (512, 4), (2048, 16)))
    table = np.zeros((33, 1152), np.float32)
    table[bucket, np.arange(1152)] = 1.0
    table[32] = np.where(count > 0, np.log(np.maximum(count, 1)), NEG)
    freq = (np.float32(10000.0) ** (-np.arange(0, 32, 2, dtype=np.float32) / np.float32(32)))
    return table, np.tile(freq, 8).astype(np.float32).reshape(P, 1)


def kernel(**inputs):
    import concourse.bacc as _bacc
    from concourse.bass_utils import run_bass_kernel_spmd as _run

    nc = _bacc.Bacc("TRN2", target_bir_lowering=False, num_devices=1)
    arrays, args = {}, []
    table, freq = shape_tables()
    for name in _INS + ["bucket_table", "rope_freq"]:
        a = {"bucket_table": table, "rope_freq": freq}.get(name)
        a = np.ascontiguousarray(inputs[name] if a is None else a)
        arrays[f"in_{name}"] = a
        args.append(nc.dram_tensor(f"in_{name}", a.shape, mybir.dt.from_np(a.dtype), kind="ExternalInput").ap())
    args.append(nc.dram_tensor("out_0", (1, T, D), F32, kind="ExternalOutput").ap())
    hybrid_layers(nc, *args)
    r = _run(nc, [arrays], core_ids=[0])
    return r.results[0]["out_0"]
```
